# Optimizing a Trainium2 kernel written in Bass

```python
import math
import numpy as np
import jax, jax.numpy as jnp
from jax import lax

D_MODEL = 1024
BATCH = 1
SEQ = 256
DEPTH = 2

N_EVEN = (DEPTH + 1) // 2
N_ODD = DEPTH // 2

MLSTM_HEADS = 4
MLSTM_HEAD_DIM = 128
MLSTM_W = MLSTM_HEADS * MLSTM_HEAD_DIM
MLSTM_CHUNK = 128
CONV_K = 4
NSA_HEADS = 8
NSA_GROUPS = 2
NSA_HPG = NSA_HEADS // NSA_GROUPS
NSA_HEAD_DIM = 64
NSA_W = NSA_HEADS * NSA_HEAD_DIM
NSA_KV_W = NSA_GROUPS * NSA_HEAD_DIM
CMP_LEN = 32
CMP_STRIDE = 16
CMP_HIDDEN = 128
SEL_BLOCK = 64
SEL_TOPK = 16
WINDOW = 512
Q_BLOCK = 128
ROPE_THETA = 500000.0
ROPE_DIM = NSA_HEAD_DIM // 4
EVEN_MIX_W = MLSTM_W + NSA_W
MLSTM_SPLITS = (MLSTM_W,) * 5 + (MLSTM_HEADS, MLSTM_HEADS)
NSA_SPLITS = (NSA_W,) + (NSA_KV_W,) * 6 + (3 * NSA_HEADS, NSA_W)
MLSTM_COLS = sum(MLSTM_SPLITS)
NSA_COLS = sum(NSA_SPLITS)
EVEN_IN_COLS = MLSTM_COLS + NSA_COLS
HGRN_HEADS = 8
HGRN_HEAD_DIM = 128
HGRN_W = HGRN_HEADS * HGRN_HEAD_DIM
HGRN_CHUNK = 64
ODD_IN_COLS = 4 * HGRN_W
EPS = 1e-6
NEG = -1e30


def split_cols(a, sizes):
    idx = np.cumsum(sizes)[:-1].tolist()
    return jnp.split(a, idx, axis=-1)

def rms_norm(x, w):
    xf = x.astype(jnp.float32)
    return xf * lax.rsqrt(jnp.mean(xf * xf, axis=-1, keepdims=True) + EPS) * w.astype(jnp.float32)

def heads(a, n_heads):
    b, s, _ = a.shape
    return a.reshape(b, s, n_heads, -1).transpose(0, 2, 1, 3)

def partial_rope(x, pos):
    half = ROPE_DIM // 2
    inv_freq = ROPE_THETA ** (-jnp.arange(half, dtype=jnp.float32) / half)
    ang = pos.astype(jnp.float32)[:, None] * inv_freq
    cos, sin = jnp.cos(ang), jnp.sin(ang)
    x1, x2, rest = x[..., :half], x[..., half:ROPE_DIM], x[..., ROPE_DIM:]
    return jnp.concatenate([x1 * cos - x2 * sin, x1 * sin + x2 * cos, rest], axis=-1)

def masked_softmax(s, mask):
    p = jax.nn.softmax(jnp.where(mask, s, NEG), axis=-1)
    return jnp.where(mask, p, 0.0)

def causal_conv(x, w, b):
    c = x.shape[-1]
    out = lax.conv_general_dilated(
        x, w.astype(jnp.float32).reshape(CONV_K, 1, c), window_strides=(1,),
        padding=[(CONV_K - 1, 0)], dimension_numbers=('NWC', 'WIO', 'NWC'),
        feature_group_count=c)
    return out + b

def mlstm_chunkwise(q, k, v, i_pre, f_pre):
    b_, h_, s_, d = q.shape
    L = MLSTM_CHUNK
    nc = s_ // L
    logf = jax.nn.log_sigmoid(f_pre)

    def to_chunks(a):
        return jnp.moveaxis(a.reshape(b_, h_, nc, L, *a.shape[3:]), 2, 0)

    causal = jnp.tril(jnp.ones((L, L), dtype=bool))

    def step(carry, xs):
        C, n, m = carry
        qj, kj, vj, ij, fj = xs
        bcum = jnp.cumsum(fj, axis=-1)
        D = jnp.where(causal, bcum[..., :, None] - bcum[..., None, :] + ij[..., None, :], -jnp.inf)
        inter = bcum + m[..., None]
        m_row = jnp.maximum(jnp.max(D, axis=-1), inter)
        Smat = jnp.einsum('bhjd,bhsd->bhjs', qj, kj) * jnp.exp(D - m_row[..., None])
        w_inter = jnp.exp(inter - m_row)
        num = jnp.einsum('bhjs,bhse->bhje', Smat, vj) + w_inter[..., None] * jnp.einsum('bhjd,bhde->bhje', qj, C)
        den = Smat.sum(-1) + w_inter * jnp.einsum('bhjd,bhd->bhj', qj, n)
        h = num / jnp.maximum(jnp.abs(den), jnp.exp(-m_row))[..., None]
        bL = bcum[..., -1]
        dl = bL[..., None] - bcum + ij
        m_new = jnp.maximum(bL + m, jnp.max(dl, axis=-1))
        wk = jnp.exp(dl - m_new[..., None])
        decay = jnp.exp(bL + m - m_new)
        C_new = decay[..., None, None] * C + jnp.einsum('bhs,bhsd,bhse->bhde', wk, kj, vj)
        n_new = decay[..., None] * n + jnp.einsum('bhs,bhsd->bhd', wk, kj)
        return (C_new, n_new, m_new), h

    init = (jnp.zeros((b_, h_, d, d), jnp.float32), jnp.zeros((b_, h_, d), jnp.float32),
            jnp.zeros((b_, h_), jnp.float32))
    _, hs = lax.scan(step, init, (to_chunks(q), to_chunks(k), to_chunks(v), to_chunks(i_pre), to_chunks(logf)))
    return jnp.moveaxis(hs, 0, 2).reshape(b_, h_, s_, d)

def mlstm_branch(cols, f_bias, conv_w, conv_b, head_norm):
    b_, s_, _ = cols.shape
    q, k, v, o, z, ig, fg = split_cols(cols, MLSTM_SPLITS)
    qk = jax.nn.silu(causal_conv(jnp.concatenate([q, k], axis=-1), conv_w, conv_b))
    q, k = jnp.split(qk, 2, axis=-1)
    qh = heads(q, MLSTM_HEADS)
    kh = heads(k, MLSTM_HEADS) * (MLSTM_HEAD_DIM ** -0.5)
    vh = heads(v, MLSTM_HEADS)
    i_pre = ig.transpose(0, 2, 1)
    f_pre = (fg + f_bias).transpose(0, 2, 1)
    h = mlstm_chunkwise(qh, kh, vh, i_pre, f_pre).transpose(0, 2, 1, 3)
    h = rms_norm(h, head_norm.reshape(MLSTM_HEADS, MLSTM_HEAD_DIM)).reshape(b_, s_, MLSTM_W)
    return h * jax.nn.sigmoid(o) * jax.nn.silu(z)

def compress(blocks, w1, w2):
    flat = blocks.reshape(*blocks.shape[:3], CMP_LEN * NSA_HEAD_DIM)
    return jax.nn.gelu(flat @ w1) @ w2

def nsa_branch(cols, q_norm, k_norm, ck_pos, ck_w1, ck_w2, cv_pos, cv_w1, cv_w2):
    b_, s_, _ = cols.shape
    G, R, d = NSA_GROUPS, NSA_HPG, NSA_HEAD_DIM
    q, kc, vc, ks, vs, kw, vw, gt, z = split_cols(cols, NSA_SPLITS)
    pos = jnp.arange(s_)
    qh = partial_rope(rms_norm(heads(q, NSA_HEADS), q_norm), pos) * (d ** -0.5)
    qh = qh.reshape(b_, G, R, s_, d)
    ks_h = partial_rope(rms_norm(heads(ks, G), k_norm[1]), pos)
    vs_h = heads(vs, G)
    kw_h = partial_rope(rms_norm(heads(kw, G), k_norm[2]), pos)
    vw_h = heads(vw, G)

    n_cmp = (s_ - CMP_LEN) // CMP_STRIDE + 1
    cmp_idx = np.arange(n_cmp)[:, None] * CMP_STRIDE + np.arange(CMP_LEN)[None, :]
    cmp_end = jnp.asarray(cmp_idx[:, -1])
    k_cmp = compress(heads(kc, G)[:, :, cmp_idx] + ck_pos, ck_w1, ck_w2)
    k_cmp = partial_rope(rms_norm(k_cmp, k_norm[0]), cmp_end)
    v_cmp = compress(heads(vc, G)[:, :, cmp_idx] + cv_pos, cv_w1, cv_w2)

    n_sel = s_ // SEL_BLOCK
    cs = np.arange(n_cmp) * CMP_STRIDE
    ss = np.arange(n_sel) * SEL_BLOCK
    ov = np.clip(np.minimum(cs[:, None] + CMP_LEN, ss[None, :] + SEL_BLOCK)
                 - np.maximum(cs[:, None], ss[None, :]), 0, None).astype(np.float32)
    ov = jnp.asarray(ov)
    k_top = min(SEL_TOPK, n_sel)

    gates = jax.nn.sigmoid(gt.reshape(b_, s_, NSA_HEADS, 3)).transpose(0, 2, 1, 3).reshape(b_, G, R, s_, 3)
    kw_pad = jnp.pad(kw_h, ((0, 0), (0, 0), (WINDOW, 0), (0, 0)))
    vw_pad = jnp.pad(vw_h, ((0, 0), (0, 0), (WINDOW, 0), (0, 0)))
    bi = jnp.arange(b_)[:, None, None, None]
    gi = jnp.arange(G)[None, :, None, None]
    nqb = s_ // Q_BLOCK

    def to_blocks(a):
        a = a.reshape(*a.shape[:-2], nqb, Q_BLOCK, a.shape[-1])
        return jnp.moveaxis(a, -3, 0)

    def block_fn(args):
        qb, q_blk, g_blk = args
        t = qb * Q_BLOCK + jnp.arange(Q_BLOCK)
        s_c = jnp.einsum('bgrqd,bgnd->bgrqn', q_blk, k_cmp)
        p_c = masked_softmax(s_c, cmp_end[None, :] <= t[:, None])
        o_c = jnp.einsum('bgrqn,bgnd->bgrqd', p_c, v_cmp)
        imp = jnp.einsum('bgrqn,nm->bgqm', p_c, ov)
        blk = jnp.arange(n_sel)[None, :]
        cur = (t // SEL_BLOCK)[:, None]
        forced = (blk == 0) | (blk == cur) | (blk == cur - 1)
        imp = jnp.where(blk > cur, NEG, jnp.where(forced, -NEG, imp))
        _, sel = lax.top_k(imp, k_top)
        valid = sel <= cur[None, None]
        tok = (sel[..., None] * SEL_BLOCK + jnp.arange(SEL_BLOCK)).reshape(b_, G, Q_BLOCK, k_top * SEL_BLOCK)
        tok_ok = jnp.repeat(valid, SEL_BLOCK, axis=-1) & (tok <= t[:, None])
        ks_g = ks_h[bi, gi, tok]
        vs_g = vs_h[bi, gi, tok]
        s_s = jnp.einsum('bgrqd,bgqnd->bgrqn', q_blk, ks_g)
        p_s = masked_softmax(s_s, tok_ok[:, :, None])
        o_s = jnp.einsum('bgrqn,bgqnd->bgrqd', p_s, vs_g)
        kwb = lax.dynamic_slice_in_dim(kw_pad, qb * Q_BLOCK, Q_BLOCK + WINDOW, axis=2)
        vwb = lax.dynamic_slice_in_dim(vw_pad, qb * Q_BLOCK, Q_BLOCK + WINDOW, axis=2)
        sp = qb * Q_BLOCK - WINDOW + jnp.arange(Q_BLOCK + WINDOW)
        wmask = (sp[None, :] >= 0) & (sp[None, :] <= t[:, None]) & (t[:, None] - sp[None, :] < WINDOW)
        s_w = jnp.einsum('bgrqd,bgnd->bgrqn', q_blk, kwb)
        p_w = masked_softmax(s_w, wmask)
        o_w = jnp.einsum('bgrqn,bgnd->bgrqd', p_w, vwb)
        return g_blk[..., 0:1] * o_c + g_blk[..., 1:2] * o_s + g_blk[..., 2:3] * o_w

    out = lax.map(block_fn, (jnp.arange(nqb), to_blocks(qh), to_blocks(gates)))
    out = jnp.moveaxis(out, 0, 3).reshape(b_, NSA_HEADS, s_, d).transpose(0, 2, 1, 3).reshape(b_, s_, NSA_W)
    return out * jax.nn.silu(z)

def hgrn2_chunkwise(q, k, v, logf):
    b_, h_, s_, dk = q.shape
    dv = v.shape[-1]
    L = HGRN_CHUNK
    nc = s_ // L

    def to_chunks(a):
        return jnp.moveaxis(a.reshape(b_, h_, nc, L, a.shape[-1]), 2, 0)

    causal = jnp.tril(jnp.ones((L, L), dtype=bool))[..., None]

    def step(Sst, xs):
        qj, kj, vj, gj = xs
        bcum = jnp.cumsum(gj, axis=-2)
        diff = bcum[..., :, None, :] - bcum[..., None, :, :]
        dec = jnp.exp(jnp.where(causal, diff, -jnp.inf))
        A = jnp.einsum('bhjc,bhsc,bhjsc->bhjs', qj, kj, dec)
        o = jnp.einsum('bhjs,bhsv->bhjv', A, vj) + jnp.einsum('bhjc,bhcv->bhjv', qj * jnp.exp(bcum), Sst)
        bL = bcum[..., -1, :]
        S_new = jnp.exp(bL)[..., None] * Sst + jnp.einsum('bhsc,bhsv->bhcv', kj * jnp.exp(bL[..., None, :] - bcum), vj)
        return S_new, o

    init = jnp.zeros((b_, h_, dk, dv), jnp.float32)
    _, os_ = lax.scan(step, init, (to_chunks(q), to_chunks(k), to_chunks(v), to_chunks(logf)))
    return jnp.moveaxis(os_, 0, 2).reshape(b_, h_, s_, dv)

def hgrn2_layer(h, w_in, b_in, lb, head_norm, w_out):
    b_, s_, _ = h.shape
    proj = h @ w_in + b_in
    fp, iv, qp, z = jnp.split(proj, 4, axis=-1)
    logf = jnp.log(lb + (1.0 - lb) * jax.nn.sigmoid(fp))
    k = (1.0 - lb) * jax.nn.sigmoid(-fp)
    q = jax.nn.silu(qp)
    o = hgrn2_chunkwise(heads(q, HGRN_HEADS), heads(k, HGRN_HEADS), heads(iv, HGRN_HEADS), heads(logf, HGRN_HEADS))
    o = rms_norm(o.transpose(0, 2, 1, 3), head_norm.reshape(HGRN_HEADS, HGRN_HEAD_DIM)).reshape(b_, s_, HGRN_W)
    return (o * jax.nn.silu(z)) @ w_out

def even_layer(h, w_in, b_in, f_bias, conv_w, conv_b, head_norm, q_norm, k_norm,
               ck_pos, ck_w1, ck_w2, cv_pos, cv_w1, cv_w2, w_out):
    proj = h @ w_in + b_in
    m_cols, n_cols = jnp.split(proj, [MLSTM_COLS], axis=-1)
    ya = mlstm_branch(m_cols, f_bias, conv_w, conv_b, head_norm)
    yb = nsa_branch(n_cols, q_norm, k_norm, ck_pos, ck_w1, ck_w2, cv_pos, cv_w1, cv_w2)
    return jnp.concatenate([ya, yb], axis=-1) @ w_out

def first_inputs(seed: int = 0) -> dict:
    key = jax.random.key(seed)
    ks = jax.random.split(key, 24)

    def nrm(k, shape, scale):
        return scale * jax.random.normal(k, shape, jnp.float32)

    NE, NO = N_EVEN, N_ODD
    return {
        "x": nrm(ks[0], (BATCH, SEQ, D_MODEL), 1.0),
        "norm_w": 1.0 + nrm(ks[1], (DEPTH, D_MODEL), 0.02),
        "ev_w_in": nrm(ks[2], (NE, D_MODEL, EVEN_IN_COLS), D_MODEL ** -0.5),
        "ev_b_in": nrm(ks[3], (NE, EVEN_IN_COLS), 0.02),
        "mlstm_f_bias": jnp.linspace(3.0, 6.0, MLSTM_HEADS, dtype=jnp.float32)[None, :] + nrm(ks[4], (NE, MLSTM_HEADS), 0.1),
        "mlstm_conv_w": nrm(ks[5], (NE, CONV_K, 2 * MLSTM_W), CONV_K ** -0.5),
        "mlstm_conv_b": nrm(ks[6], (NE, 2 * MLSTM_W), 0.02),
        "mlstm_head_norm": 1.0 + nrm(ks[7], (NE, MLSTM_W), 0.02),
        "nsa_q_norm": 1.0 + nrm(ks[8], (NE, NSA_HEAD_DIM), 0.02),
        "nsa_k_norm": 1.0 + nrm(ks[9], (NE, 3, NSA_HEAD_DIM), 0.02),
        "cmp_k_pos": nrm(ks[10], (NE, CMP_LEN, NSA_HEAD_DIM), 0.1),
        "cmp_k_w1": nrm(ks[11], (NE, CMP_LEN * NSA_HEAD_DIM, CMP_HIDDEN), (CMP_LEN * NSA_HEAD_DIM) ** -0.5),
        "cmp_k_w2": nrm(ks[12], (NE, CMP_HIDDEN, NSA_HEAD_DIM), CMP_HIDDEN ** -0.5),
        "cmp_v_pos": nrm(ks[13], (NE, CMP_LEN, NSA_HEAD_DIM), 0.1),
        "cmp_v_w1": nrm(ks[14], (NE, CMP_LEN * NSA_HEAD_DIM, CMP_HIDDEN), (CMP_LEN * NSA_HEAD_DIM) ** -0.5),
        "cmp_v_w2": nrm(ks[15], (NE, CMP_HIDDEN, NSA_HEAD_DIM), CMP_HIDDEN ** -0.5),
        "ev_w_out": nrm(ks[16], (NE, EVEN_MIX_W, D_MODEL), EVEN_MIX_W ** -0.5),
        "od_w_in": nrm(ks[17], (NO, D_MODEL, ODD_IN_COLS), D_MODEL ** -0.5),
        "od_b_in": nrm(ks[18], (NO, ODD_IN_COLS), 0.02),
        "hgrn_lb_logits": nrm(ks[19], (NO + 1, HGRN_W), 0.5),
        "hgrn_head_norm": 1.0 + nrm(ks[20], (NO, HGRN_W), 0.02),
        "od_w_out": nrm(ks[21], (NO, HGRN_W, D_MODEL), HGRN_W ** -0.5),
    }

def first_block(x, norm_w, ev_w_in, ev_b_in, mlstm_f_bias, mlstm_conv_w, mlstm_conv_b, mlstm_head_norm,
              nsa_q_norm, nsa_k_norm, cmp_k_pos, cmp_k_w1, cmp_k_w2, cmp_v_pos, cmp_v_w1, cmp_v_w2,
              ev_w_out, od_w_in, od_b_in, hgrn_lb_logits, hgrn_head_norm, od_w_out):
    lbs = jnp.cumsum(jax.nn.softmax(hgrn_lb_logits.astype(jnp.float32), axis=0), axis=0)
    for layer in range(DEPTH):
        h = rms_norm(x, norm_w[layer])
        j = layer // 2
        if layer % 2 == 0:
            y = even_layer(h, ev_w_in[j], ev_b_in[j], mlstm_f_bias[j], mlstm_conv_w[j], mlstm_conv_b[j],
                           mlstm_head_norm[j], nsa_q_norm[j], nsa_k_norm[j], cmp_k_pos[j], cmp_k_w1[j],
                           cmp_k_w2[j], cmp_v_pos[j], cmp_v_w1[j], cmp_v_w2[j], ev_w_out[j])
        else:
            y = hgrn2_layer(h, od_w_in[j], od_b_in[j], lbs[j], hgrn_head_norm[j], od_w_out[j])
        x = x + y.astype(x.dtype)
    return x


N_MIXERS = 3
POOL_WINDOWS = (2, 4, 8, 16)
POOL_GROUPS = len(POOL_WINDOWS)
POOL_GROUP_DIM = D_MODEL // POOL_GROUPS
SGU_CHUNK = 128
SGU_WIDTH = D_MODEL
SGU_HEAD_DIM = 128
SGU_HEADS = SGU_WIDTH // SGU_HEAD_DIM
MLA_HEADS = 16
MLA_Q_LORA = 256
MLA_KV_LORA = 128
MLA_NOPE = 128
MLA_ROPE = 64
MLA_V = 128
ROPE_THETA_2 = 10000.0
D_FF = 4 * D_MODEL
RMS_EPS = 1e-6
LN_EPS = 1e-5
MAX_POS_OFFSET = 4096
N_POOL_LAYERS = len(range(0, DEPTH, N_MIXERS))
N_SGU_LAYERS = len(range(1, DEPTH, N_MIXERS))
N_MLA_LAYERS = len(range(2, DEPTH, N_MIXERS))


def rmsnorm(x, g):
    xf = x.astype(jnp.float32)
    y = xf * lax.rsqrt(jnp.mean(xf * xf, axis=-1, keepdims=True) + RMS_EPS)
    return (y * g.astype(jnp.float32)).astype(x.dtype)

def layernorm(x, g, b):
    xf = x.astype(jnp.float32)
    mu = jnp.mean(xf, axis=-1, keepdims=True)
    xc = xf - mu
    var = jnp.mean(xc * xc, axis=-1, keepdims=True)
    y = xc * lax.rsqrt(var + LN_EPS)
    return (y * g.astype(jnp.float32) + b.astype(jnp.float32)).astype(x.dtype)

def modulate(h, shift, scale):
    return h * (1.0 + scale[:, None, :]) + shift[:, None, :]

def pool_mixer(h, w, scale):
    B_, S_, _ = h.shape
    hf = h.astype(jnp.float32).reshape(B_, S_, POOL_GROUPS, POOL_GROUP_DIM)
    cs = jnp.cumsum(hf, axis=1)
    cs = jnp.concatenate([jnp.zeros_like(cs[:, :1]), cs], axis=1)
    t = jnp.arange(S_, dtype=jnp.float32)
    outs = []
    for gi, win in enumerate(POOL_WINDOWS):
        csg = cs[:, :, gi]
        upper = csg[:, 1:]
        lower = jnp.concatenate([jnp.zeros_like(csg[:, :win - 1]), csg[:, :S_ - win + 1]], axis=1)
        count = jnp.minimum(t + 1.0, float(win))[None, :, None]
        outs.append((upper - lower) / count - hf[:, :, gi])
    pooled = jnp.stack(outs, axis=2).astype(h.dtype)
    y = jnp.einsum('bsgc,gcd->bsgd', pooled, w).reshape(B_, S_, D_MODEL)
    return y * scale

def sgu_mixer(h, w_in, ln_g, ln_b, w_s, b_s, w_out):
    B_, S_, _ = h.shape
    z = jax.nn.gelu(h @ w_in, approximate=False)
    u, v = jnp.split(z, 2, axis=-1)
    v = layernorm(v, ln_g, ln_b)
    nc = S_ // SGU_CHUNK
    v = v.reshape(B_, nc, SGU_CHUNK, SGU_HEADS, SGU_HEAD_DIM)
    mask = jnp.tril(jnp.ones((SGU_CHUNK, SGU_CHUNK), dtype=bool))
    ws = jnp.where(mask[None], w_s, 0)
    mixed = jnp.einsum('hts,bnshc->bnthc', ws, v) + b_s.T[None, None, :, :, None]
    gated = u * mixed.reshape(B_, S_, SGU_WIDTH)
    return gated @ w_out

def apply_rope(x, cos, sin):
    x1, x2 = jnp.split(x, 2, axis=-1)
    return jnp.concatenate([x1 * cos - x2 * sin, x2 * cos + x1 * sin], axis=-1)

def mla_mixer(h, positions, w_dq_dkv, q_norm_g, kv_norm_g, w_uq, w_ukv, w_o):
    B_, S_, _ = h.shape
    lat = h @ w_dq_dkv
    c_q, c_kv, k_rope = jnp.split(lat, [MLA_Q_LORA, MLA_Q_LORA + MLA_KV_LORA], axis=-1)
    c_q = rmsnorm(c_q, q_norm_g)
    c_kv = rmsnorm(c_kv, kv_norm_g)
    q = (c_q @ w_uq).reshape(B_, S_, MLA_HEADS, MLA_NOPE + MLA_ROPE)
    q_nope, q_rope = jnp.split(q, [MLA_NOPE], axis=-1)
    kv = (c_kv @ w_ukv).reshape(B_, S_, MLA_HEADS, MLA_NOPE + MLA_V)
    k_nope, v = jnp.split(kv, [MLA_NOPE], axis=-1)
    inv_freq = ROPE_THETA_2 ** (-jnp.arange(0, MLA_ROPE, 2, dtype=jnp.float32) / MLA_ROPE)
    ang = positions.astype(jnp.float32)[..., None] * inv_freq
    cos, sin = jnp.cos(ang), jnp.sin(ang)
    q_rope = apply_rope(q_rope.astype(jnp.float32), cos[:, :, None], sin[:, :, None]).astype(h.dtype)
    k_rope = apply_rope(k_rope.astype(jnp.float32), cos, sin).astype(h.dtype)
    sm_scale = (MLA_NOPE + MLA_ROPE) ** -0.5
    nb = S_ // Q_BLOCK

    def to_blocks(t):
        return jnp.moveaxis(t.reshape(B_, nb, Q_BLOCK, *t.shape[2:]), 1, 0)

    k_idx = jnp.arange(S_)

    def attend_block(args):
        qn, qr, blk = args
        s = jnp.einsum('bqhd,bkhd->bhqk', qn, k_nope, preferred_element_type=jnp.float32)
        s = s + jnp.einsum('bqhr,bkr->bhqk', qr, k_rope, preferred_element_type=jnp.float32)
        q_idx = blk * Q_BLOCK + jnp.arange(Q_BLOCK)
        causal = k_idx[None, :] <= q_idx[:, None]
        s = jnp.where(causal[None, None], s * sm_scale, -1e30)
        p = jax.nn.softmax(s, axis=-1).astype(v.dtype)
        return jnp.einsum('bhqk,bkhd->bqhd', p, v)

    out = lax.map(attend_block, (to_blocks(q_nope), to_blocks(q_rope), jnp.arange(nb)))
    out = jnp.moveaxis(out, 0, 1).reshape(B_, S_, MLA_HEADS * MLA_V)
    return out @ w_o

def sq_relu_mlp(h, w1, w2):
    return jnp.square(jax.nn.relu(h @ w1)) @ w2

def second_inputs(seed: int = 0) -> dict:
    key = jax.random.key(seed)
    ks = jax.random.split(key, 32)
    f32 = jnp.float32

    def nrm(k, shape, std):
        return jax.random.normal(k, shape, f32) * std

    def gain(k, shape):
        return 1.0 + 0.1 * jax.random.normal(k, shape, f32)

    x = jax.random.normal(ks[0], (BATCH, SEQ, D_MODEL), f32)
    c = jax.random.normal(ks[1], (BATCH, D_MODEL), f32)
    offset = jax.random.randint(ks[2], (BATCH, 1), 0, MAX_POS_OFFSET, dtype=jnp.int32)
    positions = (offset + jnp.arange(SEQ, dtype=jnp.int32)[None, :]).astype(jnp.int32)
    return {
        'x': x,
        'c': c,
        'positions': positions,
        'ada_w': nrm(ks[3], (DEPTH, D_MODEL, 6 * D_MODEL), 0.5 * D_MODEL ** -0.5),
        'ada_b': nrm(ks[4], (DEPTH, 6 * D_MODEL), 0.02),
        'norm_mix_g': gain(ks[5], (DEPTH, D_MODEL)),
        'norm_mlp_g': gain(ks[6], (DEPTH, D_MODEL)),
        'pool_w': nrm(ks[7], (N_POOL_LAYERS, POOL_GROUPS, POOL_GROUP_DIM, POOL_GROUP_DIM), POOL_GROUP_DIM ** -0.5),
        'pool_scale': gain(ks[8], (N_POOL_LAYERS, D_MODEL)),
        'sgu_w_in': nrm(ks[9], (N_SGU_LAYERS, D_MODEL, 2 * SGU_WIDTH), D_MODEL ** -0.5),
        'sgu_ln_g': gain(ks[10], (N_SGU_LAYERS, SGU_WIDTH)),
        'sgu_ln_b': nrm(ks[11], (N_SGU_LAYERS, SGU_WIDTH), 0.02),
        'sgu_w_s': nrm(ks[12], (N_SGU_LAYERS, SGU_HEADS, SGU_CHUNK, SGU_CHUNK), SGU_CHUNK ** -0.5),
        'sgu_b_s': gain(ks[13], (N_SGU_LAYERS, SGU_HEADS, SGU_CHUNK)),
        'sgu_w_out': nrm(ks[14], (N_SGU_LAYERS, SGU_WIDTH, D_MODEL), SGU_WIDTH ** -0.5),
        'mla_w_dq_dkv': nrm(ks[15], (N_MLA_LAYERS, D_MODEL, MLA_Q_LORA + MLA_KV_LORA + MLA_ROPE), D_MODEL ** -0.5),
        'mla_q_norm_g': gain(ks[16], (N_MLA_LAYERS, MLA_Q_LORA)),
        'mla_kv_norm_g': gain(ks[17], (N_MLA_LAYERS, MLA_KV_LORA)),
        'mla_w_uq': nrm(ks[18], (N_MLA_LAYERS, MLA_Q_LORA, MLA_HEADS * (MLA_NOPE + MLA_ROPE)), MLA_Q_LORA ** -0.5),
        'mla_w_ukv': nrm(ks[19], (N_MLA_LAYERS, MLA_KV_LORA, MLA_HEADS * (MLA_NOPE + MLA_V)), MLA_KV_LORA ** -0.5),
        'mla_w_o': nrm(ks[20], (N_MLA_LAYERS, MLA_HEADS * MLA_V, D_MODEL), (MLA_HEADS * MLA_V) ** -0.5),
        'mlp_w1': nrm(ks[21], (DEPTH, D_MODEL, D_FF), D_MODEL ** -0.5),
        'mlp_w2': nrm(ks[22], (DEPTH, D_FF, D_MODEL), D_FF ** -0.5),
        'final_g': gain(ks[23], (D_MODEL,)),
    }

def second_block(x, c, positions, ada_w, ada_b, norm_mix_g, norm_mlp_g, pool_w, pool_scale,
              sgu_w_in, sgu_ln_g, sgu_ln_b, sgu_w_s, sgu_b_s, sgu_w_out,
              mla_w_dq_dkv, mla_q_norm_g, mla_kv_norm_g, mla_w_uq, mla_w_ukv, mla_w_o,
              mlp_w1, mlp_w2, final_g):
    c_act = jax.nn.silu(c)
    for i in range(DEPTH):
        mod = c_act @ ada_w[i] + ada_b[i]
        sh1, sc1, g1, sh2, sc2, g2 = jnp.split(mod, 6, axis=-1)
        h = modulate(rmsnorm(x, norm_mix_g[i]), sh1, sc1)
        kind, j = i % N_MIXERS, i // N_MIXERS
        if kind == 0:
            y = pool_mixer(h, pool_w[j], pool_scale[j])
        elif kind == 1:
            y = sgu_mixer(h, sgu_w_in[j], sgu_ln_g[j], sgu_ln_b[j], sgu_w_s[j], sgu_b_s[j], sgu_w_out[j])
        else:
            y = mla_mixer(h, positions, mla_w_dq_dkv[j], mla_q_norm_g[j], mla_kv_norm_g[j],
                          mla_w_uq[j], mla_w_ukv[j], mla_w_o[j])
        x = x + g1[:, None, :] * y
        h = modulate(rmsnorm(x, norm_mlp_g[i]), sh2, sc2)
        x = x + g2[:, None, :] * sq_relu_mlp(h, mlp_w1[i], mlp_w2[i])
    return rmsnorm(x, final_g)


def setup_inputs(seed=0):
    out = dict(first_inputs(seed))
    for name, value in second_inputs(seed + 1).items():
        if name != "x":
            out[name + "_2"] = value
    return out


def reference(
    x, norm_w, ev_w_in, ev_b_in, mlstm_f_bias, mlstm_conv_w, mlstm_conv_b, mlstm_head_norm,
    nsa_q_norm, nsa_k_norm, cmp_k_pos, cmp_k_w1, cmp_k_w2, cmp_v_pos, cmp_v_w1, cmp_v_w2,
    ev_w_out, od_w_in, od_b_in, hgrn_lb_logits, hgrn_head_norm, od_w_out, c_2, positions_2,
    ada_w_2, ada_b_2, norm_mix_g_2, norm_mlp_g_2, pool_w_2, pool_scale_2, sgu_w_in_2,
    sgu_ln_g_2, sgu_ln_b_2, sgu_w_s_2, sgu_b_s_2, sgu_w_out_2, mla_w_dq_dkv_2, mla_q_norm_g_2,
    mla_kv_norm_g_2, mla_w_uq_2, mla_w_ukv_2, mla_w_o_2, mlp_w1_2, mlp_w2_2, final_g_2,
):
    x = first_block(
        x, norm_w, ev_w_in, ev_b_in, mlstm_f_bias, mlstm_conv_w, mlstm_conv_b, mlstm_head_norm,
        nsa_q_norm, nsa_k_norm, cmp_k_pos, cmp_k_w1, cmp_k_w2, cmp_v_pos, cmp_v_w1, cmp_v_w2,
        ev_w_out, od_w_in, od_b_in, hgrn_lb_logits, hgrn_head_norm, od_w_out,
    )
    return second_block(
        x, c_2, positions_2, ada_w_2, ada_b_2, norm_mix_g_2, norm_mlp_g_2, pool_w_2,
        pool_scale_2, sgu_w_in_2, sgu_ln_g_2, sgu_ln_b_2, sgu_w_s_2, sgu_b_s_2, sgu_w_out_2,
        mla_w_dq_dkv_2, mla_q_norm_g_2, mla_kv_norm_g_2, mla_w_uq_2, mla_w_ukv_2, mla_w_o_2,
        mlp_w1_2, mlp_w2_2, final_g_2,
    )


_drawn_inputs = setup_inputs


def setup_inputs(seed=0):
    import zlib

    import numpy as np

    out = dict(_drawn_inputs(seed))
    spreads = {}
    factors = {'norm_w': 2.876,
     'mlstm_conv_b': 22.182,
     'mlstm_head_norm': 8.0,
     'nsa_q_norm': 8.0,
     'nsa_k_norm': 8.0,
     'cmp_k_pos': 8.0,
     'cmp_v_pos': 3.764,
     'hgrn_head_norm': 20.189,
     'sgu_ln_g_2': 38.056,
     'sgu_ln_b_2': 200.0,
     'sgu_b_s_2': 26.128,
     'od_b_in': 4.008,
     'ada_b_2': 8.0,
     'norm_mix_g_2': 5.767,
     'norm_mlp_g_2': 8.0,
     'pool_w_2': 2.799,
     'pool_scale_2': 8.0}
    for name, (base, spread) in spreads.items():
        noise = np.random.default_rng([zlib.crc32(name.encode()), seed]).standard_normal(out[name].shape)
        drawn = base * np.exp(spread * noise) if base else spread * noise
        out[name] = __import__('jax').numpy.asarray(drawn.astype(out[name].dtype))
    for name, factor in factors.items():
        out[name] = (out[name] * factor).astype(out[name].dtype)
    return out
```

```python
from contextlib import ExitStack

import concourse.bass as bass
from concourse import mybir

F32 = mybir.dt.float32
I32 = mybir.dt.int32
ALU = mybir.AluOpType
ACT = mybir.ActivationFunctionType
AX = mybir.AxisListType.X

P = 128
T = 256
NT = T // P
D = 1024
KT = D // P
CW = 256
EPS = 1e-6
LN_EPS = 1e-5
NEG = -1e30

MH = 4
MW = MH * P
NH, NG, ND = 8, 2, 64
NR = NH // NG
NW_ = NH * ND
C_GATE = 5 * MW
C_NQ = C_GATE + 2 * MH
C_KV = C_NQ + NW_
C_GT = C_KV + 6 * NG * ND
C_NZ = C_GT + 3 * NH
NGATE = 2 * MH + 3 * NH
CMP_LEN, CMP_STRIDE = 32, 16
NCMP = (T - CMP_LEN) // CMP_STRIDE + 1
CPAD = 32
TAPS = 4
HH = 8
LEVELS = 7
FF = 4 * D
FT = FF // P
POOLS = (2, 4, 8, 16)
PADW = 16

_c = {}
_at = 0
for _n, _w in (("idn", P), ("one", P), ("b64", P), ("m1", T), ("mc", NT * NCMP), ("mc01", NT * NCMP),
               ("prm", P), ("cos", T), ("sin", T), ("tri", P), ("sel", MH * P), ("lvl", (LEVELS + 1) * P),
               ("prc", len(POOLS) * PADW), ("rg", 4)):
    _c[_n] = (_at, _at + _w)
    _at += _w
NCST = _at

PA = dict(nw=0, b20=16, bnq=36, bkv=40, bnz=46, cvb=50, mhn=58, qn=62, kn=63, kpos=66, vpos=82)
NA_ROWS = 98
PB = dict(cvw=128, odb=160, lbl=192, hhn=208, fg=216, c=224, psc=232)
NB_ROWS = 112
PC = dict(adab=256, nmix=352, nmlp=368)
NC_ROWS = 128

NSLOT = 6
NBANK = 7


def constants():
    import numpy as np
    c = np.zeros((P, NCST), np.float32)

    def put(name, a):
        lo, hi = _c[name]
        c[: a.shape[0], lo:hi] = a.reshape(a.shape[0], hi - lo)

    i = np.arange(P)
    put("idn", np.eye(P, dtype=np.float32))
    put("one", np.ones((P, P), np.float32))
    put("b64", (i[:, None] // ND == i[None] // ND).astype(np.float32))
    tri = np.where(i[None] <= i[:, None], 0.0, NEG).astype(np.float32)
    put("m1", np.concatenate([np.zeros((P, P), np.float32), tri], 1))
    t = np.arange(T).reshape(NT, P).T
    ok = (np.arange(NCMP) * CMP_STRIDE + CMP_LEN - 1)[None, None] <= t[:, :, None]
    put("mc", np.where(ok, 0.0, NEG).astype(np.float32))
    put("mc01", ok.astype(np.float32))
    half = ND // 8
    prm = np.zeros((P, P), np.float32)
    for g in range(NG):
        for d in range(half):
            prm[g * ND + d + half, g * ND + d] = -1.0
            prm[g * ND + d, g * ND + d + half] = 1.0
    put("prm", prm)
    inv = (np.float32(500000.0) ** (-np.arange(half, dtype=np.float32) / half)).astype(np.float32)
    ang = np.arange(T, dtype=np.float32)[None] * inv[:, None]
    cos, sin = np.ones((P, T), np.float32), np.zeros((P, T), np.float32)
    for g in range(NG):
        for h in range(2):
            at = g * ND + h * half
            cos[at:at + half], sin[at:at + half] = np.cos(ang), np.sin(ang)
    put("cos", cos)
    put("sin", sin)
    put("tri", (i[:, None] <= i[None]).astype(np.float32))
    sel = np.zeros((MH, MH, P), np.float32)
    for h in range(MH):
        sel[h, h] = 1.0
    put("sel", sel)
    lv = []
    for l in range(LEVELS):
        m = P >> (l + 1)
        s, j = i[:, None], i[None]
        lv.append(((s // (2 * m) == j // (2 * m)) & (s % (2 * m) < m) & (j % (2 * m) >= m)).astype(np.float32))
    lv.append(np.eye(P, dtype=np.float32))
    put("lvl", np.stack(lv, 1))
    pr = np.zeros((P, len(POOLS), PADW), np.float32)
    for g, w in enumerate(POOLS):
        pr[:, g] = w / np.minimum(np.arange(PADW) + 1.0, w)
    put("prc", pr)
    put("rg", (i[:, None] // CPAD == np.arange(4)[None]).astype(np.float32))
    return c


def weight_chunks(A):
    out = []

    def cols(name, w, c0, n=CW, rows=0):
        src = w[rows:rows + KT * P, c0:c0 + n].rearrange("(k p) n -> p k n", p=P)
        out.append((name, [((slice(0, KT), slice(0, n)), src)]))

    w = A["ev_w_in"][0]
    out.append(("gt", [((slice(0, KT), slice(0, 2 * MH)), w[:, C_GATE:C_NQ].rearrange("(k p) n -> p k n", p=P)),
                       ((slice(0, KT), slice(2 * MH, NGATE)), w[:, C_GT:C_NZ].rearrange("(k p) n -> p k n", p=P))]))
    for n, c0 in (("q", 0), ("k", MW), ("v", 2 * MW)):
        for j in range(2):
            cols(f"{n}{j}", w, c0 + j * CW)

    def paired(n, c0):
        for j in range(2):
            parts = []
            for b in range(2):
                for g in range(NG):
                    s = c0 + (g * NR + 2 * j + b) * ND
                    parts.append(((slice(0, KT), slice(b * P + g * ND, b * P + g * ND + ND)),
                                  w[:, s:s + ND].rearrange("(k p) n -> p k n", p=P)))
            out.append((f"{n}{j}", parts))

    paired("nq", C_NQ)
    for j, n in enumerate(("kcvc", "ksvs", "kwvw")):
        cols(n, w, C_KV + j * CW)
    for n, c0 in (("o", 3 * MW), ("z", 4 * MW)):
        for j in range(2):
            cols(f"{n}{j}", w, c0 + j * CW)
    paired("nz", C_NZ)
    for n in ("cmp_k_w1", "cmp_v_w1"):
        out.append((n, [((slice(0, None), slice(0, None)), A[n][0].rearrange("(m p) n -> p m n", p=P))]))
    ada = A["ada_w_2"]

    def adas(l, lo, hi):
        for j in range(lo, hi):
            cols(f"ada{l}_{j}", ada[l], j * CW)

    adas(0, 0, 24)
    wo = A["ev_w_out"][0]
    for j in range(4):
        parts = [((slice(0, MH), slice(0, CW)), wo[0:MW, j * CW:(j + 1) * CW].rearrange("(k p) n -> p k n", p=P))]
        for g in range(NG):
            parts.append(((slice(MH, KT), slice(0, CW), g),
                          wo[MW + g * NR * ND:MW + (g + 1) * NR * ND, j * CW:(j + 1) * CW]
                          .rearrange("(b d) n -> d b n", d=ND)))
        out.append((f"eo{j}", parts))
    wi = A["od_w_in"][0]
    for n, c0 in (("fp", 0), ("qp", 2 * D), ("iv", D), ("hz", 3 * D)):
        for j in range(4):
            cols(f"{n}{j}", wi, c0 + j * CW)
    adas(1, 0, 24)
    for j in range(4):
        cols(f"oo{j}", A["od_w_out"][0], j * CW)
    out.append(("pool", [((slice(0, KT), slice(0, CW)), A["pool_w_2"][0].rearrange("g (k p) n -> p (g k) n", p=P))]))

    def mlp(l):
        for j in range(FF // CW):
            cols(f"w1_{l}_{j}", A["mlp_w1_2"][l], j * CW)
        for j in range(4):
            for k in range(4):
                cols(f"w2_{l}_{j}_{k}", A["mlp_w2_2"][l], j * CW, rows=k * D)

    mlp(0)
    for j in range(8):
        cols(f"si{j}", A["sgu_w_in_2"][0], j * CW)
    for j in range(4):
        cols(f"so{j}", A["sgu_w_out_2"][0], j * CW)
    mlp(1)
    return out


def build(nc, A, cst_dram, out_dram):
    ctx = ExitStack()
    with ctx:
        sems = {}

        def S(name):
            if name not in sems:
                sems[name] = ctx.enter_context(nc.semaphore("s_" + name))
            return sems[name]

        def sb(name, shape, dt=F32):
            return ctx.enter_context(nc.sbuf_tensor(name, shape, dt))

        cst = sb("cst", [P, NCST])
        par = sb("par", [P, 384])
        xT = sb("xT", [P, KT, T])
        hT = sb("hT", [P, KT, PADW + T])
        yT = sb("yT", [P, KT, T])
        sq = sb("sq", [P, KT * T])
        wring = sb("wring", [P, NSLOT, KT * CW])
        bcb = sb("bcb", [P, 512 + 128 + 128 + 32 + 4 + 1024])
        sm = sb("sm", [P, 1024])
        mod = sb("mod", [P, 2, 48])
        nrm = sb("nrm", [P, 2 * T])
        AR = 24320
        ar = sb("ar", [P, AR])
        ps = [ctx.enter_context(nc.psum_tensor(f"ps{i}", [P, 512], F32)) for i in range(NBANK)]
        adaps = ctx.enter_context(nc.psum_tensor("adaps", [P, 512], F32))

        def K(name):
            lo, hi = _c[name]
            return cst[:, lo:hi]

        idn, one, b64 = K("idn"), K("one"), K("b64")
        hx = hT[:, :, PADW:PADW + T]

        def cut(at, size, pat=None, **kw):
            v = ar[:, at:at + size]
            return v.rearrange(pat, **kw) if pat else v

        qkp = cut(0, 8 * 259, "p (b t) -> p b t", t=259)
        qkc = cut(2072, 2048, "p (b t) -> p b t", t=T)
        vtok = cut(4120, 1024, "p (a n) -> p a n", a=NT)
        ET = cut(5144, 1536, "p (h n) -> p h n", h=MH)
        ST = cut(6680, 1536, "p (h n) -> p h n", h=MH)
        emrb = cut(8216, 1024)
        P1 = cut(0, 4096, "p (h y k) -> p h y k", h=NH, y=2)
        P0 = cut(4096, 2048, "p (h y k) -> p h y k", h=NH, y=2)
        Pc = cut(6144, 512, "p (a h n) -> p a h n", a=NT, h=NH)
        PT1 = cut(6656, 4096, "p (h y k) -> p h y k", h=NH, y=4)
        PT0 = cut(10752, 2048, "p (h y k) -> p h y k", h=NH, y=2)
        PTc = cut(12800, 512, "p (a g k) -> p a g k", a=NT, g=NG)
        at = 13312
        og = cut(at, 1024); at += 1024
        zg = cut(at, 1024); at += 1024
        nz = cut(at, 1024); at += 1024
        R = cut(at, 1536 + NCMP); at += 1552
        R2 = cut(at, 1536 + NCMP); at += 1552
        hm = cut(at, 1024); at += 1024
        XK = cut(at, 512, "p (g t) -> p g t", g=NG); at += 512
        XV = cut(at, 512, "p (g t) -> p g t", g=NG); at += 512
        kcvc = cut(at, 512, "p (y t) -> p y t", y=2); at += 512
        CR = cut(at, 960, "p (y m g n) -> p y m g n", y=2, m=16, g=NG); at += 960
        vsw = cut(at, 512, "p (y a n) -> p y a n", y=2, a=NT); at += 512
        VC = cut(at, 128); at += 128
        VC4 = cut(at, 512, "p (i d) -> p i d", i=4); at += 512
        assert at <= AR, at
        hb = cut(0, 2048)
        hb2 = cut(2048, 2048)
        hk = cut(4096, 2048)
        hq = cut(6144, 2048)
        hz = cut(8192, 2048)
        ht = cut(10240, 2048, "p (a n) -> p a n", a=NT)
        LE = [cut(12288, 2048), cut(14336, 2048)]
        LQ = [cut(16384, 2048), cut(18432, 2048)]
        ATm = cut(20480, 2048, "p (n j) -> p n j", n=2 * HH)
        AT2 = cut(22528, 1024, "p (h j) -> p h j", h=HH)
        rst = LQ[0]
        hO = hb2
        h1 = cut(0, 8192, "p (f t) -> p f t", f=FT)
        rl = [cut(8192, 512), cut(8704, 512)]
        s2 = cut(9216, 8 * 272, "p (b t) -> p b t", t=272)
        s4 = cut(9216 + 2176, 8 * 272, "p (b t) -> p b t", t=272)
        pl = cut(9216 + 4352, 2048, "p (b t) -> p b t", t=T)
        uT = cut(9216, 2048, "p (b t) -> p b t", t=T)
        vt = cut(11264, 2048, "p (a n) -> p a n", a=NT)
        xc = cut(13312, 2048, "p (a n) -> p a n", a=NT)
        lng = cut(15616, 1024)
        lnb = cut(16640, 1024)
        bsb = cut(17664, 1024, "p (h t) -> p h t", h=8)
        wst = cut(18688, 1024, "p (h t) -> p h t", h=8)
        wsT = cut(19712, 1024, "p (h t) -> p h t", h=8)
        ot = cut(0, 2048, "p (a n) -> p a n", a=NT)
        xtok = cut(0, 2048, "p (a n) -> p a n", a=NT)
        rows = [cut(2048 + i * P, P) for i in range(3)]

        smat = [0]

        def small(n):
            smat[0] += n
            assert smat[0] <= 1024
            return sm[:, smat[0] - n:smat[0]]

        gt = small(NT * NGATE).rearrange("p (a n) -> p a n", a=NT)
        acol = small(NT * MH).rearrange("p (a n) -> p a n", a=NT)
        cs = small(KT)
        mx1, mx0, mxc = small(16), small(16), small(16)
        sm1, sm0, smc = small(16), small(16), small(16)
        hk_ = small(NG * NCMP + 2)
        hv_ = small(NG * NCMP + 2)
        hvp = small(NG * 4 * CPAD)
        w2k, w2v = small(ND), small(ND)
        lb, lbt, oml, nodb = small(HH), small(HH), small(HH), small(HH)
        A1 = [small(KT), small(KT), small(KT), small(KT)]
        gsc = small(KT)
        mu, vr = small(NT), small(NT)
        var, rstd = nrm[:, 0:T], nrm[:, T:2 * T]
        rw = yT[:, :, :].rearrange("p b t -> p (b t)")[:, :]
        irow, frow, brow, arow, grow, erow, trow, orow = [rw[0:MH, i * T:(i + 1) * T] for i in range(8)]

        chunks = weight_chunks(A)
        landed, total = {}, [0] * NSLOT
        order = {}
        for i, (name, parts) in enumerate(chunks):
            total[i % NSLOT] += 16 * len(parts)
            landed[name] = (i % NSLOT, total[i % NSLOT])
            order[name] = i
        released = {}
        place = {}
        fills = [0] * NBANK
        count = dict(unit=0, chunk=0, mid=0)

        def got(eng, name):
            b, n = place[name]
            eng.wait_ge(S(f"full{b}"), n)
            return ps[b]

        def free(ins, name):
            ins.then_inc(S(f"free{place[name][0]}"), 1)

        def done(eng, name):
            b, n = place[name]
            eng.wait_ge(S(f"free{b}"), n)

        block = ctx.enter_context(nc.Block())

        @block.tensor
        def _(pe):
            def begin(name):
                b = count["unit"] % NBANK
                count["unit"] += 1
                if fills[b]:
                    pe.wait_ge(S(f"free{b}"), fills[b])
                fills[b] += 1
                place[name] = (b, fills[b])
                return ps[b]

            def end(ins, name, chunk=None):
                ins.then_inc(S(f"full{place[name][0]}"), 1)
                if chunk:
                    released[chunk] = (S(f"full{place[name][0]}"), place[name][1])

            def weights(name, w=CW):
                assert order[name] == count["chunk"], name
                count["chunk"] += 1
                slot, n = landed[name]
                pe.wait_ge(S(f"w{slot}"), n)
                return wring[:, slot, :].rearrange("p (k n) -> p k n", n=w)

            mm = pe.matmul

            def feat(name, rhs, hsem=None, chunk=None):
                o = begin(name)
                w = weights(name)
                for j in range(2):
                    for k in range(KT):
                        if hsem and j == 0:
                            pe.wait_ge(hsem, k + 1)
                        ins = mm(o[:, j * T:(j + 1) * T], w[:, k, j * P:(j + 1) * P], rhs[:, k, :],
                                 start=(k == 0), stop=(k == KT - 1))
                end(ins, name, name)

            def tok(name, act):
                o = begin(name)
                w = weights(name)
                for a in range(NT):
                    for k in range(KT):
                        ins = mm(o[:, a * CW:(a + 1) * CW], act[:, k, a * P:(a + 1) * P], w[:, k, :],
                                 start=(k == 0), stop=(k == KT - 1))
                end(ins, name, name)

            def sumsq(n):
                o = begin(f"ss{n}")
                for k in range(KT):
                    if k % 2 == 0:
                        pe.wait_ge(S("sq"), 4 * n + k // 2 + 1)
                    ins = mm(o[:, 0:T], one, sq[:, k * T:(k + 1) * T], start=(k == 0), stop=(k == KT - 1))
                end(ins, f"ss{n}")

            def ada(l, j):
                if j == 0:
                    pe.wait_ge(S("cs"), 1)
                    if l:
                        pe.wait_ge(S("mod"), 1)
                w = weights(f"ada{l}_{j}")
                for i in range(2):
                    c = l * 48 + 2 * j + i
                    for k in range(KT):
                        ins = mm(adaps[:, c:c + 1], w[:, k, i * P:(i + 1) * P], cs[:, k:k + 1],
                                 start=(k == 0), stop=(k == KT - 1))
                ins.then_inc(S("ada"), 1)
                released[f"ada{l}_{j}"] = (S("ada"), l * 24 + j + 1)

            pe.wait_ge(S("ld_cst"), 16)
            pe.wait_ge(S("ld_x"), 32)
            for i in range(4):
                o = begin(f"x{i}")
                for k in range(4):
                    f = 4 * (i % 2) + k
                    ins = pe.transpose(o[:, k * P:(k + 1) * P], xtok[:, i // 2, f * P:(f + 1) * P], idn)
                end(ins, f"x{i}")
            for i, (nm, n) in enumerate((("ld_A", NA_ROWS), ("ld_B", NB_ROWS), ("ld_C", NC_ROWS))):
                pe.wait_ge(S(nm), 16 * DMAS[nm])
                o = begin(f"par{i}")
                end(pe.transpose(o[:, 0:n], rows[i][0:n, :], idn[0:n, 0:n]), f"par{i}")
            sumsq(0)

            h0 = S("h0")
            o = begin("gt")
            w = weights("gt")
            for a in range(NT):
                for k in range(KT):
                    if a == 0:
                        pe.wait_ge(h0, k + 1)
                    ins = mm(o[:, a * NGATE:(a + 1) * NGATE], hx[:, k, a * P:(a + 1) * P], w[:, k, 0:NGATE],
                             start=(k == 0), stop=(k == KT - 1))
            end(ins, "gt", "gt")
            for n in ("q0", "q1", "k0", "k1"):
                feat(n, hx)
            tok("v0", hx)
            tok("v1", hx)
            pe.wait_ge(S("gt"), 1)
            o = begin("gtT")
            for y in range(2):
                for a in range(NT):
                    c = (y * NT + a) * P
                    ins = pe.transpose(o[0:MH, c:c + P], gt[:, a, y * MH:(y + 1) * MH], idn)
            end(ins, "gtT")
            feat("nq0", hx)
            feat("nq1", hx)
            feat("kcvc", hx)
            for n in ("ksvs", "kwvw"):
                o = begin(n)
                w = weights(n)
                for k in range(KT):
                    mm(o[:, 0:T], w[:, k, 0:P], hx[:, k, :], start=(k == 0), stop=(k == KT - 1))
                for a in range(NT):
                    for k in range(KT):
                        ins = mm(o[:, T + a * P:T + (a + 1) * P], hx[:, k, a * P:(a + 1) * P], w[:, k, P:2 * P],
                                 start=(k == 0), stop=(k == KT - 1))
                end(ins, n, n)
            pe.wait_ge(S("arow"), 1)
            o = begin("aT")
            for a in range(NT):
                ins = pe.transpose(o[:, a * MH:(a + 1) * MH], arow[:, a * P:(a + 1) * P], idn[0:MH, 0:MH])
            end(ins, "aT")
            for nm, row, sem in (("gb", grow, "grow"), ("em", erow, "erow")):
                pe.wait_ge(S(sem), 1)
                for i in range(2):
                    o = begin(f"{nm}{i}")
                    for j in range(2):
                        h = 2 * i + j
                        ins = mm(o[:, j * T:(j + 1) * T], K("sel")[0:MH, h * P:(h + 1) * P], row, start=True, stop=True)
                    end(ins, f"{nm}{i}")
            for n in ("o0", "o1", "z0", "z1", "nz0", "nz1"):
                feat(n, hx)
            o = begin("hid")
            pe.wait_ge(S("CR"), 8)
            for y, n in enumerate(("cmp_k_w1", "cmp_v_w1")):
                w = weights(n, P)
                for m in range(16):
                    ins = mm(o[:, y * 32:y * 32 + 2 * NCMP], w[:, m, :], CR[:, y, m, :, :],
                             start=(m == 0), stop=(m == 15))
                if y == 0:
                    ins.then_inc(S("mid"), 1)
                    count["mid"] += 1
                    released[n] = (S("mid"), count["mid"])
            end(ins, "hid", "cmp_v_w1")
            pe.wait_ge(S("sqR"), 1)
            for i in range(3):
                o = begin(f"rs{i}")
                end(mm(o[:, :], b64, sq[:, i * 512:(i + 1) * 512], start=True, stop=True), f"rs{i}")
            pe.wait_ge(S("qkc"), 1)
            for h in range(MH):
                o = begin(f"st{h}")
                mm(o[:, 0:T], qkc[:, MH + h, 0:P], qkc[:, h, :], start=True, stop=True)
                ins = mm(o[:, T:T + P], qkc[:, MH + h, P:T], qkc[:, h, P:T], start=True, stop=True)
                end(ins, f"st{h}")
            ada(0, 0)
            ada(0, 1)
            o = begin("cmp2")
            pe.wait_ge(S("ld_m"), 16 * DMAS["ld_m"])
            done(pe, "hid")
            for g in range(NG):
                mm(o[g * ND:(g + 1) * ND, 0:NCMP], w2k, hk_[:, g * NCMP:(g + 1) * NCMP], start=True, stop=True)
            pe.wait_ge(S("hvp"), 1)
            for g in range(NG):
                ins = mm(o[:, 64 + g * ND:64 + (g + 1) * ND], hvp[:, g * P:(g + 1) * P], w2v, start=True, stop=True)
            end(ins, "cmp2")
            ada(0, 2)
            done(pe, "v1")
            done(pe, "st3")
            for nm in ("nm", "dn"):
                for i in range(2):
                    o = begin(f"{nm}{i}")
                    for j in range(2):
                        h = 2 * i + j
                        l0 = vtok[:, 0, h * P:(h + 1) * P] if nm == "nm" else one
                        l1 = vtok[:, 1, h * P:(h + 1) * P] if nm == "nm" else one
                        mm(o[:, j * T:(j + 1) * T], l0, ST[:, h, 0:T], start=True, stop=True)
                        ins = mm(o[:, j * T + P:(j + 1) * T], l1, ST[:, h, T:T + P], start=False, stop=True,
                                 skip_group_check=True)
                    end(ins, f"{nm}{i}")
            ada(0, 3)
            ada(0, 4)
            pe.wait_ge(S("sqc"), 1)
            o = begin("rsc")
            end(mm(o[:, 0:NCMP], b64, sq[:, 1536:1536 + NCMP], start=True, stop=True), "rsc")
            pe.wait_ge(S("Rn"), 1)
            for i in range(3):
                o = begin(f"pr{i}")
                end(mm(o[:, :], K("prm"), R2[:, i * 512:(i + 1) * 512], start=True, stop=True), f"pr{i}")
            ada(0, 5)
            pe.wait_ge(S("Rnc"), 1)
            o = begin("prc")
            end(mm(o[:, 0:NCMP], K("prm"), R2[:, 1536:1536 + NCMP], start=True, stop=True), "prc")
            ada(0, 6)
            pe.wait_ge(S("sqh"), 1)
            for i in range(2):
                o = begin(f"hr{i}")
                end(mm(o[:, :], one, sq[:, i * 512:(i + 1) * 512], start=True, stop=True), f"hr{i}")
            ada(0, 7)
            pe.wait_ge(S("rope"), 1)
            for hd in range(NH):
                g, b = hd // NR, hd % NR
                gs = slice(g * ND, (g + 1) * ND)
                o = begin(f"s1_{hd}")
                for y in range(2):
                    ins = mm(o[:, y * T:(y + 1) * T], R[gs, b * T + P:b * T + T], R[gs, (4 + y) * T:(5 + y) * T],
                             start=True, stop=True)
                end(ins, f"s1_{hd}")
                if hd % 4 == 3:
                    ada(0, 8 + hd // 4)
            for i in range(4):
                o = begin(f"s0_{i}")
                for j in range(2):
                    hd = 2 * i + j
                    g, b = hd // NR, hd % NR
                    gs = slice(g * ND, (g + 1) * ND)
                    for y in range(2):
                        c = (2 * j + y) * P
                        ins = mm(o[:, c:c + P], R[gs, b * T:b * T + P], R[gs, (4 + y) * T:(4 + y) * T + P],
                                 start=True, stop=True)
                end(ins, f"s0_{i}")
            pe.wait_ge(S("ropec"), 1)
            for g in range(NG):
                o = begin(f"sc{g}")
                gs = slice(g * ND, (g + 1) * ND)
                for a in range(NT):
                    for b in range(NR):
                        c = (a * NR + b) * NCMP
                        ins = mm(o[:, c:c + NCMP], R[gs, b * T + a * P:b * T + (a + 1) * P], R[gs, 1536:1536 + NCMP],
                                 start=True, stop=True)
                end(ins, f"sc{g}")
            for j in range(10, 20):
                ada(0, j)
            pe.wait_ge(S("P0"), 1)
            for i in range(4):
                o = begin(f"t0_{i}")
                for j in range(4):
                    ins = pe.transpose(o[:, j * P:(j + 1) * P], P0[:, 2 * i + j // 2, j % 2, :], idn)
                end(ins, f"t0_{i}")
            pe.wait_ge(S("Pc"), 1)
            o = begin("tc")
            for j in range(4):
                ins = pe.transpose(o[:, j * P:(j + 1) * P],
                                   Pc[:, j // 2, 4 * (j % 2):4 * (j % 2) + 4, :].rearrange("p h n -> p (h n)"), idn)
            end(ins, "tc")
            pe.wait_ge(S("P1"), 1)
            for hd in range(NH):
                o = begin(f"t1_{hd}")
                for j in range(4):
                    ins = pe.transpose(o[:, j * P:(j + 1) * P], P1[:, hd, j // 2, (j % 2) * P:(j % 2 + 1) * P], idn)
                end(ins, f"t1_{hd}")
            for j in range(20, 24):
                ada(0, j)
            done(pe, "kwvw")
            pe.wait_ge(S("VC4"), 1)
            for n in [f"t0_{i}" for i in range(4)] + ["tc"] + [f"t1_{i}" for i in range(NH)]:
                done(pe, n)
            for i in range(2):
                o = begin(f"av{i}")
                for j in range(2):
                    b = 2 * i + j
                    for g in range(NG):
                        hd = g * NR + b
                        gs = slice(g * ND, (g + 1) * ND)
                        for a in range(NT):
                            dst = o[gs, j * T + a * P:j * T + (a + 1) * P]
                            for y in range(2):
                                for s in range(a + 1):
                                    pt = PT0[:, hd, y, :] if a == 0 else PT1[:, hd, 2 * y + s, :]
                                    mm(dst, vsw[:, y, s, gs], pt, start=(y == 0 and s == 0), stop=False)
                            ins = mm(dst, VC4[:, hd % 4, gs], PTc[:, a, g, :], start=False, stop=True)
                end(ins, f"av{i}")
            pe.wait_ge(S("yA"), 1)
            done(pe, "av0")
            done(pe, "av1")
            for j in range(4):
                feat(f"eo{j}", yT)

            sumsq(1)
            for n, f in (("fp", feat), ("qp", feat), ("iv", tok), ("hz", feat)):
                for j in range(4):
                    if n == "fp" and j == 0:
                        f(f"{n}{j}", hx, S("h1"))
                    else:
                        f(f"{n}{j}", hx)
            nada = [0]

            def some_ada(n):
                for _ in range(n):
                    if nada[0] < 24:
                        ada(1, nada[0])
                        nada[0] += 1

            for l in range(LEVELS + 1):
                pe.wait_ge(S("LQ"), l + 1)
                q = LQ[l % 2]
                if l < LEVELS:
                    for i in range(4):
                        o = begin(f"lv{l}_{i}")
                        for j in range(4):
                            c = (4 * i + j) * P
                            ins = mm(o[:, j * P:(j + 1) * P], q[:, c:c + P], q[:, c:c + P], start=True, stop=True)
                        end(ins, f"lv{l}_{i}")
                else:
                    for i in range(2):
                        o = begin(f"lv{l}_{i}")
                        for j in range(4):
                            c = (4 * i + j) * T
                            ins = mm(o[:, j * P:(j + 1) * P], q[:, c:c + P], q[:, c + P:c + T], start=True, stop=True)
                        end(ins, f"lv{l}_{i}")
                some_ada(3)
            for i in range(4):
                o = begin(f"dg_{i}")
                for j in range(4):
                    c = (4 * i + j) * P
                    ins = mm(o[:, j * P:(j + 1) * P], hk[:, c:c + P], hq[:, c:c + P], start=True, stop=True)
                end(ins, f"dg_{i}")
            some_ada(24)
            done(pe, "iv3")
            done(pe, "lv7_0")
            done(pe, "lv7_1")
            done(pe, "dg_3")
            for i in range(4):
                o = begin(f"ho{i}")
                for j in range(2):
                    h = 2 * i + j
                    v0, v1 = ht[:, 0, h * P:(h + 1) * P], ht[:, 1, h * P:(h + 1) * P]
                    mm(o[:, j * T:j * T + P], v0, ATm[:, 2 * h, :], start=True, stop=True)
                    mm(o[:, j * T + P:(j + 1) * T], v0, AT2[:, h, :], start=True, stop=False)
                    ins = mm(o[:, j * T + P:(j + 1) * T], v1, ATm[:, 2 * h + 1, :], start=False, stop=True)
                end(ins, f"ho{i}")
            for i in range(4):
                pe.wait_ge(S("sqo"), i + 1)
                o = begin(f"or{i}")
                end(mm(o[:, :], one, sq[:, i * 512:(i + 1) * 512], start=True, stop=True), f"or{i}")
            pe.wait_ge(S("yH"), 4)
            for j in range(4):
                feat(f"oo{j}", yT)

            sumsq(2)
            w = weights("pool")
            for g in range(4):
                o = begin(f"pw{g}")
                pe.wait_ge(S("pl"), g + 1)
                for j in range(2):
                    for k in range(2):
                        ins = mm(o[:, j * T:(j + 1) * T], w[:, 2 * g + k, j * P:(j + 1) * P], pl[:, 2 * g + k, :],
                                 start=(k == 0), stop=(k == 1))
                end(ins, f"pw{g}", "pool")

            def mlp(l):
                n = 3 + 2 * l
                sumsq(n)
                for j in range(FF // CW):
                    feat(f"w1_{l}_{j}", hx, S(f"h{n}") if j == 0 else None)
                for j in range(4):
                    o = begin(f"w2_{l}_{j}")
                    for q in range(4):
                        nm = f"w2_{l}_{j}_{q}"
                        w = weights(nm)
                        for k in range(KT):
                            if j == 0 and k % 2 == 0:
                                pe.wait_ge(S("sqr"), 16 * l + 4 * q + k // 2 + 1)
                            for i in range(2):
                                ins = mm(o[:, i * T:(i + 1) * T], w[:, k, i * P:(i + 1) * P], h1[:, q * KT + k, :],
                                         start=(q == 0 and k == 0 and i == 0), stop=(q == 3 and k == KT - 1),
                                         skip_group_check=True)
                        if q < 3:
                            ins.then_inc(S("mid"), 1)
                            count["mid"] += 1
                            released[nm] = (S("mid"), count["mid"])
                    end(ins, f"w2_{l}_{j}", nm)

            mlp(0)
            pe.wait_ge(S("ld_s"), 16 * DMAS["ld_s"])
            for i in range(2):
                o = begin(f"ws{i}")
                for j in range(4):
                    ins = pe.transpose(o[:, j * P:(j + 1) * P], wst[:, 4 * i + j, :], idn)
                end(ins, f"ws{i}")
            sumsq(4)
            for j in range(4):
                feat(f"si{j}", hx, S("h4") if j == 0 else None)
            for j in range(4, 8):
                tok(f"si{j}", hx)
            done(pe, "ws1")
            pe.wait_ge(S("vln"), NT)
            for i in range(4):
                o = begin(f"mx{i}")
                for j in range(2):
                    h = 2 * i + j
                    for a in range(NT):
                        ins = mm(o[:, (2 * j + a) * P:(2 * j + a + 1) * P], vt[:, a, h * P:(h + 1) * P], wsT[:, h, :],
                                 start=True, stop=True)
                end(ins, f"mx{i}")
            pe.wait_ge(S("yS"), 4)
            for j in range(4):
                feat(f"so{j}", yT)
            mlp(1)
            sumsq(6)
            pe.wait_ge(S("h6"), 8)
            for i in range(4):
                o = begin(f"f{i}")
                for k in range(4):
                    f = 4 * (i % 2) + k
                    ins = pe.transpose(o[:, k * P:(k + 1) * P], hx[:, f, (i // 2) * P:(i // 2 + 1) * P], idn)
                end(ins, f"f{i}")
            assert count["chunk"] == len(chunks)

        def row_loads():
            A_, B_, C_ = rows
            ev = A["ev_b_in"][0]

            def r128(v):
                return v.rearrange("(r f) -> r f", f=P)

            def pair(v):
                return v.rearrange("(g b d) -> g b d", g=NG, d=ND)

            a = [(A_[0:16, :], A["norm_w"].rearrange("l (r f) -> (l r) f", f=P)),
                 (A_[16:36, :], r128(ev[0:C_GATE])),
                 (A_[40:46, :], r128(ev[C_KV:C_GT])),
                 (A_[50:58, :], r128(A["mlstm_conv_b"][0])),
                 (A_[58:62, :], r128(A["mlstm_head_norm"][0])),
                 (A_[66:82, :], A["cmp_k_pos"][0].rearrange("(m l) d -> m (l d)", l=2)),
                 (A_[82:98, :], A["cmp_v_pos"][0].rearrange("(m l) d -> m (l d)", l=2))]
            for g in range(NG):
                gs = slice(g * ND, (g + 1) * ND)
                a.append((A_[36:40, gs], pair(ev[C_NQ:C_KV])[g]))
                a.append((A_[46:50, gs], pair(ev[C_NZ:C_NZ + NW_])[g]))
                a.append((A_[62:63, gs], A["nsa_q_norm"][0:1, :]))
                a.append((A_[63:66, gs], A["nsa_k_norm"][0]))
            b = [(B_[0:32, :], A["mlstm_conv_w"][0].rearrange("t (r f) -> (t r) f", f=P)),
                 (B_[32:64, :], r128(A["od_b_in"][0])),
                 (B_[64:80, :], A["hgrn_lb_logits"].rearrange("l (r f) -> (l r) f", f=P)),
                 (B_[80:88, :], r128(A["hgrn_head_norm"][0])),
                 (B_[88:96, :], r128(A["final_g_2"][0])),
                 (B_[96:104, :], r128(A["c_2"][0])),
                 (B_[104:112, :], r128(A["pool_scale_2"][0]))]
            c = [(C_[0:96, :], A["ada_b_2"].rearrange("l (r f) -> (l r) f", f=P)),
                 (C_[96:112, :], A["norm_mix_g_2"].rearrange("l (r f) -> (l r) f", f=P)),
                 (C_[112:128, :], A["norm_mlp_g_2"].rearrange("l (r f) -> (l r) f", f=P))]
            return dict(ld_A=a, ld_B=b, ld_C=c)

        BV, BVS, BVW, BG, BF, BI = 0, 512, 640, 768, 800, 804
        loads = row_loads()
        ev = A["ev_b_in"]
        loads["ld_b"] = [(bcb[:, BV:BV + 512], ev[0:1, 2 * MW:3 * MW].broadcast_to([P, 512])),
                         (bcb[:, BVS:BVS + P], ev[0:1, C_KV + 3 * P:C_KV + 4 * P].broadcast_to([P, P])),
                         (bcb[:, BVW:BVW + P], ev[0:1, C_KV + 5 * P:C_KV + 6 * P].broadcast_to([P, P])),
                         (bcb[:, BG:BG + 8], ev[0:1, C_GATE:C_NQ].broadcast_to([P, 8])),
                         (bcb[:, BG + 8:BG + 32], ev[0:1, C_GT:C_NZ].broadcast_to([P, 24])),
                         (bcb[:, BF:BF + MH], A["mlstm_f_bias"].broadcast_to([P, MH])),
                         (bcb[:, BI:BI + D], A["od_b_in"][0:1, D:2 * D].broadcast_to([P, D]))]
        loads["ld_m"] = [(w2k, A["cmp_k_w2"][0]), (w2v, A["cmp_v_w2"][0])]
        loads["ld_s"] = [(wst, A["sgu_w_s_2"][0].rearrange("h t s -> t h s")),
                         (lng, A["sgu_ln_g_2"].broadcast_to([P, D])),
                         (lnb, A["sgu_ln_b_2"].broadcast_to([P, D])),
                         (bsb.rearrange("p h t -> p (h t)"),
                          A["sgu_b_s_2"].rearrange("l h t -> l (h t)").broadcast_to([P, 8 * P]))]
        assert all(DMAS[k] == len(v) for k, v in loads.items()), {k: len(v) for k, v in loads.items()}

        @block.sync
        def _(sp):
            sp.dma_start(xtok[:, 0, :], A["x"][0, 0:P, :]).then_inc(S("ld_x"), 16)
            sp.dma_start(xtok[:, 1, :], A["x"][0, P:T, :]).then_inc(S("ld_x"), 16)
            for dst, src in loads["ld_A"]:
                sp.dma_start(dst, src).then_inc(S("ld_A"), 16)
            for i, (name, parts) in enumerate(chunks):
                if i >= NSLOT:
                    sp.wait_ge(*released[chunks[i - NSLOT][0]])
                slot = i % NSLOT
                full = wring[:, slot, :]
                w = full.rearrange("p (k n) -> p k n", n=P if name.startswith("cmp") else CW)
                for dst, src in parts:
                    if len(dst) == 3:
                        g = dst[2]
                        d = w[g * ND:(g + 1) * ND, dst[0], dst[1]]
                    else:
                        d = w[:, dst[0], dst[1]]
                    sp.dma_start(d, src).then_inc(S(f"w{slot}"), 16)
            for i in range(4):
                done(sp, f"f{i}")
            for a in range(NT):
                sp.dma_start(out_dram[0, a * P:(a + 1) * P, :], ot[:, a, :]).then_inc(S("st"), 16)
            sp.wait_ge(S("st"), 16 * NT)

        @block.gpsimd
        def _(g):
            def full(name):
                b, n = place[name]
                g.wait_ge(S(f"full{b}"), n)

            g.dma_start(cst[:, :], cst_dram).then_inc(S("ld_cst"), 16)
            for nm in ("ld_B", "ld_C", "ld_b", "ld_m"):
                for dst, src in loads[nm]:
                    g.dma_start(dst, src).then_inc(S(nm), 16)
            g.memset(hT[:, :, 0:PADW], 0.0).then_inc(S("zero"), 1)
            g.memset(hvp, 0.0).then_inc(S("zero"), 1)
            full("par2")
            g.memset(qkp[:, :, 0:3], 0.0).then_inc(S("zero"), 1)
            g.wait_ge(S("ET"), 1)
            g.wait_ge(S("ld_cst"), 16)
            tri = K("tri").unsqueeze(1).broadcast_to([P, MH, P])
            g.tensor_tensor(ET[:, :, 0:P], ET[:, :, 0:P], tri, ALU.mult).then_inc(S("ETm"), 1)
            g.tensor_tensor(ET[:, :, T:T + P], ET[:, :, T:T + P], tri, ALU.mult).then_inc(S("ETm"), 1)
            done(g, "o1")
            done(g, "z1")
            g.tensor_tensor(og, og, zg, ALU.mult).then_inc(S("oz"), 1)
            done(g, "eo3")
            g.memset(rst, 1.0).then_inc(S("rst"), 1)
            g.wait_ge(S("rst"), 1)
            g.memset(rst.rearrange("p (n t) -> p n t", t=P)[:, :, 0:1], 0.0).then_inc(S("rst"), 1)
            g.memset(ATm, 0.0).then_inc(S("AT0"), 1)
            for l in range(LEVELS + 1):
                g.wait_ge(S("LX"), l + 1)
                if l == 0:
                    g.wait_ge(S("hf"), 1)
                    done(g, "qp3")
                m = P >> (l + 1) if l < LEVELS else P
                v = LE[l % 2].rearrange("p (n y t) -> p n y t", y=2, t=m)
                qq = LQ[l % 2].rearrange("p (n y t) -> p n y t", y=2, t=m)
                if l >= 2:
                    full(f"lv{l - 2}_3")
                for y, src in ((0, hk), (1, hq)):
                    s = src.rearrange("p (n y t) -> p n y t", y=2, t=m)
                    ins = g.tensor_tensor(qq[:, :, y, :], v[:, :, y, :], s[:, :, y, :], ALU.mult)
                ins.then_inc(S("LQ"), 1)
            done(g, "oo3")
            for dst, src in loads["ld_s"]:
                g.dma_start(dst, src).then_inc(S("ld_s"), 16)
            for l in range(2):
                for j in range(FF // CW):
                    done(g, f"w1_{l}_{j}")
                    r = rl[j % 2]
                    g.tensor_tensor(h1[:, 2 * j:2 * j + 2, :].rearrange("p f t -> p (f t)"), r, r,
                                    ALU.mult).then_inc(S("sqr"), 1)

        @block.scalar
        def _(act):
            chain = [0]

            def A_(out, in_, f=ACT.Identity, **kw):
                return act.activation(out, in_, f, **kw)

            def pc(c):
                return par[:, c:c + 1]

            def norm(n, prev):
                for i in range(4):
                    if n:
                        done(act, f"{prev}{i}")
                    A_(sq[:, i * 512:(i + 1) * 512], xT[:, 2 * i:2 * i + 2, :].rearrange("p b t -> p (b t)"),
                       ACT.Square).then_inc(S("sq"), 1)
                done(act, f"ss{n}")
                A_(rstd, var, ACT.Sqrt).then_inc(S("std"), 1)

            def shift(n, l, col):
                for k in range(KT):
                    act.wait_ge(S(f"hs{n}"), k + 1)
                    A_(hx[:, k, :], hx[:, k, :], bias=mod[:, l, col + k:col + k + 1]).then_inc(S(f"h{n}"), 1)

            def both(name, dst, f, cols):
                o = got(act, name)
                for j in range(2):
                    ins = A_(dst(j), o[:, j * T:(j + 1) * T], f, bias=cols(j))
                free(ins, name)

            def whole(name, dst, f=ACT.Identity, n=512):
                free(A_(dst, got(act, name)[:, 0:n], f), name)

            for i in (0, 2):
                o = got(act, f"x{i}")
                free(A_(xT[:, 4 * (i % 2):4 * (i % 2) + 4, (i // 2) * P:(i // 2 + 1) * P],
                        o[:, :].rearrange("p (b t) -> p b t", t=P)), f"x{i}")
            for i in range(4):
                done(act, f"x{i}")
            norm(0, None)
            done(act, "par1")
            A_(cs, par[:, PB["c"]:PB["c"] + KT], ACT.Silu).then_inc(S("cs"), 1)
            act.wait_ge(S("lbx"), 1)
            A_(lb, lb, ACT.Exp)
            A_(oml, oml, ACT.Exp).then_inc(S("lbe"), 1)
            done(act, "par0")
            for i, n in enumerate(("q0", "q1", "k0", "k1")):
                both(n, lambda j: qkp[:, 2 * i + j, 3:3 + T], ACT.Identity, lambda j: pc(PA["b20"] + 2 * i + j))
            act.wait_ge(S("gt"), 1)
            A_(gt[:, :, 8:NGATE], gt[:, :, 8:NGATE], ACT.Sigmoid).then_inc(S("gsig"), 1)
            act.wait_ge(S("absf"), 1)
            A_(erow, trow, ACT.Exp, scale=-1.0).then_inc(S("a"), 1)
            act.wait_ge(S("a"), 1)
            A_(erow, erow, ACT.Ln, bias=1.0).then_inc(S("lnf"), 1)
            for i in range(2):
                both(f"nq{i}", lambda j: R[:, (2 * i + j) * T:(2 * i + j + 1) * T], ACT.Identity,
                     lambda j: pc(PA["bnq"] + 2 * i + j))
            act.wait_ge(S("bg"), 1)
            A_(erow, trow, ACT.Exp, scale=-1.0).then_inc(S("erow"), 1)
            done(act, "nq1")
            done(act, "ksvs")
            done(act, "kwvw")
            A_(sq[:, 0:1536], R[:, 0:1536], ACT.Square).then_inc(S("sqR"), 1)
            done(act, "gb1")
            e2 = ET.rearrange("p h n -> p (h n)")
            A_(e2, e2, ACT.Exp, scale=-1.0).then_inc(S("ET"), 1)
            for i in range(2):
                whole(f"em{i}", emrb[:, i * 512:(i + 1) * 512])
            for nm, t, f, c in (("o", og, ACT.Sigmoid, PA["b20"] + 12), ("z", zg, ACT.Silu, PA["b20"] + 16),
                                ("nz", nz, ACT.Silu, PA["bnz"])):
                for i in range(2):
                    both(f"{nm}{i}", lambda j: t[:, (2 * i + j) * T:(2 * i + j + 1) * T], f,
                         lambda j: pc(c + 2 * i + j))
            act.wait_ge(S("conv"), 1)
            c2 = qkc.rearrange("p b t -> p (b t)")
            A_(c2, c2, ACT.Silu).then_inc(S("qkc"), 1)
            o = got(act, "hid")
            A_(hk_[:, 0:2 * NCMP], o[:, 0:2 * NCMP], ACT.Gelu_apprx_tanh)
            free(A_(hv_[:, 0:2 * NCMP], o[:, 32:32 + 2 * NCMP], ACT.Gelu_apprx_tanh), "hid")
            done(act, "rs2")
            A_(R2[:, 0:1536], R2[:, 0:1536], ACT.Sqrt).then_inc(S("sR"), 1)
            done(act, "st3")
            for i in range(2):
                whole(f"dn{i}", e2[:, i * 512:(i + 1) * 512], ACT.Abs)
            done(act, "nm1")
            A_(sq[:, 0:1024], hm, ACT.Square).then_inc(S("sqh"), 1)
            done(act, "rsc")
            A_(R2[:, 1536:1536 + NCMP], R2[:, 1536:1536 + NCMP], ACT.Sqrt).then_inc(S("sRc"), 1)
            done(act, "hr1")
            A_(e2[:, 0:1024], e2[:, 0:1024], ACT.Sqrt).then_inc(S("sh"), 1)
            for i, v in enumerate((P0, Pc, P1)):
                act.wait_ge(S("smax"), i + 1)
                v = v[:, :, :, 0:NCMP] if i == 1 else v
                A_(v, v, ACT.Exp).then_inc(S("sexp"), 1)
            for i in range(4):
                whole(f"t0_{i}", PT0[:, 2 * i:2 * i + 2, :, :].rearrange("p h y k -> p (h y k)"))
            whole("tc", PTc.rearrange("p a g k -> p (a g k)"))
            for h in range(0, NH, 2):
                whole(f"t1_{h}", PT1[:, h, :, :].rearrange("p y k -> p (y k)"))
            norm(1, "eo")
            act.wait_ge(S("ndb"), 1)
            for i in range(4):
                o = got(act, f"fp{i}")
                for j in range(2):
                    b = 2 * i + j
                    A_(hb[:, b * T:(b + 1) * T], o[:, j * T:(j + 1) * T], ACT.Sigmoid, bias=pc(PB["odb"] + b))
                    ins = A_(hk[:, b * T:(b + 1) * T], o[:, j * T:(j + 1) * T], ACT.Sigmoid, bias=nodb[:, b:b + 1],
                             scale=-1.0)
                free(ins, f"fp{i}")
            for i in range(4):
                both(f"qp{i}", lambda j: hq[:, (2 * i + j) * T:(2 * i + j + 1) * T], ACT.Silu,
                     lambda j: pc(PB["odb"] + 16 + 2 * i + j))
            act.wait_ge(S("hf"), 1)
            A_(hb2, hb, ACT.Ln).then_inc(S("hln"), 1)
            for i in range(4):
                both(f"hz{i}", lambda j: hz[:, (2 * i + j) * T:(2 * i + j + 1) * T], ACT.Silu,
                     lambda j: pc(PB["odb"] + 24 + 2 * i + j))
            for l in range(LEVELS + 1):
                act.wait_ge(S("LE"), l + 1)
                A_(LE[l % 2], LE[l % 2], ACT.Exp).then_inc(S("LX"), 1)
            for i in range(2):
                whole(f"lv7_{i}", AT2[:, 4 * i:4 * i + 4, :].rearrange("p h j -> p (h j)"))
            for i in range(4):
                whole(f"ho{i}", hO[:, i * 512:(i + 1) * 512])
                done(act, f"ho{i}")
                A_(sq[:, i * 512:(i + 1) * 512], hO[:, i * 512:(i + 1) * 512], ACT.Square).then_inc(S("sqo"), 1)
            done(act, "or3")
            A_(LE[0], LE[0], ACT.Sqrt).then_inc(S("so"), 1)
            norm(2, "oo")
            shift(2, 0, 0)

            def mlp(l, prev):
                n = 3 + 2 * l
                norm(n, prev)
                shift(n, l, 24)
                for j in range(FF // CW):
                    i = 16 * l + j
                    if i >= 2:
                        act.wait_ge(S("sqr"), i - 1)
                    whole(f"w1_{l}_{j}", rl[j % 2], ACT.Relu)

            mlp(0, "pw")
            norm(4, "w2_0_")
            shift(4, 1, 0)
            for j in range(4):
                whole(f"si{j}", uT[:, 2 * j:2 * j + 2, :].rearrange("p b t -> p (b t)"), ACT.Gelu)
            for j in range(4):
                o = got(act, f"si{4 + j}")
                free(A_(vt[:, :, j * CW:(j + 1) * CW], o[:, :].rearrange("p (a n) -> p a n", a=NT), ACT.Gelu),
                     f"si{4 + j}")
            for a in range(NT):
                act.wait_ge(S("xc"), a + 1)
                A_(sq[:, a * D:(a + 1) * D], xc[:, a, :], ACT.Square, accum_out=vr[:, a:a + 1]).then_inc(S("vr"), 1)
            act.wait_ge(S("vre"), 1)
            A_(vr, vr, ACT.Sqrt).then_inc(S("vs"), 1)
            mlp(1, "so")
            norm(6, "w2_1_")
            for i in (0, 2):
                whole(f"f{i}", ot[:, i // 2, (i % 2) * 512:(i % 2 + 1) * 512])

        @block.vector
        def _(dve):
            chain = [0]

            def V(ins):
                chain[0] += 1
                ins.then_inc(S("v"), 1)
                dve.wait_ge(S("v"), chain[0])

            def pc(c):
                return par[:, c:c + 1]

            ts, tt, stt = dve.tensor_scalar, dve.tensor_tensor, dve.scalar_tensor_tensor
            MUL, ADD, SUB, MAX = ALU.mult, ALU.add, ALU.subtract, ALU.max

            def norm(n, gain, sem):
                o = got(dve, f"ss{n}")
                free(ts(var, o[:, 0:T], 1.0 / D, EPS, MUL, ADD), f"ss{n}")
                dve.wait_ge(S("std"), n + 1)
                V(dve.reciprocal(rstd, rstd))
                for k in range(KT):
                    stt(hx[:, k, :], xT[:, k, :], gain(k), rstd, MUL, MUL).then_inc(S(sem), 1)

            def residual(name, gain=None):
                for i in range(4):
                    o = got(dve, f"{name}{i}")
                    if gain is None:
                        x = xT[:, 2 * i:2 * i + 2, :].rearrange("p b t -> p (b t)")
                        ins = tt(x, o[:, :], x, ADD)
                    else:
                        for j in range(2):
                            b = 2 * i + j
                            ins = stt(xT[:, b, :], o[:, j * T:(j + 1) * T], gain(b), xT[:, b, :], MUL, ADD)
                    free(ins, f"{name}{i}")

            for i in (1, 3):
                o = got(dve, f"x{i}")
                free(dve.tensor_copy(xT[:, 4 * (i % 2):4 * (i % 2) + 4, (i // 2) * P:(i // 2 + 1) * P],
                                     o[:, :].rearrange("p (b t) -> p b t", t=P)), f"x{i}")
            for i, n in enumerate((NA_ROWS, NB_ROWS, NC_ROWS)):
                free(dve.tensor_copy(par[:, i * P:i * P + n], got(dve, f"par{i}")[:, 0:n]), f"par{i}")
            for i in range(4):
                done(dve, f"x{i}")
            for i in range(3):
                done(dve, f"par{i}")
            norm(0, lambda k: pc(PA["nw"] + k), "h0")
            V(ts(pc(PA["qn"]), pc(PA["qn"]), ND ** -0.5, None, MUL))
            l0, l1 = par[:, PB["lbl"]:PB["lbl"] + HH], par[:, PB["lbl"] + HH:PB["lbl"] + 2 * HH]
            V(tt(lbt, l0, l1, MAX))
            tt(lb, l0, lbt, SUB)
            tt(oml, l1, lbt, SUB).then_inc(S("lbx"), 1)
            ts(nodb, par[:, PB["odb"]:PB["odb"] + HH], -1.0, None, MUL).then_inc(S("ndb"), 1)
            dve.wait_ge(S("ld_b"), 16 * DMAS["ld_b"])
            o = got(dve, "gt")
            free(tt(gt, o[:, 0:NT * NGATE].rearrange("p (a n) -> p a n", a=NT),
                    bcb[:, BG:BG + NGATE].unsqueeze(1).broadcast_to([P, NT, NGATE]), ADD), "gt")
            done(dve, "gt")
            tt(gt[:, :, MH:2 * MH], gt[:, :, MH:2 * MH],
               bcb[:, BF:BF + MH].unsqueeze(1).broadcast_to([P, NT, MH]), ADD).then_inc(S("gt"), 1)
            dve.wait_ge(S("lbe"), 1)
            V(tt(lbt, lb, oml, ADD))
            V(dve.reciprocal(lbt, lbt))
            V(tt(lb, lb, lbt, MUL))
            V(ts(oml, lb, -1.0, 1.0, MUL, ADD))

            def tokens(name, dst, c0, b0, n, last=True):
                o = got(dve, name)
                ins = tt(dst, o[:, c0:c0 + NT * n].rearrange("p (a n) -> p a n", a=NT),
                         bcb[:, b0:b0 + n].unsqueeze(1).broadcast_to([P, NT, n]), ADD)
                free(ins, name)

            for j in range(2):
                tokens(f"v{j}", vtok[:, :, j * CW:(j + 1) * CW], 0, BV + j * CW, CW)
            free(dve.tensor_copy(rw[0:MH, 0:2 * T], got(dve, "gtT")[0:MH, :]), "gtT")
            done(dve, "gtT")
            stt(trow, frow, -1.0, frow, MUL, MAX).then_inc(S("absf"), 1)
            V(ts(frow, frow, 0.0, None, ALU.min))
            V(dve.memset(orow, 1.0))
            dve.wait_ge(S("lnf"), 1)
            V(tt(trow, frow, erow, SUB))
            V(dve.tensor_tensor_scan(brow, orow, trow, 0.0, MUL, ADD))
            tt(arow, irow, brow, SUB).then_inc(S("arow"), 1)
            dve.wait_ge(S("arow"), 1)
            dve.tensor_tensor_scan(grow, orow, arow, 0.0, MUL, MAX).then_inc(S("grow"), 1)
            dve.wait_ge(S("grow"), 1)
            tt(trow, brow, grow, ADD).then_inc(S("bg"), 1)
            o = got(dve, "kcvc")
            for y in range(2):
                ins = ts(kcvc[:, y, :], o[:, y * T:(y + 1) * T], pc(PA["bkv"] + y), None, ADD)
            free(ins, "kcvc")
            done(dve, "kcvc")
            for y, X in enumerate((XK, XV)):
                for g in range(NG):
                    src = kcvc[g * ND:(g + 1) * ND, y, :]
                    dve.tensor_copy(X[0:ND, g, :], src)
                    ins = dve.tensor_copy(X[ND:P, g, 0:T - 1], src[:, 1:T])
            V(ins)
            for y, (X, pos) in enumerate(((XK, PA["kpos"]), (XV, PA["vpos"]))):
                for g in range(NG):
                    xv = X[:, g, :].rearrange("p (n s) -> p s n", s=CMP_STRIDE)
                    for u in range(2):
                        tt(CR[:, y, 8 * u:8 * u + 8, g, :], xv[:, 0:CMP_STRIDE:2, u:u + NCMP],
                           par[:, pos + 8 * u:pos + 8 * u + 8].unsqueeze(2).broadcast_to([P, 8, NCMP]),
                           ADD).then_inc(S("CR"), 1)
            for y, n in enumerate(("ksvs", "kwvw")):
                o = got(dve, n)
                ts(R[:, (4 + y) * T:(5 + y) * T], o[:, 0:T], pc(PA["bkv"] + 2 + 2 * y), None, ADD)
                tokens(n, vsw[:, y, :, :], T, BVS + y * P, P)
            free(dve.tensor_copy(acol, got(dve, "aT")[:, 0:NT * MH].rearrange("p (a h) -> p a h", a=NT)), "aT")
            done(dve, "aT")
            for i in range(2):
                o = got(dve, f"gb{i}")
                for j in range(2):
                    h = 2 * i + j
                    ts(ET[:, h, 0:T], o[:, j * T:(j + 1) * T], acol[:, 0, h:h + 1], 0.0, SUB, MAX)
                    ins = ts(ET[:, h, T:T + P], o[:, j * T + P:(j + 1) * T], acol[:, 1, h:h + 1], 0.0, SUB, MAX)
                free(ins, f"gb{i}")
            done(dve, "k1")
            dve.wait_ge(S("zero"), 3)
            for tap in range(TAPS):
                for b in range(8):
                    w = pc(PB["cvw"] + tap * 8 + b)
                    if tap == 0:
                        ins = ts(qkc[:, b, :], qkp[:, b, 0:T], w, pc(PA["cvb"] + b), MUL, ADD)
                    else:
                        ins = stt(qkc[:, b, :], qkp[:, b, tap:tap + T], w, qkc[:, b, :], MUL, ADD)
                if tap < TAPS - 1:
                    V(ins)
                else:
                    ins.then_inc(S("conv"), 1)
            done(dve, "hid")
            hv4 = hvp.rearrange("p (g i n) -> p g i n", g=NG, i=4)
            for g in range(NG):
                ins = dve.tensor_copy(hv4[:, g, :, 0:NCMP],
                                      hv_[:, g * NCMP:(g + 1) * NCMP].unsqueeze(1).broadcast_to([P, 4, NCMP]))
            ins.then_inc(S("hvp"), 1)
            for i in range(3):
                free(ts(R2[:, i * 512:(i + 1) * 512], got(dve, f"rs{i}")[:, :], 1.0 / ND, EPS, MUL, ADD), f"rs{i}")
            dve.wait_ge(S("ETm"), 2)
            for h in range(MH):
                free(stt(ST[:, h, :], got(dve, f"st{h}")[:, 0:T + P], float(P) ** -0.5, ET[:, h, :], MUL, MUL),
                     f"st{h}")
            dve.wait_ge(S("sR"), 1)
            V(dve.reciprocal(R2[:, 0:1536], R2[:, 0:1536]))
            done(dve, "nq1")
            for lo, hi, c in ((0, 1024, PA["qn"]), (1024, 1280, PA["kn"] + 1), (1280, 1536, PA["kn"] + 2)):
                ins = stt(R2[:, lo:hi], R[:, lo:hi], pc(c), R2[:, lo:hi], MUL, MUL)
            ins.then_inc(S("Rn"), 1)
            kc = slice(1536, 1536 + NCMP)
            o = got(dve, "cmp2")
            dve.tensor_copy(R[:, kc], o[:, 0:NCMP])
            free(dve.tensor_copy(VC, o[:, 64:64 + P]), "cmp2")
            done(dve, "cmp2")
            tt(sq[:, kc], R[:, kc], R[:, kc], MUL).then_inc(S("sqc"), 1)
            for i in range(4):
                ins = ts(VC4[:, i, :], VC, K("rg")[:, i:i + 1], None, MUL)
            ins.then_inc(S("VC4"), 1)
            den = ET.rearrange("p h n -> p (h n)")[:, 0:1024]
            done(dve, "dn1")
            done(dve, "em1")
            V(tt(den, den, emrb, MAX))
            V(dve.reciprocal(den, den))
            for i in range(2):
                free(tt(hm[:, i * 512:(i + 1) * 512], got(dve, f"nm{i}")[:, :], den[:, i * 512:(i + 1) * 512], MUL),
                     f"nm{i}")
            free(ts(R2[:, kc], got(dve, "rsc")[:, 0:NCMP], 1.0 / ND, EPS, MUL, ADD), "rsc")
            dve.wait_ge(S("sRc"), 1)
            V(dve.reciprocal(R2[:, kc], R2[:, kc]))
            stt(R2[:, kc], R[:, kc], pc(PA["kn"]), R2[:, kc], MUL, MUL).then_inc(S("Rnc"), 1)
            for i in range(3):
                free(tt(R[:, i * 512:(i + 1) * 512].rearrange("p (b t) -> p b t", t=T),
                        got(dve, f"pr{i}")[:, :].rearrange("p (b t) -> p b t", t=T),
                        K("sin").unsqueeze(1).broadcast_to([P, 2, T]), MUL), f"pr{i}")
            r6 = R2[:, 0:1536].rearrange("p (b t) -> p b t", t=T)
            V(tt(r6, r6, K("cos").unsqueeze(1).broadcast_to([P, 6, T]), MUL))
            done(dve, "pr2")
            tt(R[:, 0:1536], R[:, 0:1536], R2[:, 0:1536], ADD).then_inc(S("rope"), 1)
            ends = slice(CMP_LEN - 1, T, CMP_STRIDE)
            free(tt(R[:, kc], got(dve, "prc")[:, 0:NCMP], K("sin")[:, ends], MUL), "prc")
            V(tt(R2[:, kc], R2[:, kc], K("cos")[:, ends], MUL))
            done(dve, "prc")
            tt(R[:, kc], R[:, kc], R2[:, kc], ADD).then_inc(S("ropec"), 1)
            for i in range(2):
                free(ts(den[:, i * 512:(i + 1) * 512], got(dve, f"hr{i}")[:, :], 1.0 / P, EPS, MUL, ADD), f"hr{i}")
            dve.wait_ge(S("sh"), 1)
            V(dve.reciprocal(den, den))
            for h in range(MH):
                s = slice(h * T, (h + 1) * T)
                ins = stt(hm[:, s], hm[:, s], pc(PA["mhn"] + h), den[:, s], MUL, MUL)
            V(ins)
            dve.wait_ge(S("oz"), 1)
            tt(yT[:, 0:MH, :].rearrange("p b t -> p (b t)"), hm, og, MUL).then_inc(S("yA"), 1)
            dve.wait_ge(S("yA"), 1)
            m1 = K("m1")
            for h in range(NH):
                free(tt(P1[:, h, :, :], got(dve, f"s1_{h}")[:, :].rearrange("p (y k) -> p y k", y=2),
                        m1.unsqueeze(1).broadcast_to([P, 2, T]), ADD), f"s1_{h}")
            for i in range(4):
                free(tt(P0[:, 2 * i:2 * i + 2, :, :].rearrange("p h y k -> p (h y) k"),
                        got(dve, f"s0_{i}")[:, :].rearrange("p (n k) -> p n k", k=P),
                        m1[:, P:T].unsqueeze(1).broadcast_to([P, 4, P]), ADD), f"s0_{i}")
            V(dve.memset(Pc, 0.0))
            mc = K("mc").rearrange("p (a n) -> p a n", a=NT).unsqueeze(2).broadcast_to([P, NT, NH, NCMP])
            mc01 = K("mc01").rearrange("p (a n) -> p a n", a=NT).unsqueeze(2).broadcast_to([P, NT, NH, NCMP])
            pcv = Pc[:, :, :, 0:NCMP]
            for g in range(NG):
                hs = slice(g * NR, (g + 1) * NR)
                o = got(dve, f"sc{g}")
                free(tt(pcv[:, :, hs, :], o[:, 0:NT * NR * NCMP].rearrange("p (a h n) -> p a h n", a=NT, h=NR),
                        mc[:, :, hs, :], ADD), f"sc{g}")
            done(dve, "s0_3")
            done(dve, "sc1")
            sets = []
            for v, mx, su, gate, w in ((P0, mx0, sm0, gt[:, 0, 8:NGATE], P), (pcv, mxc, smc, None, NCMP),
                                       (P1, mx1, sm1, gt[:, 1, 8:NGATE], T)):
                a, b = (NT, NH) if w == NCMP else (NH, 2)
                m4 = mx.rearrange("p (a b) -> p a b", a=a)
                s4_ = su.rearrange("p (a b) -> p a b", a=a)
                if w == NCMP:
                    gv = gt[:, :, 8:NGATE].rearrange("p a (h c) -> p a h c", c=3)[:, :, :, 0]
                else:
                    gv = gate.rearrange("p (h c) -> p h c", c=3)[:, :, 1:3]
                sets.append((v, m4, s4_, gv, [P, a, b, w]))
            for v, m4, s4_, gv, sh in sets:
                V(dve.tensor_reduce(m4, v, AX, MAX))
                tt(v, v, m4.unsqueeze(3).broadcast_to(sh), SUB).then_inc(S("smax"), 1)
            dve.wait_ge(S("gsig"), 1)
            for i, (v, m4, s4_, gv, sh) in enumerate(sets):
                dve.wait_ge(S("sexp"), i + 1)
                V(dve.tensor_reduce(s4_, v, AX, ADD))
                V(dve.reciprocal(s4_, s4_))
                V(tt(s4_, s4_, gv, MUL))
                if i == 1:
                    V(tt(v, v, mc01, MUL))
                tt(v, v, s4_.unsqueeze(3).broadcast_to(sh), MUL).then_inc(S(("P0", "Pc", "P1")[i]), 1)
            for h in range(1, NH, 2):
                free(dve.tensor_copy(PT1[:, h, :, :].rearrange("p y k -> p (y k)"), got(dve, f"t1_{h}")[:, :]),
                     f"t1_{h}")
            done(dve, "nz1")
            for i in range(2):
                free(tt(yT[:, MH + 2 * i:MH + 2 * i + 2, :].rearrange("p b t -> p (b t)"), got(dve, f"av{i}")[:, :],
                        nz[:, i * 512:(i + 1) * 512], MUL), f"av{i}")

            def modulation(l):
                dve.wait_ge(S("ada"), 24 * (l + 1))
                tt(mod[:, l, :], adaps[:, l * 48:(l + 1) * 48], par[:, PC["adab"] + 48 * l:PC["adab"] + 48 * (l + 1)],
                   ADD).then_inc(S("mod"), 1)
                dve.wait_ge(S("mod"), l + 1)
                for i, (c, g) in enumerate(((8, PC["nmix"]), (32, PC["nmlp"]))):
                    ins = stt(A1[2 * l + i], mod[:, l, c:c + KT], 1.0, par[:, g + 8 * l:g + 8 * l + 8], ADD, MUL)
                if l == 0:
                    ins = tt(gsc, mod[:, 0, 16:24], par[:, PB["psc"]:PB["psc"] + KT], MUL)
                V(ins)

            modulation(0)
            residual("eo")
            done(dve, "eo3")
            norm(1, lambda k: pc(PA["nw"] + KT + k), "h1")
            done(dve, "fp3")
            for b in range(HH):
                s = slice(b * T, (b + 1) * T)
                ts(hb[:, s], hb[:, s], oml[:, b:b + 1], lb[:, b:b + 1], MUL, ADD)
                ins = ts(hk[:, s], hk[:, s], oml[:, b:b + 1], None, MUL)
            ins.then_inc(S("hf"), 1)
            for j in range(4):
                tokens(f"iv{j}", ht[:, :, j * CW:(j + 1) * CW], 0, BI + j * CW, CW)
            dve.wait_ge(S("hln"), 1)
            dve.wait_ge(S("rst"), 2)
            V(dve.tensor_tensor_scan(hb, rst, hb2, 0.0, MUL, ADD))
            dve.wait_ge(S("AT0"), 1)

            def exponents(l):
                m = P >> (l + 1) if l < LEVELS else P
                if l >= 2:
                    dve.wait_ge(S("LQ"), l - 1)
                b = hb.rearrange("p (n y t) -> p n y t", y=2, t=m)
                e = LE[l % 2].rearrange("p (n y t) -> p n y t", y=2, t=m)
                n = 2 * HH * P // (2 * m)
                ref = b[:, :, 0, m - 1:m].broadcast_to([P, n, m])
                tt(e[:, :, 0, :], ref, b[:, :, 0, :], SUB)
                if l < LEVELS:
                    ins = tt(e[:, :, 1, :], b[:, :, 1, :], ref, SUB)
                else:
                    ins = dve.tensor_copy(e[:, :, 1, :], b[:, :, 1, :])
                ins.then_inc(S("LE"), 1)

            def pick(name, l, i):
                mask = K("lvl")[:, l * P:(l + 1) * P].bitcast(I32).unsqueeze(1).broadcast_to([P, 4, P])
                if l:
                    done(dve, f"lv{l - 1}_{i}")
                free(dve.copy_predicated(ATm[:, 4 * i:4 * i + 4, :], mask,
                                         got(dve, name)[:, :].rearrange("p (n j) -> p n j", n=4)), name)

            exponents(0)
            exponents(1)
            for l in range(LEVELS):
                for i in range(4):
                    pick(f"lv{l}_{i}", l, i)
                if l + 2 <= LEVELS:
                    exponents(l + 2)
            for i in range(4):
                pick(f"dg_{i}", LEVELS, i)
            modulation(1)
            for i in range(4):
                free(ts(LE[0][:, i * 512:(i + 1) * 512], got(dve, f"or{i}")[:, :], 1.0 / P, EPS, MUL, ADD), f"or{i}")
            dve.wait_ge(S("so"), 1)
            V(dve.reciprocal(LE[0], LE[0]))
            for h in range(HH):
                s = slice(h * T, (h + 1) * T)
                ins = stt(hO[:, s], hO[:, s], pc(PB["hhn"] + h), LE[0][:, s], MUL, MUL)
            V(ins)
            done(dve, "hz3")
            for i in range(4):
                tt(yT[:, 2 * i:2 * i + 2, :].rearrange("p b t -> p (b t)"), hO[:, i * 512:(i + 1) * 512],
                   hz[:, i * 512:(i + 1) * 512], MUL).then_inc(S("yH"), 1)
            residual("oo")
            done(dve, "oo3")
            norm(2, lambda k: A1[0][:, k:k + 1], "hs2")
            dve.wait_ge(S("h2"), KT)
            dve.wait_ge(S("zero"), 1)
            W = PADW + T
            V(tt(s2[:, :, 1:W], hT[:, :, 1:W], hT[:, :, 0:W - 1], ADD))
            V(tt(s4[:, 2:8, 3:W], s2[:, 2:8, 3:W], s2[:, 2:8, 1:W - 2], ADD))
            V(tt(s2[:, 4:8, 7:W], s4[:, 4:8, 7:W], s4[:, 4:8, 3:W - 4], ADD))
            V(tt(s4[:, 6:8, 15:W], s2[:, 6:8, 15:W], s2[:, 6:8, 7:W - 8], ADD))
            for g, win in enumerate(POOLS):
                s = (s2, s4)[g % 2][:, 2 * g:2 * g + 2, PADW:W]
                V(tt(s[:, :, 0:PADW], s[:, :, 0:PADW],
                     K("prc")[:, g * PADW:(g + 1) * PADW].unsqueeze(1).broadcast_to([P, 2, PADW]), MUL))
                stt(pl[:, 2 * g:2 * g + 2, :], s, 1.0 / win, hx[:, 2 * g:2 * g + 2, :], MUL, SUB)\
                    .then_inc(S("pl"), 1)
            residual("pw", lambda b: gsc[:, b:b + 1])
            done(dve, "pw3")

            def mlp(l):
                n = 3 + 2 * l
                norm(n, lambda k: A1[2 * l + 1][:, k:k + 1], f"hs{n}")
                residual(f"w2_{l}_", lambda b: mod[:, l, 40 + b:41 + b])
                done(dve, f"w2_{l}_3")

            mlp(0)
            dve.wait_ge(S("ld_s"), 16 * DMAS["ld_s"])
            for i in range(2):
                free(tt(wsT[:, 4 * i:4 * i + 4, :], got(dve, f"ws{i}")[:, :].rearrange("p (h t) -> p h t", h=4),
                        K("tri").unsqueeze(1).broadcast_to([P, 4, P]), MUL), f"ws{i}")
            norm(4, lambda k: A1[2][:, k:k + 1], "hs4")
            done(dve, "si7")
            V(dve.tensor_reduce(mu, vt, AX, ADD))
            V(ts(mu, mu, -1.0 / D, None, MUL))
            for a in range(NT):
                ts(xc[:, a, :], vt[:, a, :], mu[:, a:a + 1], None, ADD).then_inc(S("xc"), 1)
            dve.wait_ge(S("vr"), NT)
            ts(vr, vr, 1.0 / D, LN_EPS, MUL, ADD).then_inc(S("vre"), 1)
            dve.wait_ge(S("vs"), 1)
            V(dve.reciprocal(vr, vr))
            for a in range(NT):
                ins = stt(vt[:, a, :], xc[:, a, :], vr[:, a:a + 1], lng, MUL, MUL)
            V(ins)
            for a in range(NT):
                tt(vt[:, a, :], vt[:, a, :], lnb, ADD).then_inc(S("vln"), 1)
            done(dve, "si3")
            for i in range(4):
                t4 = xc.rearrange("p a n -> p (a n)")[:, i * 512:(i + 1) * 512]
                for j in range(2):
                    ins = tt(t4[:, j * T:(j + 1) * T].rearrange("p (a t) -> p a t", a=NT),
                             got(dve, f"mx{i}")[:, j * T:(j + 1) * T].rearrange("p (a t) -> p a t", a=NT),
                             bsb[:, 2 * i + j, :].unsqueeze(1).broadcast_to([P, NT, P]), ADD)
                free(ins, f"mx{i}")
                done(dve, f"mx{i}")
                tt(yT[:, 2 * i:2 * i + 2, :].rearrange("p b t -> p (b t)"), t4,
                   uT[:, 2 * i:2 * i + 2, :].rearrange("p b t -> p (b t)"), MUL).then_inc(S("yS"), 1)
            residual("so", lambda b: mod[:, 1, 16 + b:17 + b])
            done(dve, "so3")
            mlp(1)
            norm(6, lambda k: pc(PB["fg"] + k), "h6")
            for i in (1, 3):
                free(dve.tensor_copy(ot[:, i // 2, (i % 2) * 512:(i % 2 + 1) * 512], got(dve, f"f{i}")[:, :]), f"f{i}")


DMAS = dict(ld_A=15, ld_B=7, ld_C=3, ld_b=7, ld_m=2, ld_s=4)

_INS = ["x", "norm_w", "ev_w_in", "ev_b_in", "mlstm_f_bias", "mlstm_conv_w", "mlstm_conv_b", "mlstm_head_norm",
        "nsa_q_norm", "nsa_k_norm", "cmp_k_pos", "cmp_k_w1", "cmp_k_w2", "cmp_v_pos", "cmp_v_w1", "cmp_v_w2",
        "ev_w_out", "od_w_in", "od_b_in", "hgrn_lb_logits", "hgrn_head_norm", "od_w_out", "c_2", "ada_w_2",
        "ada_b_2", "norm_mix_g_2", "norm_mlp_g_2", "pool_w_2", "pool_scale_2", "sgu_w_in_2", "sgu_ln_g_2",
        "sgu_ln_b_2", "sgu_w_s_2", "sgu_b_s_2", "sgu_w_out_2", "mlp_w1_2", "mlp_w2_2", "final_g_2"]


def kernel(**inputs):
    import numpy as _np
    import concourse.bacc as _bacc
    from concourse import mybir as _mybir
    from concourse.bass_utils import run_bass_kernel_spmd as _run

    nc = _bacc.Bacc("TRN2", target_bir_lowering=False, num_devices=1)
    arrays, aps = {}, {}
    for name in _INS:
        a = _np.ascontiguousarray(inputs[name])
        if a.ndim == 1:
            a = a.reshape(1, -1)
        arrays[f"in_{name}"] = a
        aps[name] = nc.dram_tensor(f"in_{name}", a.shape, _mybir.dt.from_np(a.dtype), kind="ExternalInput").ap()
    arrays["in_cst"] = constants()
    cst = nc.dram_tensor("in_cst", arrays["in_cst"].shape, _mybir.dt.float32, kind="ExternalInput").ap()
    out = nc.dram_tensor("out_0", (1, T, D), _mybir.dt.float32, kind="ExternalOutput").ap()
    build(nc, aps, cst, out)
    r = _run(nc, [arrays], core_ids=[0])
    return r.results[0]["out_0"]
```

```python
from contextlib import ExitStack

import concourse.bass as bass
from concourse import mybir

F32 = mybir.dt.float32
F32R = mybir.dt.float32r
I32 = mybir.dt.int32
ALU = mybir.AluOpType
ACT = mybir.ActivationFunctionType
AX = mybir.AxisListType.X

P = 128
T = 256
NT = T // P
D = 1024
KT = D // P
CW = 256
EPS = 1e-6
LN_EPS = 1e-5
NEG = -1e30

MH = 4
MW = MH * P
NH, NG, ND = 8, 2, 64
NR = NH // NG
NW_ = NH * ND
C_GATE = 5 * MW
C_NQ = C_GATE + 2 * MH
C_KV = C_NQ + NW_
C_GT = C_KV + 6 * NG * ND
C_NZ = C_GT + 3 * NH
NGATE = 2 * MH + 3 * NH
CMP_LEN, CMP_STRIDE = 32, 16
NCMP = (T - CMP_LEN) // CMP_STRIDE + 1
CPAD = 32
TAPS = 4
HH = 8
LEVELS = 7
FF = 4 * D
FT = FF // P
POOLS = (2, 4, 8, 16)
PADW = 16

_c = {}
_at = 0
for _n, _w in (("idn", P), ("one", P), ("b64", P), ("m1", T), ("mc", NT * NCMP), ("mc01", NT * NCMP),
               ("prm", P), ("cos", T), ("sin", T), ("tri", P), ("sel", MH * P), ("lvl", (LEVELS + 1) * P),
               ("prc", len(POOLS) * PADW), ("rg", 4)):
    _c[_n] = (_at, _at + _w)
    _at += _w
NCST = _at

PA = dict(nw=0, b20=16, bnq=36, bkv=40, bnz=46, cvb=50, mhn=58, qn=62, kn=63, kpos=66, vpos=82)
NA_ROWS = 98
PB = dict(cvw=128, odb=160, lbl=192, hhn=208, fg=216, c=224, psc=232)
NB_ROWS = 112
PC = dict(adab=256, nmix=352, nmlp=368)
NC_ROWS = 128

HK = KT // 2
HN = HK * CW
NF = 4
NS = 4
NA = 2
AG = 512
NBANK = 7


def constants():
    import numpy as np
    c = np.zeros((P, NCST), np.float32)

    def put(name, a):
        lo, hi = _c[name]
        c[: a.shape[0], lo:hi] = a.reshape(a.shape[0], hi - lo)

    i = np.arange(P)
    put("idn", np.eye(P, dtype=np.float32))
    put("one", np.ones((P, P), np.float32))
    put("b64", (i[:, None] // ND == i[None] // ND).astype(np.float32))
    tri = np.where(i[None] <= i[:, None], 0.0, NEG).astype(np.float32)
    put("m1", np.concatenate([np.zeros((P, P), np.float32), tri], 1))
    t = np.arange(T).reshape(NT, P).T
    ok = (np.arange(NCMP) * CMP_STRIDE + CMP_LEN - 1)[None, None] <= t[:, :, None]
    put("mc", np.where(ok, 0.0, NEG).astype(np.float32))
    put("mc01", ok.astype(np.float32))
    half = ND // 8
    prm = np.zeros((P, P), np.float32)
    for g in range(NG):
        for d in range(half):
            prm[g * ND + d + half, g * ND + d] = -1.0
            prm[g * ND + d, g * ND + d + half] = 1.0
    put("prm", prm)
    inv = (np.float32(500000.0) ** (-np.arange(half, dtype=np.float32) / half)).astype(np.float32)
    ang = np.arange(T, dtype=np.float32)[None] * inv[:, None]
    cos, sin = np.ones((P, T), np.float32), np.zeros((P, T), np.float32)
    for g in range(NG):
        for h in range(2):
            at = g * ND + h * half
            cos[at:at + half], sin[at:at + half] = np.cos(ang), np.sin(ang)
    put("cos", cos)
    put("sin", sin)
    put("tri", (i[:, None] <= i[None]).astype(np.float32))
    sel = np.zeros((MH, MH, P), np.float32)
    for h in range(MH):
        sel[h, h] = 1.0
    put("sel", sel)
    lv = []
    for l in range(LEVELS):
        m = P >> (l + 1)
        s, j = i[:, None], i[None]
        lv.append(((s // (2 * m) == j // (2 * m)) & (s % (2 * m) < m) & (j % (2 * m) >= m)).astype(np.float32))
    lv.append(np.eye(P, dtype=np.float32))
    put("lvl", np.stack(lv, 1))
    pr = np.zeros((P, len(POOLS), PADW), np.float32)
    for g, w in enumerate(POOLS):
        pr[:, g] = w / np.minimum(np.arange(PADW) + 1.0, w)
    put("prc", pr)
    put("rg", (i[:, None] // CPAD == np.arange(4)[None]).astype(np.float32))
    return c


def weight_chunks(A):
    out = []
    allp = slice(0, P)

    def rows(w, h, c0, n, r0=0):
        return w[r0 + h * HK * P:r0 + (h + 1) * HK * P, c0:c0 + n].rearrange("(k p) n -> p k n", p=P)

    def cols(name, w, c0, r0=0):
        out.append((name, True, [[(allp, slice(0, HK), slice(0, CW), rows(w, h, c0, CW, r0))] for h in range(2)]))

    w = A["ev_w_in"][0]

    def paired(n, c0):
        for j in range(2):
            hs = []
            for h in range(2):
                parts = []
                for b in range(2):
                    for g in range(NG):
                        parts.append((allp, slice(0, HK), slice(b * P + g * ND, b * P + g * ND + ND),
                                      rows(w, h, c0 + (g * NR + 2 * j + b) * ND, ND)))
                hs.append(parts)
            out.append((f"{n}{j}", True, hs))

    def plain(n, c0):
        for j in range(2):
            cols(f"{n}{j}", w, c0 + j * CW)

    out.append(("gt", True, [[(allp, slice(0, HK), slice(0, 2 * MH), rows(w, h, C_GATE, 2 * MH)),
                              (allp, slice(0, HK), slice(2 * MH, NGATE), rows(w, h, C_GT, 3 * NH))]
                             for h in range(2)]))
    plain("q", 0)
    plain("k", MW)
    paired("nq", C_NQ)
    cols("ksvs", w, C_KV + CW)
    cols("kwvw", w, C_KV + 2 * CW)
    cols("kcvc", w, C_KV)
    plain("v", 2 * MW)
    for n in ("cmp_k_w1", "cmp_v_w1"):
        out.append((n, False, [[(allp, slice(0, 2 * HK), slice(0, P),
                                 A[n][0][h * 8 * P:(h + 1) * 8 * P, :].rearrange("(m p) n -> p m n", p=P))]
                               for h in range(2)]))
    plain("o", 3 * MW)
    plain("z", 4 * MW)
    paired("nz", C_NZ)
    wo = A["ev_w_out"][0]
    for j in range(4):
        low = [(slice(g * ND, (g + 1) * ND), slice(0, HK), slice(0, CW),
                wo[MW + g * NR * ND:MW + (g + 1) * NR * ND, j * CW:(j + 1) * CW].rearrange("(b d) n -> d b n", d=ND))
               for g in range(NG)]
        out.append((f"eo{j}", True, [[(allp, slice(0, HK), slice(0, CW), rows(wo, 0, j * CW, CW))], low]))
    wi = A["od_w_in"][0]
    for n, c0 in (("fp", 0), ("qp", 2 * D), ("iv", D), ("hz", 3 * D)):
        for j in range(4):
            cols(f"{n}{j}", wi, c0 + j * CW)
    for j in range(4):
        cols(f"oo{j}", A["od_w_out"][0], j * CW)
    out.append(("pool", False, [[(allp, slice(0, HK), slice(0, CW),
                                  A["pool_w_2"][0][2 * h:2 * h + 2].rearrange("g (k p) n -> p (g k) n", p=P))]
                                for h in range(2)]))

    def mlp(l):
        for j in range(FF // CW):
            cols(f"w1_{l}_{j}", A["mlp_w1_2"][l], j * CW)
        for j in range(4):
            for k in range(4):
                cols(f"w2_{l}_{j}_{k}", A["mlp_w2_2"][l], j * CW, r0=k * D)

    mlp(0)
    for j in (4, 5, 6, 7, 0, 1, 2, 3):
        cols(f"si{j}", A["sgu_w_in_2"][0], j * CW)
    for j in range(4):
        cols(f"so{j}", A["sgu_w_out_2"][0], j * CW)
    mlp(1)
    return out


def stream(A):
    chunks = weight_chunks(A)
    spread = {}
    for name, _, _ in chunks:
        if name == "gt" or name.startswith("cmp"):
            spread[name] = (0, 0)
        elif name[:2] in ("fp", "qp", "iv", "hz"):
            spread[name] = (0, 2)
        elif name.startswith("w1_0"):
            spread[name] = (1, 1)
        elif name.startswith("w2_0"):
            spread[name] = (1, 2)
    early = [n for n, _, _ in chunks[1:22] if not n.startswith("cmp")][:16]
    spread.update({n: (0, 1) for n in early})
    out, at, s = [], [0, 0], 0
    for name, split, halves in chunks:
        for h, parts in enumerate(halves):
            out.append(("w", dict(i=s, name=name, split=split, parts=parts)))
            s += 1
        l, n = spread.get(name, (0, 0))
        for _ in range(n):
            out.append(("a", (l, at[l] // 4, at[l] % 4)))
            at[l] += 1
    n = 4 * 6 * D // AG
    assert at == [n, n], at
    return chunks, out


def build(nc, A, cst_dram, out_dram):
    ctx = ExitStack()
    with ctx:
        sems = {}

        def S(name):
            if name not in sems:
                sems[name] = ctx.enter_context(nc.semaphore("s_" + name))
            return sems[name]

        def sb(name, shape, dt=F32):
            return ctx.enter_context(nc.sbuf_tensor(name, shape, dt))

        cst = sb("cst", [P, NCST])
        par = sb("par", [P, 384])
        xT = sb("xT", [P, KT, T])
        hT = sb("hT", [P, KT, PADW + T])
        hh = sb("hh", [P, KT, T], F32R)
        hl = sb("hl", [P, KT, T], F32R)
        wf = sb("wf", [P, NF, HN])
        wh = sb("wh", [P, NS, HN], F32R)
        wl = sb("wl", [P, NS, HN], F32R)
        wa = sb("wa", [P, NA, 2 * AG])
        acc = sb("acc", [P, 2, AG])
        bcb = sb("bcb", [P, 512 + 128 + 128 + 32 + 4 + 1024])
        sm = sb("sm", [P, 1024])
        mod = sb("mod", [P, 2, 48])
        rstd = sb("rstd", [P, T])[:, :]
        AR = 20640
        with nc.sbuf_tensor("ar", [P, AR], F32) as ar:
            pass
        h1s = [sb(f"h1{n}", [P, FT * T], F32R) for n in "hl"]
        ps = [ctx.enter_context(nc.psum_tensor(f"ps{i}", [P, 512], F32)) for i in range(NBANK)]
        adaps = ctx.enter_context(nc.psum_tensor("adaps", [P, 512], F32))

        def K(name):
            lo, hi = _c[name]
            return cst[:, lo:hi]

        idn, one, b64 = K("idn"), K("one"), K("b64")
        hx = hT[:, :, PADW:PADW + T]
        sq = hT[:, :, :].rearrange("p b t -> p (b t)")[:, 0:KT * T]

        def cut(at, size, pat=None, **kw):
            v = ar[:, at:at + size]
            return v.rearrange(pat, **kw) if pat else v

        qkp = cut(0, 8 * 259, "p (b t) -> p b t", t=259)
        qkc = cut(2072, 2048, "p (b t) -> p b t", t=T)
        vtok = cut(4120, 1024, "p (a n) -> p a n", a=NT)
        ET = cut(5144, 1536, "p (h n) -> p h n", h=MH)
        ST = cut(6680, 1536, "p (h n) -> p h n", h=MH)
        emrb = cut(8216, 1024)
        hm = cut(0, 1024)
        P1 = cut(0, 4096, "p (h y k) -> p h y k", h=NH, y=2)
        P0 = cut(4096, 2048, "p (h y k) -> p h y k", h=NH, y=2)
        Pc = cut(6144, 512, "p (a h n) -> p a h n", a=NT, h=NH)
        PT1 = cut(6656, 4096, "p (h y k) -> p h y k", h=NH, y=4)
        PT0 = cut(10752, 2048, "p (h y k) -> p h y k", h=NH, y=2)
        PTc = cut(12800, 512, "p (a g k) -> p a g k", a=NT, g=NG)
        XK = cut(9240, 512, "p (g t) -> p g t", g=NG)
        XV = cut(9752, 512, "p (g t) -> p g t", g=NG)
        kcvc = cut(10264, 512, "p (y t) -> p y t", y=2)
        CR = cut(10776, 960, "p (y m g n) -> p y m g n", y=2, m=16, g=NG)
        irow, frow, brow, arow, erow, trow = [ar[0:MH, 11736 + i * T:11736 + (i + 1) * T] for i in range(6)]
        ifrow = ar[0:MH, 11736:11736 + 2 * T]
        grow, orow = irow, frow
        at = 13312
        og = cut(at, 1024); at += 1024
        zg = cut(at, 1024); at += 1024
        nz = cut(at, 1024); at += 1024
        R = cut(at, 1536 + NCMP); at += 1552
        R2 = cut(at, 1536 + NCMP); at += 1552
        vsw = cut(at, 512, "p (y a n) -> p y a n", y=2, a=NT); at += 512
        VC = cut(at, P); at += P
        VC4 = cut(at, 4 * P, "p (i d) -> p i d", i=4); at += 4 * P
        assert at <= AR, at
        hb = cut(0, 2048)
        hk = cut(2048, 2048)
        hq = cut(4096, 2048)
        hz = cut(6144, 2048)
        ht = cut(8192, 2048, "p (a n) -> p a n", a=NT)
        L3 = [cut(10240, 2048), cut(12288, 2048), cut(14336, 2048)]
        ATm = cut(16384, 2048, "p (n j) -> p n j", n=2 * HH)
        AT2 = cut(18432, 1024, "p (h j) -> p h j", h=HH)
        hb2 = L3[0]
        rst = L3[1]
        hO, hR = L3[0], L3[1]
        h1h, h1l = [t[:, :].rearrange("p (f t) -> p f t", t=T) for t in h1s]
        rl = [sq[:, 0:512], sq[:, 512:1024]]
        r2 = [sq[:, 1024:1536], sq[:, 1536:2048]]
        lng = bcb[:, 804:804 + D]
        lnb = cut(16384, 1024)
        bsb = cut(17408, 1024, "p (h t) -> p h t", h=8)
        wsT = cut(18432, 1024, "p (h t) -> p h t", h=8)
        wst = K("lvl").rearrange("p (h t) -> p h t", h=8)
        uT = cut(0, 2048, "p (b t) -> p b t", t=T)
        vt = cut(2048, 2048, "p (a n) -> p a n", a=NT)
        xc = cut(4096, 2048, "p (a n) -> p a n", a=NT)
        s2 = cut(0, 8 * 272, "p (b t) -> p b t", t=272)
        s4 = cut(2176, 8 * 272, "p (b t) -> p b t", t=272)
        pl = cut(4352, 2048, "p (b t) -> p b t", t=T)
        ot = cut(0, 2048, "p (a n) -> p a n", a=NT)
        xtok = cut(0, 2048, "p (a n) -> p a n", a=NT)
        rows = [cut(2048 + i * P, P) for i in range(3)]

        smat = [0]

        def small(n):
            smat[0] += n
            assert smat[0] <= 1024
            return sm[:, smat[0] - n:smat[0]]

        gt = small(NT * NGATE).rearrange("p (a n) -> p a n", a=NT)
        acol = small(NT * MH).rearrange("p (a n) -> p a n", a=NT)
        cs = small(KT)
        mx1, mx0, mxc = small(16), small(16), small(16)
        sm1, sm0, smc = small(16), small(16), small(16)
        hk_ = small(NG * NCMP + 2)
        hv_ = small(NG * NCMP + 2)
        hvp = small(NG * 4 * CPAD)
        w2k, w2v = small(ND), small(ND)
        lb, lbt, oml, nodb = small(HH), small(HH), small(HH), small(HH)
        A1 = [small(KT), small(KT), small(KT), small(KT)]
        gsc = small(KT)
        mu, vr = small(NT), small(NT)

        chunks, items = stream(A)
        halves = [x for kind, x in items if kind == "w"]
        splits = [x for x in halves if x["split"]]
        chunk_at = {name: i for i, (name, _, _) in enumerate(chunks)}
        landed = [0] * NF
        for x in halves:
            x["slot"] = x["i"] % NF
            landed[x["slot"]] += 16 * len(x["parts"])
            x["landed"] = landed[x["slot"]]
        for n, x in enumerate(splits):
            x["n"], x["sslot"] = n, n % NS
            x["low"] = ("P", "V")[n % 2]
            x["low_n"] = n // 2 + 1
        released = {}
        place = {}
        horizon = {}
        fills = [0] * NBANK
        count = dict(unit=0, chunk=0, half=0, mid=0)

        def wf_free(x):
            return (S("wl" + x["low"]), x["low_n"]) if x["split"] else released[x["i"]]

        def loaded(x, *tiles):
            n = NGATE if x["name"] == "gt" else CW
            return [t.rearrange("p (k n) -> p k n", n=CW)[:, :, 0:n] for t in tiles]

        def high(eng, x):
            eng.wait_ge(S(f"w{x['slot']}"), x["landed"])
            if x["n"] >= NS:
                eng.wait_ge(*released[splits[x["n"] - NS]["i"]])
            h, f = loaded(x, wh[:, x["sslot"], :], wf[:, x["slot"], :])
            eng.activation(h, f, ACT.Copy).then_inc(S("wh"), 1)

        def low(eng, x):
            eng.wait_ge(S("wh"), x["n"] + 1)
            l, f, h = loaded(x, wl[:, x["sslot"], :], wf[:, x["slot"], :], wh[:, x["sslot"], :])
            eng.tensor_tensor(l, f, h, ALU.subtract).then_inc(S("wl" + x["low"]), 1)

        progress = dict(A=0, P=0, V=0)
        passed = dict(A=0, P=0, V=0)
        steps = [0]

        def modulation_step(eng, l, g, q):
            n = steps[0]
            steps[0] += 1
            a = acc[:, g % 2, :]
            eng.wait_ge(S(f"la{n % NA}"), 16 * (n // NA + 1))
            if n == 0:
                eng.wait_ge(S("cs"), 1)
            if q == 0 and n >= 8:
                eng.wait_ge(S("ada"), n // 4 - 1)
            if n:
                eng.wait_ge(S("wa"), n)
            w = wa[:, n % NA, :].rearrange("p (k n) -> p k n", n=AG)
            if q == 0:
                ins = eng.tensor_scalar(a, w[:, 0, :], cs[:, 0:1], None, ALU.mult)
            else:
                ins = eng.scalar_tensor_tensor(a, w[:, 0, :], cs[:, 2 * q:2 * q + 1], a, ALU.mult, ALU.add)
            ins.then_inc(S("wa_first"), 1)
            eng.wait_ge(S("wa_first"), n + 1)
            eng.scalar_tensor_tensor(a, w[:, 1, :], cs[:, 2 * q + 1:2 * q + 2], a, ALU.mult,
                                     ALU.add).then_inc(S("wa"), 1)

        def keep(who, eng, name):
            n = horizon[name]
            while progress[who] < len(items):
                kind, x = items[progress[who]]
                if kind == "w":
                    if x["i"] >= n:
                        break
                    if x["split"] and who == "A":
                        high(eng, x)
                    elif x["split"] and who == x["low"]:
                        low(eng, x)
                elif who == "V":
                    if passed[who] >= n:
                        break
                    modulation_step(eng, *x)
                if kind == "w":
                    passed[who] = x["i"] + 1
                progress[who] += 1

        def got(eng, name):
            ahead(eng, name)
            b, n = place[name]
            eng.wait_ge(S(f"full{b}"), n)
            return ps[b]

        def free(ins, name):
            ins.then_inc(S(f"free{place[name][0]}"), 1)

        def done(eng, name):
            ahead(eng, name)
            b, n = place[name]
            eng.wait_ge(S(f"free{b}"), n)

        ahead_of = {}

        def ahead(eng, name):
            for e, f in ahead_of.values():
                if e is eng:
                    f(name)

        block = ctx.enter_context(nc.Block())

        @block.tensor
        def _(pe):
            def begin(name, n=1):
                b = count["unit"] % NBANK
                count["unit"] += 1
                if fills[b]:
                    pe.wait_ge(S(f"free{b}"), fills[b])
                fills[b] += 1
                place[name] = (b, fills[b])
                horizon[name] = 2 * (count["chunk"] + n - 1) + NS
                return ps[b]

            def end(ins, name):
                ins.then_inc(S(f"full{place[name][0]}"), 1)

            mm = pe.matmul

            def chunk(name, product, last, k_tiles=HK, w=CW, first=None):
                assert chunk_at[name] == count["chunk"], name
                count["chunk"] += 1
                for h in range(2):
                    x = halves[2 * chunk_at[name] + h]
                    if x["split"]:
                        pe.wait_ge(S("wl" + x["low"]), x["low_n"])
                        hi = wh[:, x["sslot"], :].rearrange("p (k n) -> p k n", n=w)
                        lo = wl[:, x["sslot"], :].rearrange("p (k n) -> p k n", n=w)
                    else:
                        pe.wait_ge(S(f"w{x['slot']}"), x["landed"])
                        hi = lo = wf[:, x["slot"], :].rearrange("p (k n) -> p k n", n=w)
                    for k in range(k_tiles):
                        ins = product(hi[:, k, :], lo[:, k, :], h * k_tiles + k)
                    if h == 0 and first:
                        released[x["i"]] = (S(f"full{place[first][0]}"), place[first][1])
                    elif h == 0:
                        ins.then_inc(S("half"), 1)
                        count["half"] += 1
                        released[x["i"]] = (S("half"), count["half"])
                    elif last:
                        released[x["i"]] = (S(f"full{place[last][0]}"), place[last][1])
                    else:
                        ins.then_inc(S("mid"), 1)
                        count["mid"] += 1
                        released[x["i"]] = (S("mid"), count["mid"])
                return ins

            def three(o, wa_, wb_, xa_, xb_, first, last):
                mm(o, wa_, xa_, start=first, stop=False, skip_group_check=True)
                mm(o, wa_, xb_, start=False, stop=False, skip_group_check=True)
                return mm(o, wb_, xa_, start=False, stop=last, skip_group_check=True)

            def feat(name, sem=None, at=0):
                o = begin(name)

                def product(hi, lo, k):
                    if sem and k % 2 == 0:
                        pe.wait_ge(sem, at + k // 2 + 1)
                    for j in range(2):
                        c = slice(j * P, (j + 1) * P)
                        ins = three(o[:, j * T:(j + 1) * T], hi[:, c], lo[:, c], hh[:, k, :], hl[:, k, :],
                                    k == 0 and j == 0, k == KT - 1)
                    return ins

                end(chunk(name, product, name), name)

            def tok(name, c0=0, n=CW, sem=None):
                o = begin(name)

                def product(hi, lo, k):
                    if sem and k % 2 == 0:
                        pe.wait_ge(sem, k // 2 + 1)
                    for a in range(NT):
                        t = slice(a * P, (a + 1) * P)
                        ins = three(o[:, a * n:(a + 1) * n], hh[:, k, t], hl[:, k, t], hi[:, c0:c0 + n],
                                    lo[:, c0:c0 + n], k == 0 and a == 0, k == KT - 1)
                    return ins

                end(chunk(name, product, name), name)

            def keys_values(name):
                o = begin(name)

                def product(hi, lo, k):
                    three(o[:, 0:T], hi[:, 0:P], lo[:, 0:P], hh[:, k, :], hl[:, k, :], k == 0, k == KT - 1)
                    for a in range(NT):
                        t = slice(a * P, (a + 1) * P)
                        ins = three(o[:, T + a * P:T + (a + 1) * P], hh[:, k, t], hl[:, k, t], hi[:, P:2 * P],
                                    lo[:, P:2 * P], False, k == KT - 1)
                    return ins

                end(chunk(name, product, name), name)

            def sumsq(n):
                o = begin(f"ss{n}")
                for k in range(KT):
                    if k % 2 == 0:
                        pe.wait_ge(S("sq"), 4 * n + k // 2 + 1)
                    ins = mm(o[:, 0:T], one, sq[:, k * T:(k + 1) * T], start=(k == 0), stop=(k == KT - 1))
                end(ins, f"ss{n}")

            def ada(l, g):
                if l and g == 0:
                    pe.wait_ge(S("mod"), 1)
                pe.wait_ge(S("wa"), 4 * (12 * l + g + 1))
                for i in range(AG // P):
                    c = l * 48 + g * (AG // P) + i
                    ins = mm(adaps[:, c:c + 1], acc[:, g % 2, i * P:(i + 1) * P], one[:, 0:1], start=True, stop=True)
                ins.then_inc(S("ada"), 1)

            pe.wait_ge(S("ld_cst"), 16)
            pe.wait_ge(S("ld_x"), 32)
            for i in range(4):
                o = begin(f"x{i}")
                for k in range(4):
                    f = 4 * (i % 2) + k
                    ins = pe.transpose(o[:, k * P:(k + 1) * P], xtok[:, i // 2, f * P:(f + 1) * P], idn)
                end(ins, f"x{i}")

            def vectors(i, sem, n):
                pe.wait_ge(S(sem), 16 * DMAS[sem])
                o = begin(f"par{i}")
                end(pe.transpose(o[:, 0:n], rows[i][0:n, :], idn[0:n, 0:n]), f"par{i}")

            vectors(0, "ld_A", NA_ROWS)
            sumsq(0)
            vectors(1, "ld_B", NB_ROWS)
            vectors(2, "ld_C", NC_ROWS)

            tok("gt", 0, NGATE, S("hp0"))
            for n in ("q0", "q1", "k0", "k1"):
                feat(n)
            pe.wait_ge(S("gt"), 1)
            o = begin("gtT")
            for y in range(2):
                for a in range(NT):
                    c = (y * NT + a) * P
                    ins = pe.transpose(o[0:MH, c:c + P], gt[:, a, y * MH:(y + 1) * MH], idn)
            end(ins, "gtT")
            feat("nq0")
            feat("nq1")
            ada(0, 0)
            keys_values("ksvs")
            keys_values("kwvw")
            pe.wait_ge(S("arow"), 1)
            o = begin("aT")
            for a in range(NT):
                ins = pe.transpose(o[:, a * MH:(a + 1) * MH], arow[:, a * P:(a + 1) * P], idn[0:MH, 0:MH])
            end(ins, "aT")

            def spread_rows(nm, row, sem):
                pe.wait_ge(S(sem), 1)
                for i in range(2):
                    o = begin(f"{nm}{i}")
                    for j in range(2):
                        h = 2 * i + j
                        ins = mm(o[:, j * T:(j + 1) * T], K("sel")[0:MH, h * P:(h + 1) * P], row, start=True, stop=True)
                    end(ins, f"{nm}{i}")

            spread_rows("gb", grow, "grow")
            feat("kcvc")
            spread_rows("em", erow, "erow")
            tok("v0")
            ada(0, 1)
            pe.wait_ge(S("sqR"), 1)
            for i in range(3):
                o = begin(f"rs{i}")
                end(mm(o[:, :], b64, sq[:, i * 512:(i + 1) * 512], start=True, stop=True), f"rs{i}")
            tok("v1")
            pe.wait_ge(S("qkc"), 1)
            for h in range(MH):
                o = begin(f"st{h}")
                mm(o[:, 0:T], qkc[:, MH + h, 0:P], qkc[:, h, :], start=True, stop=True)
                ins = mm(o[:, T:T + P], qkc[:, MH + h, P:T], qkc[:, h, P:T], start=True, stop=True)
                end(ins, f"st{h}")
            o = begin("hid")
            pe.wait_ge(S("CR"), 8)
            for y, n in enumerate(("cmp_k_w1", "cmp_v_w1")):
                def product(w, _, m):
                    return mm(o[:, y * 32:y * 32 + 2 * NCMP], w, CR[:, y, m, :, :], start=(m == 0), stop=(m == 15))

                ins = chunk(n, product, "hid" if y else None, 2 * HK, P)
            end(ins, "hid")
            feat("o0")
            done(pe, "v1")
            done(pe, "st3")
            for nm in ("nm", "dn"):
                for i in range(2):
                    o = begin(f"{nm}{i}")
                    for j in range(2):
                        h = 2 * i + j
                        l0 = vtok[:, 0, h * P:(h + 1) * P] if nm == "nm" else one
                        l1 = vtok[:, 1, h * P:(h + 1) * P] if nm == "nm" else one
                        mm(o[:, j * T:(j + 1) * T], l0, ST[:, h, 0:T], start=True, stop=True)
                        ins = mm(o[:, j * T + P:(j + 1) * T], l1, ST[:, h, T:T + P], start=False, stop=True,
                                 skip_group_check=True)
                    end(ins, f"{nm}{i}")
            o = begin("cmp2")
            pe.wait_ge(S("ld_m"), 16 * DMAS["ld_m"])
            done(pe, "hid")
            for g in range(NG):
                mm(o[g * ND:(g + 1) * ND, 0:NCMP], w2k, hk_[:, g * NCMP:(g + 1) * NCMP], start=True, stop=True)
            pe.wait_ge(S("hvp"), 1)
            for g in range(NG):
                ins = mm(o[:, 64 + g * ND:64 + (g + 1) * ND], hvp[:, g * P:(g + 1) * P], w2v, start=True, stop=True)
            end(ins, "cmp2")
            pe.wait_ge(S("Rn"), 1)
            for i in range(3):
                o = begin(f"pr{i}")
                end(mm(o[:, :], K("prm"), R2[:, i * 512:(i + 1) * 512], start=True, stop=True), f"pr{i}")
            feat("o1")
            ada(0, 2)
            pe.wait_ge(S("sqc"), 1)
            o = begin("rsc")
            end(mm(o[:, 0:NCMP], b64, sq[:, 1536:1536 + NCMP], start=True, stop=True), "rsc")
            pe.wait_ge(S("sqh"), 1)
            for i in range(2):
                o = begin(f"hr{i}")
                end(mm(o[:, :], one, sq[:, i * 512:(i + 1) * 512], start=True, stop=True), f"hr{i}")
            feat("z0")
            pe.wait_ge(S("Rnc"), 1)
            o = begin("prc")
            end(mm(o[:, 0:NCMP], K("prm"), R2[:, 1536:1536 + NCMP], start=True, stop=True), "prc")
            pe.wait_ge(S("rope"), 1)
            for i in range(4):
                o = begin(f"s0_{i}")
                for j in range(2):
                    hd = 2 * i + j
                    g, b = hd // NR, hd % NR
                    gs = slice(g * ND, (g + 1) * ND)
                    for y in range(2):
                        c = (2 * j + y) * P
                        ins = mm(o[:, c:c + P], R[gs, b * T:b * T + P], R[gs, (4 + y) * T:(4 + y) * T + P],
                                 start=True, stop=True)
                end(ins, f"s0_{i}")
            pe.wait_ge(S("ropec"), 1)
            for g in range(NG):
                o = begin(f"sc{g}")
                gs = slice(g * ND, (g + 1) * ND)
                for a in range(NT):
                    for b in range(NR):
                        c = (a * NR + b) * NCMP
                        ins = mm(o[:, c:c + NCMP], R[gs, b * T + a * P:b * T + (a + 1) * P], R[gs, 1536:1536 + NCMP],
                                 start=True, stop=True)
                end(ins, f"sc{g}")
            for hd in range(NH):
                g, b = hd // NR, hd % NR
                gs = slice(g * ND, (g + 1) * ND)
                o = begin(f"s1_{hd}")
                for y in range(2):
                    ins = mm(o[:, y * T:(y + 1) * T], R[gs, b * T + P:b * T + T], R[gs, (4 + y) * T:(5 + y) * T],
                             start=True, stop=True)
                end(ins, f"s1_{hd}")
            feat("z1")
            feat("nz0")
            feat("nz1")
            ada(0, 3)
            pe.wait_ge(S("P0"), 1)
            for i in range(4):
                o = begin(f"t0_{i}")
                for j in range(4):
                    ins = pe.transpose(o[:, j * P:(j + 1) * P], P0[:, 2 * i + j // 2, j % 2, :], idn)
                end(ins, f"t0_{i}")
            pe.wait_ge(S("Pc"), 1)
            o = begin("tc")
            for j in range(4):
                ins = pe.transpose(o[:, j * P:(j + 1) * P],
                                   Pc[:, j // 2, 4 * (j % 2):4 * (j % 2) + 4, :].rearrange("p h n -> p (h n)"), idn)
            end(ins, "tc")
            pe.wait_ge(S("P1"), 1)
            for hd in range(NH):
                o = begin(f"t1_{hd}")
                for j in range(4):
                    ins = pe.transpose(o[:, j * P:(j + 1) * P], P1[:, hd, j // 2, (j % 2) * P:(j % 2 + 1) * P], idn)
                end(ins, f"t1_{hd}")
            done(pe, "kwvw")
            pe.wait_ge(S("VC4"), 1)
            for n in [f"t0_{i}" for i in range(4)] + ["tc"] + [f"t1_{i}" for i in range(NH)]:
                done(pe, n)
            for i in range(2):
                o = begin(f"av{i}")
                for j in range(2):
                    b = 2 * i + j
                    for g in range(NG):
                        hd = g * NR + b
                        gs = slice(g * ND, (g + 1) * ND)
                        for a in range(NT):
                            dst = o[gs, j * T + a * P:j * T + (a + 1) * P]
                            for y in range(2):
                                for s in range(a + 1):
                                    pt = PT0[:, hd, y, :] if a == 0 else PT1[:, hd, 2 * y + s, :]
                                    mm(dst, vsw[:, y, s, gs], pt, start=(y == 0 and s == 0), stop=False)
                            ins = mm(dst, VC4[:, hd % 4, gs], PTc[:, a, g, :], start=False, stop=True)
                end(ins, f"av{i}")
            for j in range(4):
                feat(f"eo{j}", S("yp"))

            sumsq(1)
            for n, f in (("fp", feat), ("qp", feat)):
                for j in range(4):
                    f(f"{n}{j}", S("hp1") if n == "fp" and j == 0 else None)
                    if j % 2 == 1 and (n, j) != ("fp", 1):
                        ada(0, 3 + (n == "qp") * 2 + j // 2)

            def level(l):
                pe.wait_ge(S("LQ"), l + 1)
                q = L3[l % 3]
                for i in range(4 if l < LEVELS else 2):
                    o = begin(f"lv{l}_{i}")
                    for j in range(4):
                        c = (4 * i + j) * (P if l < LEVELS else T)
                        r = c if l < LEVELS else c + P
                        ins = mm(o[:, j * P:(j + 1) * P], q[:, c:c + P], q[:, r:r + P], start=True, stop=True)
                    end(ins, f"lv{l}_{i}")

            for j in range(4):
                tok(f"iv{j}")
                if j % 2 == 1:
                    ada(0, 7 + j // 2)
            for i in range(4):
                o = begin(f"dg_{i}")
                for j in range(4):
                    c = (4 * i + j) * P
                    ins = mm(o[:, j * P:(j + 1) * P], hk[:, c:c + P], hq[:, c:c + P], start=True, stop=True)
                end(ins, f"dg_{i}")
            for l in range(LEVELS + 1):
                level(l)
                if l < 4:
                    feat(f"hz{l}")
                if l in (0, 3, 5):
                    ada(0, {0: 9, 3: 10, 5: 11}[l])
            done(pe, "iv3")
            done(pe, "lv7_0")
            done(pe, "lv7_1")
            done(pe, f"lv{LEVELS - 1}_3")
            for i in range(4):
                o = begin(f"ho{i}")
                for j in range(2):
                    h = 2 * i + j
                    v0, v1 = ht[:, 0, h * P:(h + 1) * P], ht[:, 1, h * P:(h + 1) * P]
                    mm(o[:, j * T:j * T + P], v0, ATm[:, 2 * h, :], start=True, stop=True)
                    mm(o[:, j * T + P:(j + 1) * T], v0, AT2[:, h, :], start=True, stop=False)
                    ins = mm(o[:, j * T + P:(j + 1) * T], v1, ATm[:, 2 * h + 1, :], start=False, stop=True)
                end(ins, f"ho{i}")
            for i in range(4):
                pe.wait_ge(S("sqo"), i + 1)
                o = begin(f"or{i}")
                end(mm(o[:, :], one, sq[:, i * 512:(i + 1) * 512], start=True, stop=True), f"or{i}")
            for j in range(4):
                feat(f"oo{j}", S("yp"), 4)

            sumsq(2)
            for g in range(4):
                begin(f"pw{g}")

            def product(w, _, n):
                g, k = n // 2, n % 2
                b, _ = place[f"pw{g}"]
                if k == 0:
                    pe.wait_ge(S("pl"), g + 1)
                for j in range(2):
                    ins = mm(ps[b][:, j * T:(j + 1) * T], w[:, j * P:(j + 1) * P], pl[:, n, :],
                             start=(k == 0 and j == 0), stop=(k == 1), skip_group_check=True)
                if k == 1 and g < 3:
                    end(ins, f"pw{g}")
                return ins

            end(chunk("pool", product, "pw3", first="pw1"), "pw3")

            def mlp(l):
                n = 3 + 2 * l
                sumsq(n)
                for j in range(FF // CW):
                    feat(f"w1_{l}_{j}", S(f"hp{n}") if j == 0 else None)
                    if l == 0 and j % 4 == 3 and j > 3:
                        ada(1, j // 4 - 1)
                for j in range(4):
                    o = begin(f"w2_{l}_{j}", 4)
                    for q in range(4):
                        def product(hi, lo, k):
                            if j == 0 and k % 2 == 0:
                                pe.wait_ge(S("h1l"), 16 * l + 4 * q + k // 2 + 1)
                            for i in range(2):
                                c = slice(i * P, (i + 1) * P)
                                ins = three(o[:, i * T:(i + 1) * T], hi[:, c], lo[:, c], h1h[:, q * KT + k, :],
                                            h1l[:, q * KT + k, :], q == 0 and k == 0 and i == 0,
                                            q == 3 and k == KT - 1)
                            return ins

                        ins = chunk(f"w2_{l}_{j}_{q}", product, f"w2_{l}_{j}" if q == 3 else None)
                        if q == 3:
                            end(ins, f"w2_{l}_{j}")
                        if l == 0 and q % 2 == 1:
                            ada(1, 3 + 2 * j + q // 2)
                if l == 0:
                    ada(1, 11)

            mlp(0)
            pe.wait_ge(S("ld_s"), 16 * DMAS["ld_s"])
            for i in range(2):
                o = begin(f"ws{i}")
                for j in range(4):
                    ins = pe.transpose(o[:, j * P:(j + 1) * P], wst[:, 4 * i + j, :], idn)
                end(ins, f"ws{i}")
            sumsq(4)
            for j in range(4, 8):
                tok(f"si{j}", sem=S("hp4") if j == 4 else None)
            for j in range(4):
                feat(f"si{j}")
            done(pe, "ws1")
            pe.wait_ge(S("vln"), NT)
            for i in range(4):
                o = begin(f"mx{i}")
                for j in range(2):
                    h = 2 * i + j
                    for a in range(NT):
                        ins = mm(o[:, (2 * j + a) * P:(2 * j + a + 1) * P], vt[:, a, h * P:(h + 1) * P], wsT[:, h, :],
                                 start=True, stop=True)
                end(ins, f"mx{i}")
            for j in range(4):
                feat(f"so{j}", S("yp"), 8)
            mlp(1)
            sumsq(6)
            pe.wait_ge(S("hs6"), 4)
            for i in range(4):
                o = begin(f"f{i}")
                for k in range(4):
                    f = 4 * (i % 2) + k
                    ins = pe.transpose(o[:, k * P:(k + 1) * P], hx[:, f, (i // 2) * P:(i // 2 + 1) * P], idn)
                end(ins, f"f{i}")
            assert count["chunk"] == len(chunks)

        def row_loads():
            A_, B_, C_ = rows
            ev = A["ev_b_in"][0]

            def r128(v):
                return v.rearrange("(r f) -> r f", f=P)

            def pair(v):
                return v.rearrange("(g b d) -> g b d", g=NG, d=ND)

            a = [(A_[0:16, :], A["norm_w"].rearrange("l (r f) -> (l r) f", f=P)),
                 (A_[16:36, :], r128(ev[0:C_GATE])),
                 (A_[40:46, :], r128(ev[C_KV:C_GT])),
                 (A_[50:58, :], r128(A["mlstm_conv_b"][0])),
                 (A_[58:62, :], r128(A["mlstm_head_norm"][0])),
                 (A_[66:82, :], A["cmp_k_pos"][0].rearrange("(m l) d -> m (l d)", l=2)),
                 (A_[82:98, :], A["cmp_v_pos"][0].rearrange("(m l) d -> m (l d)", l=2))]
            for g in range(NG):
                gs = slice(g * ND, (g + 1) * ND)
                a.append((A_[36:40, gs], pair(ev[C_NQ:C_KV])[g]))
                a.append((A_[46:50, gs], pair(ev[C_NZ:C_NZ + NW_])[g]))
                a.append((A_[62:63, gs], A["nsa_q_norm"][0:1, :]))
                a.append((A_[63:66, gs], A["nsa_k_norm"][0]))
            b = [(B_[0:32, :], A["mlstm_conv_w"][0].rearrange("t (r f) -> (t r) f", f=P)),
                 (B_[32:64, :], r128(A["od_b_in"][0])),
                 (B_[64:80, :], A["hgrn_lb_logits"].rearrange("l (r f) -> (l r) f", f=P)),
                 (B_[80:88, :], r128(A["hgrn_head_norm"][0])),
                 (B_[88:96, :], r128(A["final_g_2"][0])),
                 (B_[96:104, :], r128(A["c_2"][0])),
                 (B_[104:112, :], r128(A["pool_scale_2"][0]))]
            c = [(C_[0:96, :], A["ada_b_2"].rearrange("l (r f) -> (l r) f", f=P)),
                 (C_[96:112, :], A["norm_mix_g_2"].rearrange("l (r f) -> (l r) f", f=P)),
                 (C_[112:128, :], A["norm_mlp_g_2"].rearrange("l (r f) -> (l r) f", f=P))]
            return dict(ld_A=a, ld_B=b, ld_C=c)

        BV, BVS, BVW, BG, BF, BI = 0, 512, 640, 768, 800, 804
        loads = row_loads()
        ev = A["ev_b_in"]
        loads["ld_b"] = [(bcb[:, BV:BV + 512], ev[0:1, 2 * MW:3 * MW].broadcast_to([P, 512])),
                         (bcb[:, BVS:BVS + P], ev[0:1, C_KV + 3 * P:C_KV + 4 * P].broadcast_to([P, P])),
                         (bcb[:, BVW:BVW + P], ev[0:1, C_KV + 5 * P:C_KV + 6 * P].broadcast_to([P, P])),
                         (bcb[:, BG:BG + 8], ev[0:1, C_GATE:C_NQ].broadcast_to([P, 8])),
                         (bcb[:, BG + 8:BG + 32], ev[0:1, C_GT:C_NZ].broadcast_to([P, 24])),
                         (bcb[:, BF:BF + MH], A["mlstm_f_bias"].broadcast_to([P, MH])),
                         (bcb[:, BI:BI + D], A["od_b_in"][0:1, D:2 * D].broadcast_to([P, D]))]
        loads["ld_m"] = [(w2k, A["cmp_k_w2"][0]), (w2v, A["cmp_v_w2"][0])]
        loads["ld_s"] = [(wst, A["sgu_w_s_2"][0].rearrange("h t s -> t h s")),
                         (lng, A["sgu_ln_g_2"].broadcast_to([P, D])),
                         (lnb, A["sgu_ln_b_2"].broadcast_to([P, D])),
                         (bsb.rearrange("p h t -> p (h t)"),
                          A["sgu_b_s_2"].rearrange("l h t -> l (h t)").broadcast_to([P, 8 * P]))]
        assert all(DMAS[k] == len(v) for k, v in loads.items()), {k: len(v) for k, v in loads.items()}

        @block.sync
        def _(sp):
            sp.dma_start(xtok[:, 0, :], A["x"][0, 0:P, :]).then_inc(S("ld_x"), 16)
            sp.dma_start(xtok[:, 1, :], A["x"][0, P:T, :]).then_inc(S("ld_x"), 16)
            for dst, src in loads["ld_A"]:
                sp.dma_start(dst, src).then_inc(S("ld_A"), 16)
            na = 0
            for kind, x in items:
                if kind == "w":
                    if x["i"] >= NF:
                        sp.wait_ge(*wf_free(halves[x["i"] - NF]))
                    w = wf[:, x["slot"], :].rearrange("p (k n) -> p k n", n=P if x["name"].startswith("cmp") else CW)
                    for p, k, c, src in x["parts"]:
                        sp.dma_start(w[p, k, c], src).then_inc(S(f"w{x['slot']}"), 16)
                else:
                    l, g, q = x
                    if na >= NA:
                        sp.wait_ge(S("wa"), na - NA + 1)
                    sp.dma_start(wa[:, na % NA, :].rearrange("p (k n) -> p k n", n=AG),
                                 A["ada_w_2"][l][q * 2 * P:(q + 1) * 2 * P, g * AG:(g + 1) * AG]
                                 .rearrange("(k p) n -> p k n", p=P)).then_inc(S(f"la{na % NA}"), 16)
                    na += 1
            for i in range(4):
                done(sp, f"f{i}")
            for a in range(NT):
                sp.dma_start(out_dram[0, a * P:(a + 1) * P, :], ot[:, a, :]).then_inc(S("st"), 16)
            sp.wait_ge(S("st"), 16 * NT)

        @block.gpsimd
        def _(g):
            ahead_of["P"] = (g, lambda name: keep("P", g, name))
            def full(name):
                ahead(g, name)
                b, n = place[name]
                g.wait_ge(S(f"full{b}"), n)

            g.dma_start(cst[:, :], cst_dram).then_inc(S("ld_cst"), 16)
            for nm in ("ld_B", "ld_C", "ld_b", "ld_m"):
                for dst, src in loads[nm]:
                    g.dma_start(dst, src).then_inc(S(nm), 16)
            g.memset(hvp, 0.0).then_inc(S("zero"), 1)
            full("par2")
            g.memset(qkp[:, :, 0:3], 0.0).then_inc(S("zero"), 1)
            ahead(g, "gb1")
            g.wait_ge(S("ET"), 1)
            g.wait_ge(S("ld_cst"), 16)
            tri = K("tri").unsqueeze(1).broadcast_to([P, MH, P])
            g.tensor_tensor(ET[:, :, 0:P], ET[:, :, 0:P], tri, ALU.mult).then_inc(S("ETm"), 1)
            g.tensor_tensor(ET[:, :, T:T + P], ET[:, :, T:T + P], tri, ALU.mult).then_inc(S("ETm"), 1)
            for n in ("o0", "o1", "z0", "z1"):
                done(g, n)
            g.tensor_tensor(og, og, zg, ALU.mult).then_inc(S("oz"), 1)
            for n in ("nz0", "nz1", "eo0", "eo1", "eo2", "eo3"):
                done(g, n)
            g.memset(rst, 1.0).then_inc(S("rst"), 1)
            g.wait_ge(S("rst"), 1)
            g.memset(rst.rearrange("p (n t) -> p n t", t=P)[:, :, 0:1], 0.0).then_inc(S("rst"), 1)
            g.memset(ATm, 0.0).then_inc(S("AT0"), 1)
            for n in [f"fp{i}" for i in range(4)] + [f"qp{i}" for i in range(4)] + [f"iv{i}" for i in range(4)]:
                done(g, n)
            for l in range(LEVELS + 1):
                ahead(g, "dg_3" if l == 0 else f"hz{l - 1}" if l < 5 else f"lv{l - 3}_3")
                g.wait_ge(S("LX"), l + 1)
                m = P >> (l + 1) if l < LEVELS else P
                v = L3[l % 3].rearrange("p (n y t) -> p n y t", y=2, t=m)
                for y, src in ((0, hk), (1, hq)):
                    s = src.rearrange("p (n y t) -> p n y t", y=2, t=m)
                    ins = g.tensor_tensor(v[:, :, y, :], v[:, :, y, :], s[:, :, y, :], ALU.mult)
                ins.then_inc(S("LQ"), 1)
            for j in range(4):
                done(g, f"oo{j}")
            for dst, src in loads["ld_s"]:
                g.dma_start(dst, src).then_inc(S("ld_s"), 16)
            full("ss2")
            g.memset(hT[:, :, 0:PADW], 0.0).then_inc(S("zero"), 1)

            def hidden(l):
                for j in range(FF // CW):
                    done(g, f"w1_{l}_{j}")
                    g.wait_ge(S("h1h"), 16 * l + j + 1)
                    g.tensor_tensor(h1l[:, 2 * j:2 * j + 2, :].rearrange("p f t -> p (f t)"), r2[j % 2],
                                    h1h[:, 2 * j:2 * j + 2, :].rearrange("p f t -> p (f t)"),
                                    ALU.subtract).then_inc(S("h1l"), 1)
                for j in range(4):
                    done(g, f"w2_{l}_{j}")

            hidden(0)
            for n in [f"si{j}" for j in (4, 5, 6, 7, 0, 1, 2, 3)] + [f"so{j}" for j in range(4)]:
                done(g, n)
            hidden(1)

        @block.scalar
        def _(act):
            ahead_of["A"] = (act, lambda name: keep("A", act, name))
            chain = [0]

            def A_(out, in_, f=ACT.Identity, **kw):
                return act.activation(out, in_, f, **kw)

            def step(ins):
                chain[0] += 1
                ins.then_inc(S("a"), 1)
                act.wait_ge(S("a"), chain[0])

            def pc(c):
                return par[:, c:c + 1]

            def flat(v):
                return v.rearrange("p b t -> p (b t)")

            def root(names, dst, n, mean, eps, sem):
                for i, nm in enumerate(names):
                    free(A_(dst[:, i * n:(i + 1) * n], got(act, nm)[:, 0:n], ACT.Ln, scale=1.0 / mean, bias=eps), nm)
                for nm in names:
                    done(act, nm)
                A_(dst, dst, ACT.Exp, scale=-0.5).then_inc(S(sem), 1)

            def norm(n, prev, shift=None):
                for i in range(4):
                    if n:
                        done(act, f"{prev}{i}")
                    A_(sq[:, i * 512:(i + 1) * 512], flat(xT[:, 2 * i:2 * i + 2, :]),
                       ACT.Square).then_inc(S("sq"), 1)
                root([f"ss{n}"], rstd, T, D, EPS, "std")
                if n == 6:
                    return
                for q in range(4):
                    act.wait_ge(S(f"hs{n}"), q + 1)
                    if shift is None:
                        ins = A_(flat(hh[:, 2 * q:2 * q + 2, :]), hx[:, 2 * q:2 * q + 2, :], ACT.Copy)
                    else:
                        l, c = shift
                        for k in (2 * q, 2 * q + 1):
                            ins = A_(hx[:, k, :] if n == 2 else hh[:, k, :], hx[:, k, :],
                                     bias=mod[:, l, c + k:c + k + 1])
                    ins.then_inc(S(f"hh{n}"), 1)

            def parts(src, at, sem, before):
                ahead(act, before)
                act.wait_ge(*sem)
                A_(flat(hh[:, at:at + 2, :]), src, ACT.Copy).then_inc(S("yh"), 1)

            def both(name, dst, f, cols):
                o = got(act, name)
                for j in range(2):
                    ins = A_(dst(j), o[:, j * T:(j + 1) * T], f, bias=cols(j))
                free(ins, name)

            def whole(name, dst, f=ACT.Identity, n=512):
                free(A_(dst, got(act, name)[:, 0:n], f), name)

            for i in (0, 2):
                o = got(act, f"x{i}")
                free(A_(xT[:, 4 * (i % 2):4 * (i % 2) + 4, (i // 2) * P:(i // 2 + 1) * P],
                        o[:, :].rearrange("p (b t) -> p b t", t=P)), f"x{i}")
            for i in range(4):
                done(act, f"x{i}")
            norm(0, None)
            done(act, "par1")
            A_(cs, par[:, PB["c"]:PB["c"] + KT], ACT.Silu).then_inc(S("cs"), 1)
            act.wait_ge(S("lbx"), 1)
            A_(lb, lb, ACT.Exp)
            A_(oml, oml, ACT.Exp).then_inc(S("lbe"), 1)
            done(act, "par0")
            for i, n in enumerate(("q0", "q1", "k0", "k1")):
                both(n, lambda j: qkp[:, 2 * i + j, 3:3 + T], ACT.Identity, lambda j: pc(PA["b20"] + 2 * i + j))
            act.wait_ge(S("gt"), 1)
            A_(gt[:, :, 8:NGATE], gt[:, :, 8:NGATE], ACT.Sigmoid).then_inc(S("gsig"), 1)
            ahead(act, "gtT")
            act.wait_ge(S("absf"), 1)
            step(A_(erow, trow, ACT.Exp, scale=-1.0))
            A_(erow, erow, ACT.Ln, bias=1.0).then_inc(S("lnf"), 1)
            for i in range(2):
                both(f"nq{i}", lambda j: R[:, (2 * i + j) * T:(2 * i + j + 1) * T], ACT.Identity,
                     lambda j: pc(PA["bnq"] + 2 * i + j))
            ahead(act, "ksvs")
            act.wait_ge(S("conv"), 1)
            A_(flat(qkc), flat(qkc), ACT.Silu).then_inc(S("qkc"), 1)
            ahead(act, "kwvw")
            act.wait_ge(S("bg"), 1)
            A_(erow, trow, ACT.Exp, scale=-1.0).then_inc(S("erow"), 1)
            done(act, "nq1")
            done(act, "ksvs")
            done(act, "kwvw")
            A_(sq[:, 0:1536], R[:, 0:1536], ACT.Square).then_inc(S("sqR"), 1)
            done(act, "gb1")
            e2 = flat(ET)
            A_(e2, e2, ACT.Exp, scale=-1.0).then_inc(S("ET"), 1)
            for i in range(2):
                whole(f"em{i}", emrb[:, i * 512:(i + 1) * 512])
            root(["rs0", "rs1", "rs2"], R2[:, 0:1536], 512, ND, EPS, "sR")
            o = got(act, "hid")
            A_(hk_[:, 0:2 * NCMP], o[:, 0:2 * NCMP], ACT.Gelu_apprx_tanh)
            free(A_(hv_[:, 0:2 * NCMP], o[:, 32:32 + 2 * NCMP], ACT.Gelu_apprx_tanh), "hid")

            def gate(nm, i):
                t, f, c = dict(o=(og, ACT.Sigmoid, PA["b20"] + 12), z=(zg, ACT.Silu, PA["b20"] + 16),
                               nz=(nz, ACT.Silu, PA["bnz"]))[nm]
                both(f"{nm}{i}", lambda j: t[:, (2 * i + j) * T:(2 * i + j + 1) * T], f, lambda j: pc(c + 2 * i + j))

            gate("o", 0)
            for i in range(2):
                whole(f"dn{i}", e2[:, i * 512:(i + 1) * 512], ACT.Abs)
            done(act, "nm1")
            A_(sq[:, 0:1024], hm, ACT.Square).then_inc(S("sqh"), 1)
            gate("o", 1)
            root(["rsc"], R2[:, 1536:1536 + NCMP], NCMP, ND, EPS, "sRc")
            root(["hr0", "hr1"], e2[:, 0:1024], 512, P, EPS, "sh")
            gate("z", 0)
            for i, v in enumerate((P0, Pc, P1)):
                if i == 2:
                    gate("z", 1)
                    gate("nz", 0)
                ahead(act, ("s0_3", "sc1", "nz0")[i])
                act.wait_ge(S("smax"), i + 1)
                v = v[:, :, :, 0:NCMP] if i == 1 else v
                A_(v, v, ACT.Exp).then_inc(S("sexp"), 1)
            gate("nz", 1)
            for i in range(4):
                whole(f"t0_{i}", PT0[:, 2 * i:2 * i + 2, :, :].rearrange("p h y k -> p (h y k)"))
            whole("tc", PTc.rearrange("p a g k -> p (a g k)"))
            for h in range(0, NH, 2):
                whole(f"t1_{h}", PT1[:, h, :, :].rearrange("p y k -> p (y k)"))
            for i in range(2):
                parts(og[:, i * 512:(i + 1) * 512], 2 * i, (S("yA"), 1), "nz1")
            for i in range(2):
                done(act, f"av{i}")
                A_(flat(hh[:, MH + 2 * i:MH + 2 * i + 2, :]), nz[:, i * 512:(i + 1) * 512],
                   ACT.Copy).then_inc(S("yh"), 1)
            norm(1, "eo")
            act.wait_ge(S("ndb"), 1)
            for i in range(4):
                o = got(act, f"fp{i}")
                for j in range(2):
                    b = 2 * i + j
                    A_(hb[:, b * T:(b + 1) * T], o[:, j * T:(j + 1) * T], ACT.Sigmoid, bias=pc(PB["odb"] + b))
                    ins = A_(hk[:, b * T:(b + 1) * T], o[:, j * T:(j + 1) * T], ACT.Sigmoid, bias=nodb[:, b:b + 1],
                             scale=-1.0)
                free(ins, f"fp{i}")
            ahead(act, "qp0")
            act.wait_ge(S("hf"), 1)
            A_(hb2, hb, ACT.Ln).then_inc(S("hln"), 1)
            for i in range(4):
                both(f"qp{i}", lambda j: hq[:, (2 * i + j) * T:(2 * i + j + 1) * T], ACT.Silu,
                     lambda j: pc(PB["odb"] + 16 + 2 * i + j))
            for i in range(4):
                done(act, f"iv{i}")
            for l in range(LEVELS + 1):
                ahead(act, "dg_3" if l < 3 else f"lv{l - 3}_3")
                act.wait_ge(S("LE"), l + 1)
                A_(L3[l % 3], L3[l % 3], ACT.Exp).then_inc(S("LX"), 1)
                if 1 <= l <= 4:
                    both(f"hz{l - 1}", lambda j: hz[:, (2 * l - 2 + j) * T:(2 * l - 1 + j) * T], ACT.Silu,
                         lambda j: pc(PB["odb"] + 24 + 2 * l - 2 + j))
            for i in range(2):
                whole(f"lv7_{i}", AT2[:, 4 * i:4 * i + 4, :].rearrange("p h j -> p (h j)"))
            for i in range(4):
                whole(f"ho{i}", hO[:, i * 512:(i + 1) * 512])
                done(act, f"ho{i}")
                A_(sq[:, i * 512:(i + 1) * 512], hO[:, i * 512:(i + 1) * 512], ACT.Square).then_inc(S("sqo"), 1)
            root([f"or{i}" for i in range(4)], hR, 512, P, EPS, "so")
            for i in range(4):
                parts(hO[:, i * 512:(i + 1) * 512], 2 * i, (S("yH"), i + 1), "or3")
            norm(2, "oo", (0, 0))

            def mlp(l, prev):
                norm(3 + 2 * l, prev, (l, 24))

                def copy(j):
                    done(act, f"w1_{l}_{j}")
                    A_(flat(h1h[:, 2 * j:2 * j + 2, :]), r2[j % 2], ACT.Copy).then_inc(S("h1h"), 1)

                for j in range(FF // CW):
                    o = got(act, f"w1_{l}_{j}")
                    if j >= 2:
                        done(act, f"w1_{l}_{j - 2}")
                    A_(rl[j % 2], o[:, :], ACT.Relu).then_inc(S("relu"), 1)
                    if j:
                        copy(j - 1)
                copy(FF // CW - 1)

            mlp(0, "pw")
            norm(4, "w2_0_", (1, 0))
            for j in range(4):
                o = got(act, f"si{4 + j}")
                free(A_(vt[:, :, j * CW:(j + 1) * CW], o[:, :].rearrange("p (a n) -> p a n", a=NT), ACT.Gelu),
                     f"si{4 + j}")
            whole("si0", flat(uT[:, 0:2, :]), ACT.Gelu)
            for a in range(NT):
                act.wait_ge(S("xc"), a + 1)
                A_(sq[:, a * D:(a + 1) * D], xc[:, a, :], ACT.Square, accum_out=vr[:, a:a + 1]).then_inc(S("vr"), 1)
            act.wait_ge(S("vr"), NT)
            step(A_(vr, vr, ACT.Ln, scale=1.0 / D, bias=LN_EPS))
            A_(vr, vr, ACT.Exp, scale=-0.5).then_inc(S("vs"), 1)
            for j in range(1, 4):
                whole(f"si{j}", flat(uT[:, 2 * j:2 * j + 2, :]), ACT.Gelu)
            for i in range(4):
                parts(flat(xc)[:, i * 512:(i + 1) * 512], 2 * i, (S("yS"), i + 1), f"mx{i}")
            mlp(1, "so")
            norm(6, "w2_1_")
            for i in (0, 2):
                whole(f"f{i}", ot[:, i // 2, (i % 2) * 512:(i % 2 + 1) * 512])

        @block.vector
        def _(dve):
            ahead_of["V"] = (dve, lambda name: keep("V", dve, name))
            chain = [0]

            def V(ins):
                chain[0] += 1
                ins.then_inc(S("v"), 1)
                dve.wait_ge(S("v"), chain[0])

            def pc(c):
                return par[:, c:c + 1]

            ts, tt, stt = dve.tensor_scalar, dve.tensor_tensor, dve.scalar_tensor_tensor
            MUL, ADD, SUB, MAX = ALU.mult, ALU.add, ALU.subtract, ALU.max

            def norm(n, gain, shift=None):
                ahead(dve, f"ss{n}")
                dve.wait_ge(S("std"), n + 1)

                def scale(q):
                    for k in (2 * q, 2 * q + 1):
                        ins = stt(hx[:, k, :], xT[:, k, :], gain(k), rstd, MUL, MUL)
                    ins.then_inc(S(f"hs{n}"), 1)

                scale(0)
                scale(1)
                for q in range(4):
                    if n not in (2, 6):
                        dve.wait_ge(S(f"hh{n}"), q + 1)
                        if shift is None:
                            ins = tt(hl[:, 2 * q:2 * q + 2, :], hx[:, 2 * q:2 * q + 2, :], hh[:, 2 * q:2 * q + 2, :], SUB)
                        else:
                            l, c = shift
                            for k in (2 * q, 2 * q + 1):
                                ins = stt(hl[:, k, :], hx[:, k, :], mod[:, l, c + k:c + k + 1], hh[:, k, :], ADD, SUB)
                        ins.then_inc(S(f"hp{n}"), 1)
                    if q < 2:
                        scale(q + 2)

            yparts = [0]

            def parts(src, at):
                yparts[0] += 1
                dve.wait_ge(S("yh"), yparts[0])
                tt(hl[:, at:at + 2, :].rearrange("p b t -> p (b t)"), src,
                   hh[:, at:at + 2, :].rearrange("p b t -> p (b t)"), SUB).then_inc(S("yp"), 1)

            def residual(name, gain=None):
                for i in range(4):
                    o = got(dve, f"{name}{i}")
                    if gain is None:
                        x = xT[:, 2 * i:2 * i + 2, :].rearrange("p b t -> p (b t)")
                        ins = tt(x, o[:, :], x, ADD)
                    else:
                        for j in range(2):
                            b = 2 * i + j
                            ins = stt(xT[:, b, :], o[:, j * T:(j + 1) * T], gain(b), xT[:, b, :], MUL, ADD)
                    free(ins, f"{name}{i}")

            for i in (1, 3):
                o = got(dve, f"x{i}")
                free(dve.tensor_copy(xT[:, 4 * (i % 2):4 * (i % 2) + 4, (i // 2) * P:(i // 2 + 1) * P],
                                     o[:, :].rearrange("p (b t) -> p b t", t=P)), f"x{i}")
            for i, n in enumerate((NA_ROWS, NB_ROWS, NC_ROWS)):
                free(dve.tensor_copy(par[:, i * P:i * P + n], got(dve, f"par{i}")[:, 0:n]), f"par{i}")
                done(dve, f"par{i}")
                if i == 0:
                    for j in range(4):
                        done(dve, f"x{j}")
                    norm(0, lambda k: pc(PA["nw"] + k))
            V(ts(pc(PA["qn"]), pc(PA["qn"]), ND ** -0.5, None, MUL))
            l0, l1 = par[:, PB["lbl"]:PB["lbl"] + HH], par[:, PB["lbl"] + HH:PB["lbl"] + 2 * HH]
            V(tt(lbt, l0, l1, MAX))
            tt(lb, l0, lbt, SUB)
            tt(oml, l1, lbt, SUB).then_inc(S("lbx"), 1)
            ts(nodb, par[:, PB["odb"]:PB["odb"] + HH], -1.0, None, MUL).then_inc(S("ndb"), 1)
            dve.wait_ge(S("ld_b"), 16 * DMAS["ld_b"])
            o = got(dve, "gt")
            free(tt(gt, o[:, 0:NT * NGATE].rearrange("p (a n) -> p a n", a=NT),
                    bcb[:, BG:BG + NGATE].unsqueeze(1).broadcast_to([P, NT, NGATE]), ADD), "gt")
            done(dve, "gt")
            tt(gt[:, :, MH:2 * MH], gt[:, :, MH:2 * MH],
               bcb[:, BF:BF + MH].unsqueeze(1).broadcast_to([P, NT, MH]), ADD).then_inc(S("gt"), 1)
            dve.wait_ge(S("lbe"), 1)
            V(tt(lbt, lb, oml, ADD))
            V(dve.reciprocal(lbt, lbt))
            V(tt(lb, lb, lbt, MUL))
            V(ts(oml, lb, -1.0, 1.0, MUL, ADD))

            def tokens(name, dst, c0, b0, n, last=True):
                o = got(dve, name)
                ins = tt(dst, o[:, c0:c0 + NT * n].rearrange("p (a n) -> p a n", a=NT),
                         bcb[:, b0:b0 + n].unsqueeze(1).broadcast_to([P, NT, n]), ADD)
                free(ins, name)

            free(dve.tensor_copy(ifrow, got(dve, "gtT")[0:MH, :]), "gtT")
            done(dve, "gtT")
            stt(trow, frow, -1.0, frow, MUL, MAX).then_inc(S("absf"), 1)
            dve.wait_ge(S("absf"), 1)
            done(dve, "k1")
            dve.wait_ge(S("zero"), 2)
            for tap in range(TAPS):
                for b in range(8):
                    w = pc(PB["cvw"] + tap * 8 + b)
                    if tap == 0:
                        ins = ts(qkc[:, b, :], qkp[:, b, 0:T], w, pc(PA["cvb"] + b), MUL, ADD)
                    else:
                        ins = stt(qkc[:, b, :], qkp[:, b, tap:tap + T], w, qkc[:, b, :], MUL, ADD)
                if tap < TAPS - 1:
                    V(ins)
                else:
                    ins.then_inc(S("conv"), 1)
                if tap == 1:
                    V(ts(frow, frow, 0.0, None, ALU.min))
                    dve.wait_ge(S("lnf"), 1)
                    V(tt(trow, frow, erow, SUB))
                    V(dve.memset(orow, 1.0))
                    V(dve.tensor_tensor_scan(brow, orow, trow, 0.0, MUL, ADD))
                    tt(arow, irow, brow, SUB).then_inc(S("arow"), 1)
                    dve.wait_ge(S("arow"), 1)
                    dve.tensor_tensor_scan(grow, orow, arow, 0.0, MUL, MAX).then_inc(S("grow"), 1)
                    dve.wait_ge(S("grow"), 1)
                    tt(trow, brow, grow, ADD).then_inc(S("bg"), 1)
            for y, n in enumerate(("ksvs", "kwvw")):
                o = got(dve, n)
                ts(R[:, (4 + y) * T:(5 + y) * T], o[:, 0:T], pc(PA["bkv"] + 2 + 2 * y), None, ADD)
                tokens(n, vsw[:, y, :, :], T, BVS + y * P, P)
            free(dve.tensor_copy(acol, got(dve, "aT")[:, 0:NT * MH].rearrange("p (a h) -> p a h", a=NT)), "aT")
            done(dve, "aT")
            for i in range(2):
                o = got(dve, f"gb{i}")
                for j in range(2):
                    h = 2 * i + j
                    ts(ET[:, h, 0:T], o[:, j * T:(j + 1) * T], acol[:, 0, h:h + 1], 0.0, SUB, MAX)
                    ins = ts(ET[:, h, T:T + P], o[:, j * T + P:(j + 1) * T], acol[:, 1, h:h + 1], 0.0, SUB, MAX)
                free(ins, f"gb{i}")
            o = got(dve, "kcvc")
            for y in range(2):
                ins = ts(kcvc[:, y, :], o[:, y * T:(y + 1) * T], pc(PA["bkv"] + y), None, ADD)
            free(ins, "kcvc")
            done(dve, "kcvc")
            for y, X in enumerate((XK, XV)):
                for g in range(NG):
                    src = kcvc[g * ND:(g + 1) * ND, y, :]
                    dve.tensor_copy(X[0:ND, g, :], src)
                    ins = dve.tensor_copy(X[ND:P, g, 0:T - 1], src[:, 1:T])
            V(ins)
            for y, (X, pos) in enumerate(((XK, PA["kpos"]), (XV, PA["vpos"]))):
                for g in range(NG):
                    xv = X[:, g, :].rearrange("p (n s) -> p s n", s=CMP_STRIDE)
                    for u in range(2):
                        tt(CR[:, y, 8 * u:8 * u + 8, g, :], xv[:, 0:CMP_STRIDE:2, u:u + NCMP],
                           par[:, pos + 8 * u:pos + 8 * u + 8].unsqueeze(2).broadcast_to([P, 8, NCMP]),
                           ADD).then_inc(S("CR"), 1)
            tokens("v0", vtok[:, :, 0:CW], 0, BV, CW)
            ahead(dve, "rs2")
            dve.wait_ge(S("sR"), 1)
            done(dve, "nq1")
            for lo, hi, c in ((0, 1024, PA["qn"]), (1024, 1280, PA["kn"] + 1), (1280, 1536, PA["kn"] + 2)):
                ins = stt(R2[:, lo:hi], R[:, lo:hi], pc(c), R2[:, lo:hi], MUL, MUL)
            ins.then_inc(S("Rn"), 1)
            tokens("v1", vtok[:, :, CW:2 * CW], 0, BV + CW, CW)
            dve.wait_ge(S("ETm"), 2)
            for h in range(MH):
                free(stt(ST[:, h, :], got(dve, f"st{h}")[:, 0:T + P], float(P) ** -0.5, ET[:, h, :], MUL, MUL),
                     f"st{h}")
            done(dve, "hid")
            hv4 = hvp.rearrange("p (g i n) -> p g i n", g=NG, i=4)
            for g in range(NG):
                ins = dve.tensor_copy(hv4[:, g, :, 0:NCMP],
                                      hv_[:, g * NCMP:(g + 1) * NCMP].unsqueeze(1).broadcast_to([P, 4, NCMP]))
            ins.then_inc(S("hvp"), 1)
            den = ET.rearrange("p h n -> p (h n)")[:, 0:1024]
            done(dve, "dn1")
            done(dve, "em1")
            V(tt(den, den, emrb, MAX))
            V(dve.reciprocal(den, den))
            for i in range(2):
                free(tt(hm[:, i * 512:(i + 1) * 512], got(dve, f"nm{i}")[:, :], den[:, i * 512:(i + 1) * 512], MUL),
                     f"nm{i}")
            kc = slice(1536, 1536 + NCMP)
            o = got(dve, "cmp2")
            dve.tensor_copy(R[:, kc], o[:, 0:NCMP])
            free(dve.tensor_copy(VC, o[:, 64:64 + P]), "cmp2")
            done(dve, "cmp2")
            tt(sq[:, kc], R[:, kc], R[:, kc], MUL).then_inc(S("sqc"), 1)
            for i in range(4):
                ins = ts(VC4[:, i, :], VC, K("rg")[:, i:i + 1], None, MUL)
            ins.then_inc(S("VC4"), 1)
            for i in range(3):
                free(tt(R[:, i * 512:(i + 1) * 512].rearrange("p (b t) -> p b t", t=T),
                        got(dve, f"pr{i}")[:, :].rearrange("p (b t) -> p b t", t=T),
                        K("sin").unsqueeze(1).broadcast_to([P, 2, T]), MUL), f"pr{i}")
            r6 = R2[:, 0:1536].rearrange("p (b t) -> p b t", t=T)
            V(tt(r6, r6, K("cos").unsqueeze(1).broadcast_to([P, 6, T]), MUL))
            done(dve, "pr2")
            tt(R[:, 0:1536], R[:, 0:1536], R2[:, 0:1536], ADD).then_inc(S("rope"), 1)
            ahead(dve, "rsc")
            dve.wait_ge(S("sRc"), 1)
            stt(R2[:, kc], R[:, kc], pc(PA["kn"]), R2[:, kc], MUL, MUL).then_inc(S("Rnc"), 1)
            ends = slice(CMP_LEN - 1, T, CMP_STRIDE)
            free(tt(R[:, kc], got(dve, "prc")[:, 0:NCMP], K("sin")[:, ends], MUL), "prc")
            V(tt(R2[:, kc], R2[:, kc], K("cos")[:, ends], MUL))
            done(dve, "prc")
            tt(R[:, kc], R[:, kc], R2[:, kc], ADD).then_inc(S("ropec"), 1)
            dve.wait_ge(S("rope"), 1)
            ahead(dve, "hr1")
            dve.wait_ge(S("sh"), 1)
            for h in range(MH):
                s = slice(h * T, (h + 1) * T)
                ins = stt(R2[:, s], hm[:, s], pc(PA["mhn"] + h), den[:, s], MUL, MUL)
            V(ins)
            m1 = K("m1")
            mc = K("mc").rearrange("p (a n) -> p a n", a=NT).unsqueeze(2).broadcast_to([P, NT, NH, NCMP])
            mc01 = K("mc01").rearrange("p (a n) -> p a n", a=NT).unsqueeze(2).broadcast_to([P, NT, NH, NCMP])
            pcv = Pc[:, :, :, 0:NCMP]
            g3 = gt[:, :, 8:NGATE].rearrange("p a (h c) -> p a h c", c=3)
            sets = [(v, mx.rearrange("p (a b) -> p a b", a=sh[1]), su.rearrange("p (a b) -> p a b", a=sh[1]), gv, sh)
                    for v, mx, su, gv, sh in ((P0, mx0, sm0, g3[:, 0, :, 1:3], [P, NH, 2, P]),
                                              (pcv, mxc, smc, g3[:, :, :, 0], [P, NT, NH, NCMP]),
                                              (P1, mx1, sm1, g3[:, 1, :, 1:3], [P, NH, 2, T]))]

            def less_max(i):
                v, mx, _, _, sh = sets[i]
                V(dve.tensor_reduce(mx, v, AX, MAX))
                tt(v, v, mx.unsqueeze(3).broadcast_to(sh), SUB).then_inc(S("smax"), 1)

            def weigh(i, before):
                v, _, su, gv, sh = sets[i]
                ahead(dve, before)
                dve.wait_ge(S("sexp"), i + 1)
                V(dve.tensor_reduce(su, v, AX, ADD))
                V(dve.reciprocal(su, su))
                V(tt(su, su, gv, MUL))
                if i == 1:
                    V(tt(v, v, mc01, MUL))
                tt(v, v, su.unsqueeze(3).broadcast_to(sh), MUL).then_inc(S(("P0", "Pc", "P1")[i]), 1)

            V(dve.memset(Pc, 0.0))
            for i in range(4):
                free(tt(P0[:, 2 * i:2 * i + 2, :, :].rearrange("p h y k -> p (h y) k"),
                        got(dve, f"s0_{i}")[:, :].rearrange("p (n k) -> p n k", k=P),
                        m1[:, P:T].unsqueeze(1).broadcast_to([P, 4, P]), ADD), f"s0_{i}")
            for g in range(NG):
                hs = slice(g * NR, (g + 1) * NR)
                o = got(dve, f"sc{g}")
                free(tt(pcv[:, :, hs, :], o[:, 0:NT * NR * NCMP].rearrange("p (a h n) -> p a h n", a=NT, h=NR),
                        mc[:, :, hs, :], ADD), f"sc{g}")
            done(dve, "s0_3")
            less_max(0)
            done(dve, "sc1")
            less_max(1)
            for h in range(NH):
                free(tt(P1[:, h, :, :], got(dve, f"s1_{h}")[:, :].rearrange("p (y k) -> p y k", y=2),
                        m1.unsqueeze(1).broadcast_to([P, 2, T]), ADD), f"s1_{h}")
            for h in range(NH):
                done(dve, f"s1_{h}")
            less_max(2)
            dve.wait_ge(S("gsig"), 1)
            weigh(0, "z1")
            weigh(1, "z1")
            weigh(2, "nz0")
            ahead(dve, "nz1")
            dve.wait_ge(S("oz"), 1)
            tt(og, R2[:, 0:1024], og, MUL).then_inc(S("yA"), 1)
            for h in range(1, NH, 2):
                free(dve.tensor_copy(PT1[:, h, :, :].rearrange("p y k -> p (y k)"), got(dve, f"t1_{h}")[:, :]),
                     f"t1_{h}")
            done(dve, "nz1")
            for i in range(2):
                parts(og[:, i * 512:(i + 1) * 512], 2 * i)
            for i in range(2):
                n = nz[:, i * 512:(i + 1) * 512]
                free(tt(n, got(dve, f"av{i}")[:, :], n, MUL), f"av{i}")
                parts(n, MH + 2 * i)

            def modulation(l):
                dve.wait_ge(S("ada"), 12 * (l + 1))
                tt(mod[:, l, :], adaps[:, l * 48:(l + 1) * 48], par[:, PC["adab"] + 48 * l:PC["adab"] + 48 * (l + 1)],
                   ADD).then_inc(S("mod"), 1)
                dve.wait_ge(S("mod"), l + 1)
                for i, (c, g) in enumerate(((8, PC["nmix"]), (32, PC["nmlp"]))):
                    ins = stt(A1[2 * l + i], mod[:, l, c:c + KT], 1.0, par[:, g + 8 * l:g + 8 * l + 8], ADD, MUL)
                if l == 0:
                    ins = tt(gsc, mod[:, 0, 16:24], par[:, PB["psc"]:PB["psc"] + KT], MUL)
                V(ins)

            residual("eo")
            done(dve, "eo3")
            norm(1, lambda k: pc(PA["nw"] + KT + k))
            done(dve, "fp3")
            for b in range(HH):
                s = slice(b * T, (b + 1) * T)
                ts(hb[:, s], hb[:, s], oml[:, b:b + 1], lb[:, b:b + 1], MUL, ADD)
                ins = ts(hk[:, s], hk[:, s], oml[:, b:b + 1], None, MUL)
            ins.then_inc(S("hf"), 1)
            for j in range(4):
                tokens(f"iv{j}", ht[:, :, j * CW:(j + 1) * CW], 0, BI + j * CW, CW)
            dve.wait_ge(S("hln"), 1)
            dve.wait_ge(S("rst"), 2)
            V(dve.tensor_tensor_scan(hb, rst, hb2, 0.0, MUL, ADD))
            dve.wait_ge(S("AT0"), 1)

            def exponents(l):
                m = P >> (l + 1) if l < LEVELS else P
                if l >= 3:
                    got(dve, f"lv{l - 3}_3")
                b = hb.rearrange("p (n y t) -> p n y t", y=2, t=m)
                e = L3[l % 3].rearrange("p (n y t) -> p n y t", y=2, t=m)
                n = 2 * HH * P // (2 * m)
                ref = b[:, :, 0, m - 1:m].broadcast_to([P, n, m])
                tt(e[:, :, 0, :], ref, b[:, :, 0, :], SUB)
                if l < LEVELS:
                    ins = tt(e[:, :, 1, :], b[:, :, 1, :], ref, SUB)
                else:
                    ins = dve.tensor_copy(e[:, :, 1, :], b[:, :, 1, :])
                ins.then_inc(S("LE"), 1)

            def lmask(l):
                return K("lvl")[:, l * P:(l + 1) * P].bitcast(I32).unsqueeze(1).broadcast_to([P, 4, P])

            def pick(name, l, i):
                if l == LEVELS:
                    return free(dve.copy_predicated(ATm[:, 4 * i:4 * i + 4, :], lmask(l),
                                                    got(dve, name)[:, :].rearrange("p (n j) -> p n j", n=4)), name)
                done(dve, f"lv{l - 1}_{i}" if l else f"dg_{i}")
                free(dve.copy_predicated(ATm[:, 4 * i:4 * i + 4, :], lmask(l),
                                         got(dve, name)[:, :].rearrange("p (n j) -> p n j", n=4)), name)

            exponents(0)
            exponents(1)
            for i in range(4):
                pick(f"dg_{i}", LEVELS, i)
            exponents(2)
            for l in range(LEVELS):
                for i in range(4):
                    pick(f"lv{l}_{i}", l, i)
                if l + 3 <= LEVELS:
                    exponents(l + 3)
            for i in range(4):
                ahead(dve, f"or{i}")
            dve.wait_ge(S("so"), 1)
            done(dve, "hz3")
            for i in range(4):
                for h in (2 * i, 2 * i + 1):
                    s = slice(h * T, (h + 1) * T)
                    ins = stt(hO[:, s], hO[:, s], pc(PB["hhn"] + h), hR[:, s], MUL, MUL)
                V(ins)
                s = slice(i * 512, (i + 1) * 512)
                tt(hO[:, s], hO[:, s], hz[:, s], MUL).then_inc(S("yH"), 1)
            for i in range(4):
                parts(hO[:, i * 512:(i + 1) * 512], 2 * i)
            ahead(dve, "or3")
            modulation(0)
            residual("oo")
            done(dve, "oo3")
            norm(2, lambda k: A1[0][:, k:k + 1])
            dve.wait_ge(S("hh2"), 4)
            dve.wait_ge(S("zero"), 3)
            W = PADW + T
            V(tt(s2[:, :, 1:W], hT[:, :, 1:W], hT[:, :, 0:W - 1], ADD))
            V(tt(s4[:, 2:8, 3:W], s2[:, 2:8, 3:W], s2[:, 2:8, 1:W - 2], ADD))
            V(tt(s2[:, 4:8, 7:W], s4[:, 4:8, 7:W], s4[:, 4:8, 3:W - 4], ADD))
            V(tt(s4[:, 6:8, 15:W], s2[:, 6:8, 15:W], s2[:, 6:8, 7:W - 8], ADD))
            for g, win in enumerate(POOLS):
                s = (s2, s4)[g % 2][:, 2 * g:2 * g + 2, PADW:W]
                V(tt(s[:, :, 0:PADW], s[:, :, 0:PADW],
                     K("prc")[:, g * PADW:(g + 1) * PADW].unsqueeze(1).broadcast_to([P, 2, PADW]), MUL))
                stt(pl[:, 2 * g:2 * g + 2, :], s, 1.0 / win, hx[:, 2 * g:2 * g + 2, :], MUL, SUB)\
                    .then_inc(S("pl"), 1)
            residual("pw", lambda b: gsc[:, b:b + 1])
            done(dve, "pw3")

            def mlp(l):
                n = 3 + 2 * l
                norm(n, lambda k: A1[2 * l + 1][:, k:k + 1], (l, 24))
                for j in range(FF // CW):
                    i = 16 * l + j
                    o = got(dve, f"w1_{l}_{j}")
                    dve.wait_ge(S("relu"), i + 1)
                    if j >= 2:
                        dve.wait_ge(S("h1l"), i - 1)
                    free(stt(r2[j % 2], o[:, :], 0.0, rl[j % 2], MAX, MUL), f"w1_{l}_{j}")
                residual(f"w2_{l}_", lambda b: mod[:, l, 40 + b:41 + b])
                done(dve, f"w2_{l}_3")

            mlp(0)
            modulation(1)
            dve.wait_ge(S("ld_s"), 16 * DMAS["ld_s"])
            for i in range(2):
                free(tt(wsT[:, 4 * i:4 * i + 4, :], got(dve, f"ws{i}")[:, :].rearrange("p (h t) -> p h t", h=4),
                        K("tri").unsqueeze(1).broadcast_to([P, 4, P]), MUL), f"ws{i}")
            norm(4, lambda k: A1[2][:, k:k + 1], (1, 0))
            done(dve, "si7")
            V(dve.tensor_reduce(mu, vt, AX, ADD))
            V(ts(mu, mu, -1.0 / D, None, MUL))
            for a in range(NT):
                ts(xc[:, a, :], vt[:, a, :], mu[:, a:a + 1], None, ADD).then_inc(S("xc"), 1)
            ahead(dve, "si0")
            dve.wait_ge(S("vs"), 1)
            for a in range(NT):
                ins = stt(vt[:, a, :], xc[:, a, :], vr[:, a:a + 1], lng, MUL, MUL)
            V(ins)
            for a in range(NT):
                tt(vt[:, a, :], vt[:, a, :], lnb, ADD).then_inc(S("vln"), 1)
            done(dve, "si3")
            for i in range(4):
                t4 = xc.rearrange("p a n -> p (a n)")[:, i * 512:(i + 1) * 512]
                for j in range(2):
                    ins = tt(t4[:, j * T:(j + 1) * T].rearrange("p (a t) -> p a t", a=NT),
                             got(dve, f"mx{i}")[:, j * T:(j + 1) * T].rearrange("p (a t) -> p a t", a=NT),
                             bsb[:, 2 * i + j, :].unsqueeze(1).broadcast_to([P, NT, P]), ADD)
                free(ins, f"mx{i}")
                done(dve, f"mx{i}")
                tt(t4, t4, uT[:, 2 * i:2 * i + 2, :].rearrange("p b t -> p (b t)"), MUL).then_inc(S("yS"), 1)
                if i:
                    parts(xc.rearrange("p a n -> p (a n)")[:, (i - 1) * 512:i * 512], 2 * i - 2)
            parts(xc.rearrange("p a n -> p (a n)")[:, 3 * 512:], 6)
            residual("so", lambda b: mod[:, 1, 16 + b:17 + b])
            done(dve, "so3")
            mlp(1)
            norm(6, lambda k: pc(PB["fg"] + k))
            for i in (1, 3):
                free(dve.tensor_copy(ot[:, i // 2, (i % 2) * 512:(i % 2 + 1) * 512], got(dve, f"f{i}")[:, :]), f"f{i}")


DMAS = dict(ld_A=15, ld_B=7, ld_C=3, ld_b=7, ld_m=2, ld_s=4)

_INS = ["x", "norm_w", "ev_w_in", "ev_b_in", "mlstm_f_bias", "mlstm_conv_w", "mlstm_conv_b", "mlstm_head_norm",
        "nsa_q_norm", "nsa_k_norm", "cmp_k_pos", "cmp_k_w1", "cmp_k_w2", "cmp_v_pos", "cmp_v_w1", "cmp_v_w2",
        "ev_w_out", "od_w_in", "od_b_in", "hgrn_lb_logits", "hgrn_head_norm", "od_w_out", "c_2", "ada_w_2",
        "ada_b_2", "norm_mix_g_2", "norm_mlp_g_2", "pool_w_2", "pool_scale_2", "sgu_w_in_2", "sgu_ln_g_2",
        "sgu_ln_b_2", "sgu_w_s_2", "sgu_b_s_2", "sgu_w_out_2", "mlp_w1_2", "mlp_w2_2", "final_g_2"]


def kernel(**inputs):
    import numpy as _np
    import concourse.bacc as _bacc
    from concourse import mybir as _mybir
    from concourse.bass_utils import run_bass_kernel_spmd as _run

    nc = _bacc.Bacc("TRN2", target_bir_lowering=False, num_devices=1)
    arrays, aps = {}, {}
    for name in _INS:
        a = _np.ascontiguousarray(inputs[name])
        if a.ndim == 1:
            a = a.reshape(1, -1)
        arrays[f"in_{name}"] = a
        aps[name] = nc.dram_tensor(f"in_{name}", a.shape, _mybir.dt.from_np(a.dtype), kind="ExternalInput").ap()
    arrays["in_cst"] = constants()
    cst = nc.dram_tensor("in_cst", arrays["in_cst"].shape, _mybir.dt.float32, kind="ExternalInput").ap()
    out = nc.dram_tensor("out_0", (1, T, D), _mybir.dt.float32, kind="ExternalOutput").ap()
    build(nc, aps, cst, out)
    r = _run(nc, [arrays], core_ids=[0])
    return r.results[0]["out_0"]
```

```python
from contextlib import ExitStack

import concourse.bass as bass
from concourse import mybir

F32 = mybir.dt.float32
F32R = mybir.dt.float32r
I32 = mybir.dt.int32
ALU = mybir.AluOpType
ACT = mybir.ActivationFunctionType
AX = mybir.AxisListType.X

P = 128
T = 256
NT = T // P
D = 1024
KT = D // P
CW = 256
EPS = 1e-6
LN_EPS = 1e-5
NEG = -1e30

MH = 4
MW = MH * P
NH, NG, ND = 8, 2, 64
NR = NH // NG
NW_ = NH * ND
C_GATE = 5 * MW
C_NQ = C_GATE + 2 * MH
C_KV = C_NQ + NW_
C_GT = C_KV + 6 * NG * ND
C_NZ = C_GT + 3 * NH
NGATE = 2 * MH + 3 * NH
CMP_LEN, CMP_STRIDE = 32, 16
NCMP = (T - CMP_LEN) // CMP_STRIDE + 1
CPAD = 32
TAPS = 4
HH = 8
LEVELS = 7
FF = 4 * D
FT = FF // P
POOLS = (2, 4, 8, 16)
PADW = 16

_c = {}
_at = 0
for _n, _w in (("idn", P), ("one", P), ("mD", P), ("m64", P), ("row1", 2 * MH - 1), ("rowP", 2 * MH - 1),
               ("rowQ", 22), ("selQ", 6 * P), ("m1", T), ("mc", NT * NCMP), ("mc01", NT * NCMP),
               ("prm", P), ("cos", T), ("sin", T), ("tri", P), ("sel", MH * P), ("lvl", (LEVELS + 1) * P),
               ("prc", len(POOLS) * PADW), ("rg", 4)):
    _c[_n] = (_at, _at + _w)
    _at += _w
NCST = _at

PA = dict(nw=0, b20=16, bnq=36, bkv=40, bnz=46, cvb=50, mhn=58, qn=62, kn=63, kpos=66, vpos=82)
NA_ROWS = 98
PB = dict(cvw=128, odb=160, lbl=192, hhn=208, fg=216, c=224, psc=232)
NB_ROWS = 112
PC = dict(adab=256, nmix=352, nmlp=368)
NC_ROWS = 128

HK = KT // 2
HN = HK * CW
NF = 4
NS = 4
NA = 2
AG = 512
PIECES = ((0, 1), (1, 2), (2, 4), (4, 6), (6, 8))
LK0 = 5
NBANK = 7


def constants():
    import numpy as np
    c = np.zeros((P, NCST), np.float32)

    def put(name, a):
        lo, hi = _c[name]
        c[: a.shape[0], lo:hi] = a.reshape(a.shape[0], hi - lo)

    i = np.arange(P)
    put("idn", np.eye(P, dtype=np.float32))
    put("one", np.ones((P, P), np.float32))
    put("mD", np.full((P, P), 1 / D, np.float32))
    put("m64", (i[:, None] // ND == i[None] // ND).astype(np.float32) / ND)
    for n, v in (("row1", 1.0), ("rowP", 1 / P)):
        a = np.zeros((P, 2 * MH - 1), np.float32)
        a[:, MH - 1] = v
        put(n, a)
    a = np.zeros((P, 22), np.float32)
    a[:ND, 10] = a[ND:, 11] = 1 / ND
    put("rowQ", a)
    a = np.zeros((12, 6, NG, ND), np.float32)
    for b in range(6):
        for g in range(NG):
            a[2 * b + g, b, g] = 1.0
    put("selQ", a)
    tri = np.where(i[None] <= i[:, None], 0.0, NEG).astype(np.float32)
    put("m1", np.concatenate([np.zeros((P, P), np.float32), tri], 1))
    t = np.arange(T).reshape(NT, P).T
    ok = (np.arange(NCMP) * CMP_STRIDE + CMP_LEN - 1)[None, None] <= t[:, :, None]
    put("mc", np.where(ok, 0.0, NEG).astype(np.float32))
    put("mc01", ok.astype(np.float32))
    half = ND // 8
    prm = np.zeros((P, P), np.float32)
    for g in range(NG):
        for d in range(half):
            prm[g * ND + d + half, g * ND + d] = -1.0
            prm[g * ND + d, g * ND + d + half] = 1.0
    put("prm", prm)
    inv = (np.float32(500000.0) ** (-np.arange(half, dtype=np.float32) / half)).astype(np.float32)
    ang = np.arange(T, dtype=np.float32)[None] * inv[:, None]
    cos, sin = np.ones((P, T), np.float32), np.zeros((P, T), np.float32)
    for g in range(NG):
        for h in range(2):
            at = g * ND + h * half
            cos[at:at + half], sin[at:at + half] = np.cos(ang), np.sin(ang)
    put("cos", cos)
    put("sin", sin)
    put("tri", (i[:, None] <= i[None]).astype(np.float32))
    sel = np.zeros((MH, MH, P), np.float32)
    for h in range(MH):
        sel[h, h] = 1.0
    put("sel", sel)
    lv = []
    for l in range(LEVELS):
        m = P >> (l + 1)
        s, j = i[:, None], i[None]
        lv.append(((s // (2 * m) == j // (2 * m)) & (s % (2 * m) < m) & (j % (2 * m) >= m)).astype(np.float32))
    lv.append(np.eye(P, dtype=np.float32))
    put("lvl", np.stack(lv, 1))
    pr = np.zeros((P, len(POOLS), PADW), np.float32)
    for g, w in enumerate(POOLS):
        pr[:, g] = w / np.minimum(np.arange(PADW) + 1.0, w)
    put("prc", pr)
    put("rg", (i[:, None] // CPAD == np.arange(4)[None]).astype(np.float32))
    return c


def weight_chunks(A):
    out = []
    allp = slice(0, P)

    def rows(w, h, c0, n, r0=0):
        return w[r0 + h * HK * P:r0 + (h + 1) * HK * P, c0:c0 + n].rearrange("(k p) n -> p k n", p=P)

    def cols(name, w, c0, r0=0):
        out.append((name, True, [[(allp, slice(0, HK), slice(0, CW), rows(w, h, c0, CW, r0))] for h in range(2)]))

    w = A["ev_w_in"][0]

    def paired(n, c0):
        for j in range(2):
            hs = []
            for h in range(2):
                parts = []
                for b in range(2):
                    for g in range(NG):
                        parts.append((allp, slice(0, HK), slice(b * P + g * ND, b * P + g * ND + ND),
                                      rows(w, h, c0 + (g * NR + 2 * j + b) * ND, ND)))
                hs.append(parts)
            out.append((f"{n}{j}", True, hs))

    def plain(n, c0):
        for j in range(2):
            cols(f"{n}{j}", w, c0 + j * CW)

    out.append(("gt", True, [[(allp, slice(0, HK), slice(0, 2 * MH), rows(w, h, C_GATE, 2 * MH)),
                              (allp, slice(0, HK), slice(2 * MH, NGATE), rows(w, h, C_GT, 3 * NH))]
                             for h in range(2)]))
    plain("q", 0)
    plain("k", MW)
    paired("nq", C_NQ)
    cols("ksvs", w, C_KV + CW)
    cols("kwvw", w, C_KV + 2 * CW)
    cols("kcvc", w, C_KV)
    plain("v", 2 * MW)
    for n in ("cmp_k_w1", "cmp_v_w1"):
        out.append((n, False, [[(allp, slice(0, 2 * HK), slice(0, P),
                                 A[n][0][h * 8 * P:(h + 1) * 8 * P, :].rearrange("(m p) n -> p m n", p=P))]
                               for h in range(2)]))
    plain("o", 3 * MW)
    plain("z", 4 * MW)
    paired("nz", C_NZ)
    wo = A["ev_w_out"][0]
    for j in range(4):
        low = [(slice(g * ND, (g + 1) * ND), slice(0, HK), slice(0, CW),
                wo[MW + g * NR * ND:MW + (g + 1) * NR * ND, j * CW:(j + 1) * CW].rearrange("(b d) n -> d b n", d=ND))
               for g in range(NG)]
        out.append((f"eo{j}", True, [[(allp, slice(0, HK), slice(0, CW), rows(wo, 0, j * CW, CW))], low]))
    wi = A["od_w_in"][0]
    for n, c0 in (("fp", 0), ("qp", 2 * D), ("iv", D), ("hz", 3 * D)):
        for j in range(4):
            cols(f"{n}{j}", wi, c0 + j * CW)
    for j in range(4):
        cols(f"oo{j}", A["od_w_out"][0], j * CW)
    out.append(("pool", False, [[(allp, slice(0, HK), slice(0, CW),
                                  A["pool_w_2"][0][2 * h:2 * h + 2].rearrange("g (k p) n -> p (g k) n", p=P))]
                                for h in range(2)]))

    def mlp(l):
        for j in range(FF // CW):
            cols(f"w1_{l}_{j}", A["mlp_w1_2"][l], j * CW)
        for j in range(4):
            for k in range(4):
                cols(f"w2_{l}_{j}_{k}", A["mlp_w2_2"][l], j * CW, r0=k * D)

    mlp(0)
    for j in (4, 5, 6, 7, 0, 1, 2, 3):
        cols(f"si{j}", A["sgu_w_in_2"][0], j * CW)
    for j in range(4):
        cols(f"so{j}", A["sgu_w_out_2"][0], j * CW)
    mlp(1)
    return out


def stream(A):
    chunks = weight_chunks(A)
    spread = {}

    def give(names, l, n):
        for i, name in enumerate(names):
            k = (i + 1) * n // len(names) - i * n // len(names)
            if k:
                spread.setdefault(name, []).append((l, k))

    def named(*starts):
        return [n for n, _, _ in chunks if n.startswith(starts)]

    give([n for n, _, _ in chunks[1:22] if not n.startswith("cmp")][:16], 0, 16)
    give(named("fp", "qp", "iv", "hz")[:15], 0, 24)
    give(named("w1_0")[:8], 0, 8)
    give(named("w1_0")[8:], 1, 12)
    give(named("w2_0")[:14], 1, 12)
    give(named("si", "so")[:10], 1, 16)
    give(named("w1_1")[:12], 1, 8)
    out, at, s = [], [0, 0], 0
    for name, split, halves in chunks:
        for h, parts in enumerate(halves):
            out.append(("w", dict(i=s, name=name, split=split, parts=parts)))
            s += 1
        for l, n in spread.get(name, ()):
            for _ in range(n):
                out.append(("a", (l, at[l] // 4, at[l] % 4)))
                at[l] += 1
    n = 4 * 6 * D // AG
    assert at == [n, n], at
    return chunks, out


def build(nc, A, cst_dram, out_dram):
    ctx = ExitStack()
    with ctx:
        sems = {}

        def S(name):
            if name not in sems:
                sems[name] = ctx.enter_context(nc.semaphore("s_" + name))
            return sems[name]

        def sb(name, shape, dt=F32):
            return ctx.enter_context(nc.sbuf_tensor(name, shape, dt))

        cst = sb("cst", [P, NCST])
        par = sb("par", [P, 384])
        xT = sb("xT", [P, KT, T])
        hT = sb("hT", [P, KT, PADW + T])
        hh = sb("hh", [P, KT, T], F32R)
        hl = sb("hl", [P, KT, T], F32R)
        wf = sb("wf", [P, NF, HN])
        wh = sb("wh", [P, NS, HN], F32R)
        wl = sb("wl", [P, NS, HN], F32R)
        wa = sb("wa", [P, NA, 2 * AG])
        acc = sb("acc", [P, 2, AG])
        bcb = sb("bcb", [P, 512 + 128 + 128 + 32 + 4 + 1024])
        sm = sb("sm", [P, 1024])
        mod = sb("mod", [P, 2, 48])
        rstd = sb("rstd", [P, T])[:, :]
        AR = 20640
        with nc.sbuf_tensor("ar", [P, AR], F32) as ar:
            pass
        h1s = [sb(f"h1{n}", [P, FT * T], F32R) for n in "hl"]
        ps = [ctx.enter_context(nc.psum_tensor(f"ps{i}", [P, 512], F32)) for i in range(NBANK)]
        adaps = ctx.enter_context(nc.psum_tensor("adaps", [P, 512], F32))

        def K(name):
            lo, hi = _c[name]
            return cst[:, lo:hi]

        idn, one = K("idn"), K("one")
        hx = hT[:, :, PADW:PADW + T]
        sq = hT[:, :, :].rearrange("p b t -> p (b t)")[:, 0:KT * T]

        def cut(at, size, pat=None, **kw):
            v = ar[:, at:at + size]
            return v.rearrange(pat, **kw) if pat else v

        qkp = cut(0, 8 * 259, "p (b t) -> p b t", t=259)
        qkc = cut(2072, 2048, "p (b t) -> p b t", t=T)
        vtok = cut(4120, 1024, "p (a n) -> p a n", a=NT)
        ET = cut(5144, 1536, "p (h n) -> p h n", h=MH)
        ST = cut(6680, 1536, "p (h n) -> p h n", h=MH)
        denb = cut(8216, 1024)
        hm = cut(9240, 1024)
        P1 = cut(0, 4096, "p (h y k) -> p h y k", h=NH, y=2)
        P0 = cut(4096, 2048, "p (h y k) -> p h y k", h=NH, y=2)
        Pc = cut(6144, 512, "p (a h n) -> p a h n", a=NT, h=NH)
        PT1 = cut(6656, 4096, "p (h y k) -> p h y k", h=NH, y=4)
        PT0 = cut(10752, 2048, "p (h y k) -> p h y k", h=NH, y=2)
        PTc = cut(12800, 512, "p (a g k) -> p a g k", a=NT, g=NG)
        XK = cut(9240, 512, "p (g t) -> p g t", g=NG)
        XV = cut(9752, 512, "p (g t) -> p g t", g=NG)
        kcvc = cut(10264, 512, "p (y t) -> p y t", y=2)
        CR = cut(10776, 960, "p (y m g n) -> p y m g n", y=2, m=16, g=NG)
        irow, frow, brow, arow, erow, trow = [ar[0:MH, 11736 + i * T:11736 + (i + 1) * T] for i in range(6)]
        ifrow = ar[0:MH, 11736:11736 + 2 * T]
        grow, orow = irow, frow
        drow, hrow = brow, arow
        at = 13312
        og = cut(at, 1024); at += 1024
        zg = cut(at, 1024); at += 1024
        nz = cut(at, 1024); at += 1024
        R = cut(at, 1536 + NCMP); at += 1552
        R2 = cut(at, 1536 + NCMP); at += 1552
        vsw = cut(at, 512, "p (y a n) -> p y a n", y=2, a=NT); at += 512
        VC = cut(at, P); at += P
        VC4 = cut(at, 4 * P, "p (i d) -> p i d", i=4); at += 4 * P
        assert at <= AR, at
        hb = cut(0, 2048)
        hk = cut(2048, 2048)
        hq = cut(4096, 2048)
        hz = cut(6144, 2048)
        ht = cut(8192, 2048, "p (a n) -> p a n", a=NT)
        L3 = [cut(10240, 2048), cut(12288, 2048), cut(14336, 2048)]
        ATm = cut(16384, 2048, "p (n j) -> p n j", n=2 * HH)
        AT2 = cut(18432, 1024, "p (h j) -> p h j", h=HH)
        hb2 = L3[0]
        rst = L3[1]
        hO = L3[0]
        h1h, h1l = [t[:, :].rearrange("p (f t) -> p f t", t=T) for t in h1s]
        rl = [sq[:, 0:512], sq[:, 512:1024]]
        r2 = [sq[:, 1024:1536], sq[:, 1536:2048]]
        lng = bcb[:, 804:804 + D]
        lnb = cut(16384, 1024)
        bsb = cut(17408, 1024, "p (h t) -> p h t", h=8)
        wsT = cut(18432, 1024, "p (h t) -> p h t", h=8)
        wst = K("lvl").rearrange("p (h t) -> p h t", h=8)
        uT = cut(0, 2048, "p (b t) -> p b t", t=T)
        vt = cut(2048, 2048, "p (a n) -> p a n", a=NT)
        xc = cut(4096, 2048, "p (a n) -> p a n", a=NT)
        s2 = cut(0, 8 * 272, "p (b t) -> p b t", t=272)
        s4 = cut(2176, 8 * 272, "p (b t) -> p b t", t=272)
        pl = cut(4352, 2048, "p (b t) -> p b t", t=T)
        ot = cut(0, 2048, "p (a n) -> p a n", a=NT)
        xtok = cut(0, 2048, "p (a n) -> p a n", a=NT)
        rows = [cut(2048 + i * P, P) for i in range(3)]

        smat = [0]

        def small(n):
            smat[0] += n
            assert smat[0] <= 1024
            return sm[:, smat[0] - n:smat[0]]

        gt = small(NT * NGATE).rearrange("p (a n) -> p a n", a=NT)
        acol = small(NT * MH).rearrange("p (a n) -> p a n", a=NT)
        cs = small(KT)
        mx1, mx0, mxc = small(16), small(16), small(16)
        sm1, sm0, smc = small(16), small(16), small(16)
        hk_ = small(NG * NCMP + 2)
        hv_ = small(NG * NCMP + 2)
        hvp = small(NG * 4 * CPAD)
        w2k, w2v = small(ND), small(ND)
        lb, lbt, oml, nodb = small(HH), small(HH), small(HH), small(HH)
        A1 = [small(KT), small(KT), small(KT), small(KT)]
        gsc = small(KT)
        early = small(1)
        qrow = small(T)[0:12, :]
        oroot = ar[0:MH, 19456:19456 + 2 * T]
        mu, vr = small(NT), small(NT)

        chunks, items = stream(A)
        halves = [x for kind, x in items if kind == "w"]
        splits = [x for x in halves if x["split"]]
        chunk_at = {name: i for i, (name, _, _) in enumerate(chunks)}
        landed = [0] * NF
        for x in halves:
            x["slot"] = x["i"] % NF
            landed[x["slot"]] += 16 * len(x["parts"])
            x["landed"] = landed[x["slot"]]
        for n, x in enumerate(splits):
            x["n"], x["sslot"] = n, n % NS
            x["low"] = ("P", "V")[n % 2]
            x["low_n"] = n // 2 + 1
        released = {}
        place = {}
        horizon = {}
        fills = [0] * NBANK
        count = dict(unit=0, chunk=0, half=0, mid=0)

        def wf_free(x):
            return (S("wl" + x["low"]), x["low_n"]) if x["split"] else released[x["i"]]

        def loaded(x, *tiles):
            n = NGATE if x["name"] == "gt" else CW
            return [t.rearrange("p (k n) -> p k n", n=CW)[:, :, 0:n] for t in tiles]

        def high(eng, x):
            eng.wait_ge(S(f"w{x['slot']}"), x["landed"])
            if x["n"] >= NS:
                eng.wait_ge(*released[splits[x["n"] - NS]["i"]])
            h, f = loaded(x, wh[:, x["sslot"], :], wf[:, x["slot"], :])
            eng.activation(h, f, ACT.Copy).then_inc(S("wh"), 1)

        def low(eng, x):
            eng.wait_ge(S("wh"), x["n"] + 1)
            l, f, h = loaded(x, wl[:, x["sslot"], :], wf[:, x["slot"], :], wh[:, x["sslot"], :])
            eng.tensor_tensor(l, f, h, ALU.subtract).then_inc(S("wl" + x["low"]), 1)

        groups, c = [], 0
        for kind, x in items:
            if kind == "w":
                c = x["i"] // 2
            elif x[2] == 3:
                groups.append((x[0], x[1], c))
        STAGES = [(0, 0, 40), (0, 40, 48), (1, 0, 24), (1, 24, 40), (1, 40, 48)]
        progress = dict(A=0, P=0, V=0)
        passed = dict(A=0, P=0, V=0)
        steps = [0]

        def modulation_step(eng, l, g, q):
            n = steps[0]
            steps[0] += 1
            a = acc[:, g % 2, :]
            eng.wait_ge(S(f"la{n % NA}"), 16 * (n // NA + 1))
            if n == 0:
                eng.wait_ge(S("cs"), 1)
            if q == 0 and n >= 8:
                eng.wait_ge(S("ada"), n // 4 - 1)
            if n:
                eng.wait_ge(S("wa"), n)
            w = wa[:, n % NA, :].rearrange("p (k n) -> p k n", n=AG)
            if q == 0:
                ins = eng.tensor_scalar(a, w[:, 0, :], cs[:, 0:1], None, ALU.mult)
            else:
                ins = eng.scalar_tensor_tensor(a, w[:, 0, :], cs[:, 2 * q:2 * q + 1], a, ALU.mult, ALU.add)
            ins.then_inc(S("wa_first"), 1)
            eng.wait_ge(S("wa_first"), n + 1)
            eng.scalar_tensor_tensor(a, w[:, 1, :], cs[:, 2 * q + 1:2 * q + 2], a, ALU.mult,
                                     ALU.add).then_inc(S("wa"), 1)

        def keep(who, eng, name):
            n = horizon[name]
            while progress[who] < len(items):
                kind, x = items[progress[who]]
                if kind == "w":
                    if x["i"] >= n:
                        break
                    if x["split"] and who == "A":
                        high(eng, x)
                    elif x["split"] and who == x["low"]:
                        low(eng, x)
                elif who == "V":
                    if passed[who] >= n:
                        break
                    modulation_step(eng, *x)
                if kind == "w":
                    passed[who] = x["i"] + 1
                progress[who] += 1

        def got(eng, name):
            ahead(eng, name)
            b, n = place[name]
            eng.wait_ge(S(f"full{b}"), n)
            return ps[b]

        def free(ins, name):
            ins.then_inc(S(f"free{place[name][0]}"), 1)

        def done(eng, name):
            ahead(eng, name)
            b, n = place[name]
            eng.wait_ge(S(f"free{b}"), n)

        def pool_group(g, eng, step):
            win, W = POOLS[g], PADW + T
            eng.wait_ge(S("hh2"), g + 2)
            b = slice(2 * g, 2 * g + 2)
            src, dst, span = hT, s2, 1
            while span < win:
                at = 2 * span - 1
                step(eng.tensor_tensor(dst[:, b, at:W], src[:, b, at:W], src[:, b, at - span:W - span], ALU.add))
                src, dst, span = dst, (s4 if dst is s2 else s2), 2 * span
            s = src[:, b, PADW:W]
            step(eng.tensor_tensor(s[:, :, 0:PADW], s[:, :, 0:PADW],
                                   K("prc")[:, g * PADW:(g + 1) * PADW].unsqueeze(1).broadcast_to([P, 2, PADW]),
                                   ALU.mult))
            step(eng.tensor_scalar(s, s, 1.0 / win, None, ALU.mult))
            return eng.tensor_tensor(pl[:, b, :], s, hx[:, b, :], ALU.subtract)

        ahead_of = {}

        def ahead(eng, name):
            for e, f in ahead_of.values():
                if e is eng:
                    f(name)

        block = ctx.enter_context(nc.Block())

        @block.tensor
        def _(pe):
            def begin(name, n=1):
                b = count["unit"] % NBANK
                count["unit"] += 1
                if fills[b]:
                    pe.wait_ge(S(f"free{b}"), fills[b])
                fills[b] += 1
                place[name] = (b, fills[b])
                horizon[name] = 2 * (count["chunk"] + n - 1) + NS if n else 0
                if name[:2] in ("ss", "ws", "mx", "or", "ob"):
                    horizon[name] -= 2
                return ps[b]

            def end(ins, name):
                ins.then_inc(S(f"full{place[name][0]}"), 1)

            mm = pe.matmul

            def chunk(name, product, last, k_tiles=HK, w=CW, first=None):
                assert chunk_at[name] == count["chunk"], name
                modulations(count["chunk"] - 1)
                count["chunk"] += 1
                for h in range(2):
                    x = halves[2 * chunk_at[name] + h]
                    if x["split"]:
                        pe.wait_ge(S("wl" + x["low"]), x["low_n"])
                        hi = wh[:, x["sslot"], :].rearrange("p (k n) -> p k n", n=w)
                        lo = wl[:, x["sslot"], :].rearrange("p (k n) -> p k n", n=w)
                    else:
                        pe.wait_ge(S(f"w{x['slot']}"), x["landed"])
                        hi = lo = wf[:, x["slot"], :].rearrange("p (k n) -> p k n", n=w)
                    for k in range(k_tiles):
                        ins = product(hi[:, k, :], lo[:, k, :], h * k_tiles + k)
                    if h == 0 and first:
                        released[x["i"]] = (S(f"full{place[first][0]}"), place[first][1])
                    elif h == 0:
                        ins.then_inc(S("half"), 1)
                        count["half"] += 1
                        released[x["i"]] = (S("half"), count["half"])
                    elif last:
                        released[x["i"]] = (S(f"full{place[last][0]}"), place[last][1])
                    else:
                        ins.then_inc(S("mid"), 1)
                        count["mid"] += 1
                        released[x["i"]] = (S("mid"), count["mid"])
                return ins

            def three(o, wa_, wb_, xa_, xb_, first, last):
                mm(o, wa_, xa_, start=first, stop=False, skip_group_check=True)
                mm(o, wa_, xb_, start=False, stop=False, skip_group_check=True)
                return mm(o, wb_, xa_, start=False, stop=last, skip_group_check=True)

            def operand(sem, at, k):
                if at is None:
                    n = [i for i, (lo, _) in enumerate(PIECES) if lo == k]
                    if n:
                        pe.wait_ge(sem, n[0] + 1)
                elif k % 2 == 0:
                    pe.wait_ge(sem, at + k // 2 + 1)

            def feat(name, sem=None, at=None):
                o = begin(name)

                def product(hi, lo, k):
                    if sem:
                        operand(sem, at, k)
                    for j in range(2):
                        c = slice(j * P, (j + 1) * P)
                        ins = three(o[:, j * T:(j + 1) * T], hi[:, c], lo[:, c], hh[:, k, :], hl[:, k, :],
                                    k == 0 and j == 0, k == KT - 1)
                    return ins

                end(chunk(name, product, name), name)

            def tok(name, c0=0, n=CW, sem=None):
                o = begin(name)

                def product(hi, lo, k):
                    if sem:
                        operand(sem, None, k)
                    for a in range(NT):
                        t = slice(a * P, (a + 1) * P)
                        ins = three(o[:, a * n:(a + 1) * n], hh[:, k, t], hl[:, k, t], hi[:, c0:c0 + n],
                                    lo[:, c0:c0 + n], k == 0 and a == 0, k == KT - 1)
                    return ins

                end(chunk(name, product, name), name)

            def keys_values(name):
                o = begin(name)

                def product(hi, lo, k):
                    three(o[:, 0:T], hi[:, 0:P], lo[:, 0:P], hh[:, k, :], hl[:, k, :], k == 0, k == KT - 1)
                    for a in range(NT):
                        t = slice(a * P, (a + 1) * P)
                        ins = three(o[:, T + a * P:T + (a + 1) * P], hh[:, k, t], hl[:, k, t], hi[:, P:2 * P],
                                    lo[:, P:2 * P], False, k == KT - 1)
                    return ins

                end(chunk(name, product, name), name)

            def sumsq(n):
                o = begin(f"ss{n}")
                for k in range(KT):
                    if k % 2 == 0:
                        pe.wait_ge(S("sq"), 4 * n + k // 2 + 1)
                    ins = mm(o[:, 0:T], K("mD"), sq[:, k * T:(k + 1) * T], start=(k == 0), stop=(k == KT - 1))
                end(ins, f"ss{n}")
                modulations(count["chunk"])

            def ada(l, g):
                stage = [k for k, (n, c, _) in enumerate(STAGES) if (n, c) == (l, 4 * g)]
                if stage and stage[0]:
                    pe.wait_ge(S("mod"), stage[0])
                pe.wait_ge(S("wa"), 4 * (12 * l + g + 1))
                for i in range(AG // P):
                    c = l * 48 + g * (AG // P) + i
                    ins = mm(adaps[:, c:c + 1], acc[:, g % 2, i * P:(i + 1) * P], one[:, 0:1], start=True, stop=True)
                ins.then_inc(S("ada"), 1)

            def modulations(n):
                while groups and groups[0][2] < n:
                    ada(*groups.pop(0)[:2])

            pe.wait_ge(S("ld_cst0"), 16)
            pe.wait_ge(S("ld_x"), 32)
            for i in range(4):
                o = begin(f"x{i}", 0)
                for k in range(4):
                    f = 4 * (i % 2) + k
                    ins = pe.transpose(o[:, k * P:(k + 1) * P], xtok[:, i // 2, f * P:(f + 1) * P], idn)
                end(ins, f"x{i}")

            def vectors(i, sem, n):
                pe.wait_ge(S(sem), 16 * DMAS[sem])
                o = begin(f"par{i}", i and 1)
                end(pe.transpose(o[:, 0:n], rows[i][0:n, :], idn[0:n, 0:n]), f"par{i}")

            vectors(0, "ld_A", NA_ROWS)
            sumsq(0)
            vectors(1, "ld_B", NB_ROWS)
            vectors(2, "ld_C", NC_ROWS)

            tok("gt", 0, NGATE, S("hp0"))
            for n in ("q0", "q1", "k0", "k1"):
                feat(n)
            pe.wait_ge(S("gt"), 1)
            o = begin("gtT")
            for y in range(2):
                for a in range(NT):
                    c = (y * NT + a) * P
                    ins = pe.transpose(o[0:MH, c:c + P], gt[:, a, y * MH:(y + 1) * MH], idn)
            end(ins, "gtT")
            feat("nq0")
            feat("nq1")
            keys_values("ksvs")
            keys_values("kwvw")
            pe.wait_ge(S("arow"), 1)
            o = begin("aT")
            for a in range(NT):
                ins = pe.transpose(o[:, a * MH:(a + 1) * MH], arow[:, a * P:(a + 1) * P], idn[0:MH, 0:MH])
            end(ins, "aT")

            def spread_rows(nm, row, sem):
                pe.wait_ge(S("ld_cst"), 16)
                pe.wait_ge(S(sem), 1)
                for i in range(2):
                    o = begin(f"{nm}{i}")
                    for j in range(2):
                        h = 2 * i + j
                        ins = mm(o[:, j * T:(j + 1) * T], K("sel")[0:MH, h * P:(h + 1) * P], row, start=True, stop=True)
                    end(ins, f"{nm}{i}")

            spread_rows("gb", grow, "grow")
            feat("kcvc")
            tok("v0")
            pe.wait_ge(S("sqR"), 1)
            o = begin("rs")
            for b in range(6):
                ins = mm(o[0:12, 0:T], K("rowQ")[:, 10 - 2 * b:22 - 2 * b], sq[:, b * T:(b + 1) * T],
                         start=(b == 0), stop=(b == 5))
            end(ins, "rs")
            tok("v1")
            pe.wait_ge(S("qrow"), 1)
            for i in range(3):
                o = begin(f"rb{i}")
                for j in range(2):
                    b = 2 * i + j
                    ins = mm(o[:, j * T:(j + 1) * T], K("selQ")[0:12, b * P:(b + 1) * P], qrow, start=True, stop=True)
                end(ins, f"rb{i}")
            pe.wait_ge(S("qkc"), 1)
            for h in range(MH):
                o = begin(f"st{h}")
                mm(o[:, 0:T], qkc[:, MH + h, 0:P], qkc[:, h, :], start=True, stop=True)
                ins = mm(o[:, T:T + P], qkc[:, MH + h, P:T], qkc[:, h, P:T], start=True, stop=True)
                end(ins, f"st{h}")
            o = begin("hid")
            pe.wait_ge(S("CR"), 8)
            for y, n in enumerate(("cmp_k_w1", "cmp_v_w1")):
                def product(w, _, m):
                    return mm(o[:, y * 32:y * 32 + 2 * NCMP], w, CR[:, y, m, :, :], start=(m == 0), stop=(m == 15))

                ins = chunk(n, product, "hid" if y else None, 2 * HK, P)
            end(ins, "hid")
            feat("o0")
            done(pe, "v1")
            done(pe, "st3")
            o = begin("dn")
            for h in range(MH):
                w = K("row1")[:, MH - 1 - h:2 * MH - 1 - h]
                mm(o[0:MH, 0:T], w, ST[:, h, 0:T], start=(h == 0), stop=False, skip_group_check=True)
                ins = mm(o[0:MH, P:T], w, ST[:, h, T:T + P], start=False, stop=(h == MH - 1), skip_group_check=True)
            end(ins, "dn")
            o = begin("cmp2")
            pe.wait_ge(S("ld_m"), 16 * DMAS["ld_m"])
            done(pe, "hid")
            for g in range(NG):
                mm(o[g * ND:(g + 1) * ND, 0:NCMP], w2k, hk_[:, g * NCMP:(g + 1) * NCMP], start=True, stop=True)
            pe.wait_ge(S("hvp"), 1)
            for g in range(NG):
                ins = mm(o[:, 64 + g * ND:64 + (g + 1) * ND], hvp[:, g * P:(g + 1) * P], w2v, start=True, stop=True)
            end(ins, "cmp2")
            for i in range(3):
                done(pe, f"rb{i}")
            for i in range(3):
                o = begin(f"pr{i}")
                end(mm(o[:, :], K("prm"), R2[:, i * 512:(i + 1) * 512], start=True, stop=True), f"pr{i}")
            feat("o1")
            pe.wait_ge(S("sqc"), 1)
            o = begin("rsc")
            end(mm(o[:, 0:NCMP], K("m64"), sq[:, 1536:1536 + NCMP], start=True, stop=True), "rsc")
            spread_rows("dr", drow, "drow")
            for i in range(2):
                o = begin(f"nm{i}")
                for j in range(2):
                    h = 2 * i + j
                    mm(o[:, j * T:(j + 1) * T], vtok[:, 0, h * P:(h + 1) * P], ST[:, h, 0:T], start=True, stop=True)
                    ins = mm(o[:, j * T + P:(j + 1) * T], vtok[:, 1, h * P:(h + 1) * P], ST[:, h, T:T + P],
                             start=False, stop=True, skip_group_check=True)
                end(ins, f"nm{i}")
            feat("z0")
            pe.wait_ge(S("sqh"), 1)
            o = begin("hr")
            for h in range(MH):
                ins = mm(o[0:MH, 0:T], K("rowP")[:, MH - 1 - h:2 * MH - 1 - h], sq[:, h * T:(h + 1) * T],
                         start=(h == 0), stop=(h == MH - 1))
            end(ins, "hr")
            pe.wait_ge(S("Rnc"), 1)
            o = begin("prc")
            end(mm(o[:, 0:NCMP], K("prm"), R2[:, 1536:1536 + NCMP], start=True, stop=True), "prc")
            pe.wait_ge(S("rope"), 1)
            for i in range(4):
                o = begin(f"s0_{i}")
                for j in range(2):
                    hd = 2 * i + j
                    g, b = hd // NR, hd % NR
                    gs = slice(g * ND, (g + 1) * ND)
                    for y in range(2):
                        c = (2 * j + y) * P
                        ins = mm(o[:, c:c + P], R[gs, b * T:b * T + P], R[gs, (4 + y) * T:(4 + y) * T + P],
                                 start=True, stop=True)
                end(ins, f"s0_{i}")
            pe.wait_ge(S("ropec"), 1)
            for g in range(NG):
                o = begin(f"sc{g}")
                gs = slice(g * ND, (g + 1) * ND)
                for a in range(NT):
                    for b in range(NR):
                        c = (a * NR + b) * NCMP
                        ins = mm(o[:, c:c + NCMP], R[gs, b * T + a * P:b * T + (a + 1) * P], R[gs, 1536:1536 + NCMP],
                                 start=True, stop=True)
                end(ins, f"sc{g}")
            for hd in range(NH):
                g, b = hd // NR, hd % NR
                gs = slice(g * ND, (g + 1) * ND)
                o = begin(f"s1_{hd}")
                for y in range(2):
                    ins = mm(o[:, y * T:(y + 1) * T], R[gs, b * T + P:b * T + T], R[gs, (4 + y) * T:(5 + y) * T],
                             start=True, stop=True)
                end(ins, f"s1_{hd}")
            feat("z1")
            spread_rows("hb", hrow, "hrow")
            feat("nz0")
            feat("nz1")
            pe.wait_ge(S("P0"), 1)
            for i in range(4):
                o = begin(f"t0_{i}")
                for j in range(4):
                    ins = pe.transpose(o[:, j * P:(j + 1) * P], P0[:, 2 * i + j // 2, j % 2, :], idn)
                end(ins, f"t0_{i}")
            pe.wait_ge(S("Pc"), 1)
            o = begin("tc")
            for j in range(4):
                ins = pe.transpose(o[:, j * P:(j + 1) * P],
                                   Pc[:, j // 2, 4 * (j % 2):4 * (j % 2) + 4, :].rearrange("p h n -> p (h n)"), idn)
            end(ins, "tc")
            for hd in range(NH):
                if hd % 4 == 0:
                    pe.wait_ge(S("P1"), hd // 4 + 1)
                o = begin(f"t1_{hd}")
                for j in range(4):
                    ins = pe.transpose(o[:, j * P:(j + 1) * P], P1[:, hd, j // 2, (j % 2) * P:(j % 2 + 1) * P], idn)
                end(ins, f"t1_{hd}")
            done(pe, "kwvw")
            pe.wait_ge(S("VC4"), 1)
            for n in [f"t0_{i}" for i in range(4)] + ["tc"] + [f"t1_{i}" for i in range(NH)]:
                done(pe, n)
            for i in range(2):
                o = begin(f"av{i}")
                for j in range(2):
                    b = 2 * i + j
                    for g in range(NG):
                        hd = g * NR + b
                        gs = slice(g * ND, (g + 1) * ND)
                        for a in range(NT):
                            dst = o[gs, j * T + a * P:j * T + (a + 1) * P]
                            for y in range(2):
                                for s in range(a + 1):
                                    pt = PT0[:, hd, y, :] if a == 0 else PT1[:, hd, 2 * y + s, :]
                                    mm(dst, vsw[:, y, s, gs], pt, start=(y == 0 and s == 0), stop=False)
                            ins = mm(dst, VC4[:, hd % 4, gs], PTc[:, a, g, :], start=False, stop=True)
                end(ins, f"av{i}")
            for j in range(4):
                feat(f"eo{j}", S("yp"), 0)

            sumsq(1)
            for n, f in (("fp", feat), ("qp", feat)):
                for j in range(4):
                    f(f"{n}{j}", S("hp1") if n == "fp" and j == 0 else None)

            def level(l):
                pe.wait_ge(S("LQ"), l + 1)
                if l >= LK0:
                    pe.wait_ge(S("LK"), l - LK0 + 1)
                q = L3[l % 3]
                for i in range(4 if l < LEVELS else 2):
                    o = begin(f"lv{l}_{i}")
                    for j in range(4):
                        c = (4 * i + j) * (P if l < LEVELS else T)
                        r = c if l < LEVELS else c + P
                        ins = mm(o[:, j * P:(j + 1) * P], q[:, c:c + P], q[:, r:r + P], start=True, stop=True)
                    end(ins, f"lv{l}_{i}")

            for j in range(4):
                tok(f"iv{j}")
            for i in range(4):
                o = begin(f"dg_{i}")
                for j in range(4):
                    c = (4 * i + j) * P
                    ins = mm(o[:, j * P:(j + 1) * P], hk[:, c:c + P], hq[:, c:c + P], start=True, stop=True)
                end(ins, f"dg_{i}")
            for l in range(LEVELS + 1):
                level(l)
                if l < 4:
                    feat(f"hz{l}")
            done(pe, "iv3")
            done(pe, "lv7_0")
            done(pe, "lv7_1")
            done(pe, f"lv{LEVELS - 1}_3")
            for i in range(4):
                o = begin(f"ho{i}")
                for j in range(2):
                    h = 2 * i + j
                    v0, v1 = ht[:, 0, h * P:(h + 1) * P], ht[:, 1, h * P:(h + 1) * P]
                    mm(o[:, j * T:j * T + P], v0, ATm[:, 2 * h, :], start=True, stop=True)
                    mm(o[:, j * T + P:(j + 1) * T], v0, AT2[:, h, :], start=True, stop=False)
                    ins = mm(o[:, j * T + P:(j + 1) * T], v1, ATm[:, 2 * h + 1, :], start=False, stop=True)
                end(ins, f"ho{i}")
            for y in range(2):
                o = begin(f"or{y}")
                for r in range(MH):
                    h = MH * y + r
                    if h % 2 == 0:
                        pe.wait_ge(S("sqo"), h // 2 + 1)
                    ins = mm(o[0:MH, 0:T], K("rowP")[:, MH - 1 - r:2 * MH - 1 - r], sq[:, h * T:(h + 1) * T],
                             start=(r == 0), stop=(r == MH - 1))
                end(ins, f"or{y}")
            for i in range(4):
                o = begin(f"ob{i}")
                pe.wait_ge(S("orow"), i // 2 + 1)
                for j in range(2):
                    y, r = (2 * i + j) // MH, (2 * i + j) % MH
                    ins = mm(o[:, j * T:(j + 1) * T], K("sel")[0:MH, r * P:(r + 1) * P], oroot[:, y * T:(y + 1) * T],
                             start=True, stop=True)
                end(ins, f"ob{i}")
            for j in range(4):
                feat(f"oo{j}", S("yp"), 4)

            sumsq(2)
            for g in range(4):
                begin(f"pw{g}")

            def product(w, _, n):
                g, k = n // 2, n % 2
                b, _ = place[f"pw{g}"]
                if k == 0 and g < 3:
                    pe.wait_ge(S("pl"), g + 1)
                elif k == 0:
                    pe.wait_ge(S("plP"), 1)
                for j in range(2):
                    ins = mm(ps[b][:, j * T:(j + 1) * T], w[:, j * P:(j + 1) * P], pl[:, n, :],
                             start=(k == 0 and j == 0), stop=(k == 1), skip_group_check=True)
                if k == 1 and g < 3:
                    end(ins, f"pw{g}")
                return ins

            end(chunk("pool", product, "pw3", first="pw1"), "pw3")

            def mlp(l):
                n = 3 + 2 * l
                sumsq(n)
                for j in range(FF // CW):
                    feat(f"w1_{l}_{j}", S(f"hp{n}") if j == 0 else None)
                for j in range(4):
                    o = begin(f"w2_{l}_{j}", 4)
                    for q in range(4):
                        def product(hi, lo, k):
                            if j == 0 and k % 2 == 0:
                                pe.wait_ge(S("h1l"), 16 * l + 4 * q + k // 2 + 1)
                            for i in range(2):
                                c = slice(i * P, (i + 1) * P)
                                ins = three(o[:, i * T:(i + 1) * T], hi[:, c], lo[:, c], h1h[:, q * KT + k, :],
                                            h1l[:, q * KT + k, :], q == 0 and k == 0 and i == 0,
                                            q == 3 and k == KT - 1)
                            return ins

                        ins = chunk(f"w2_{l}_{j}_{q}", product, f"w2_{l}_{j}" if q == 3 else None)
                        if q == 3:
                            end(ins, f"w2_{l}_{j}")

            mlp(0)
            pe.wait_ge(S("ld_s"), 16 * DMAS["ld_s"])
            for i in range(2):
                o = begin(f"ws{i}")
                for j in range(4):
                    ins = pe.transpose(o[:, j * P:(j + 1) * P], wst[:, 4 * i + j, :], idn)
                end(ins, f"ws{i}")
            sumsq(4)
            for j in range(4, 8):
                tok(f"si{j}", sem=S("hp4") if j == 4 else None)
            for j in range(4):
                feat(f"si{j}")
            done(pe, "ws1")
            pe.wait_ge(S("vln"), NT)
            for i in range(4):
                o = begin(f"mx{i}")
                for j in range(2):
                    h = 2 * i + j
                    for a in range(NT):
                        ins = mm(o[:, (2 * j + a) * P:(2 * j + a + 1) * P], vt[:, a, h * P:(h + 1) * P], wsT[:, h, :],
                                 start=True, stop=True)
                end(ins, f"mx{i}")
            for j in range(4):
                feat(f"so{j}", S("yp"), 8)
            mlp(1)
            sumsq(6)
            for i in range(4):
                o = begin(f"f{i}")
                for k in range(4):
                    f = 4 * (i % 2) + k
                    if i < 2:
                        operand(S("hs6"), None, f)
                    ins = pe.transpose(o[:, k * P:(k + 1) * P], hx[:, f, (i // 2) * P:(i // 2 + 1) * P], idn)
                end(ins, f"f{i}")
            assert count["chunk"] == len(chunks)

        def row_loads():
            A_, B_, C_ = rows
            ev = A["ev_b_in"][0]

            def r128(v):
                return v.rearrange("(r f) -> r f", f=P)

            def pair(v):
                return v.rearrange("(g b d) -> g b d", g=NG, d=ND)

            a = [(A_[0:16, :], A["norm_w"].rearrange("l (r f) -> (l r) f", f=P)),
                 (A_[16:36, :], r128(ev[0:C_GATE])),
                 (A_[40:46, :], r128(ev[C_KV:C_GT])),
                 (A_[50:58, :], r128(A["mlstm_conv_b"][0])),
                 (A_[58:62, :], r128(A["mlstm_head_norm"][0])),
                 (A_[66:82, :], A["cmp_k_pos"][0].rearrange("(m l) d -> m (l d)", l=2)),
                 (A_[82:98, :], A["cmp_v_pos"][0].rearrange("(m l) d -> m (l d)", l=2))]
            for g in range(NG):
                gs = slice(g * ND, (g + 1) * ND)
                a.append((A_[36:40, gs], pair(ev[C_NQ:C_KV])[g]))
                a.append((A_[46:50, gs], pair(ev[C_NZ:C_NZ + NW_])[g]))
                a.append((A_[62:63, gs], A["nsa_q_norm"][0:1, :]))
                a.append((A_[63:66, gs], A["nsa_k_norm"][0]))
            b = [(B_[0:32, :], A["mlstm_conv_w"][0].rearrange("t (r f) -> (t r) f", f=P)),
                 (B_[32:64, :], r128(A["od_b_in"][0])),
                 (B_[64:80, :], A["hgrn_lb_logits"].rearrange("l (r f) -> (l r) f", f=P)),
                 (B_[80:88, :], r128(A["hgrn_head_norm"][0])),
                 (B_[88:96, :], r128(A["final_g_2"][0])),
                 (B_[96:104, :], r128(A["c_2"][0])),
                 (B_[104:112, :], r128(A["pool_scale_2"][0]))]
            c = [(C_[0:96, :], A["ada_b_2"].rearrange("l (r f) -> (l r) f", f=P)),
                 (C_[96:112, :], A["norm_mix_g_2"].rearrange("l (r f) -> (l r) f", f=P)),
                 (C_[112:128, :], A["norm_mlp_g_2"].rearrange("l (r f) -> (l r) f", f=P))]
            return dict(ld_A=a, ld_B=b, ld_C=c)

        BV, BVS, BVW, BG, BF, BI = 0, 512, 640, 768, 800, 804
        loads = row_loads()
        ev = A["ev_b_in"]
        loads["ld_b"] = [(bcb[:, BV:BV + 512], ev[0:1, 2 * MW:3 * MW].broadcast_to([P, 512])),
                         (bcb[:, BVS:BVS + P], ev[0:1, C_KV + 3 * P:C_KV + 4 * P].broadcast_to([P, P])),
                         (bcb[:, BVW:BVW + P], ev[0:1, C_KV + 5 * P:C_KV + 6 * P].broadcast_to([P, P])),
                         (bcb[:, BG:BG + 8], ev[0:1, C_GATE:C_NQ].broadcast_to([P, 8])),
                         (bcb[:, BG + 8:BG + 32], ev[0:1, C_GT:C_NZ].broadcast_to([P, 24])),
                         (bcb[:, BF:BF + MH], A["mlstm_f_bias"].broadcast_to([P, MH])),
                         (bcb[:, BI:BI + D], A["od_b_in"][0:1, D:2 * D].broadcast_to([P, D]))]
        loads["ld_m"] = [(w2k, A["cmp_k_w2"][0]), (w2v, A["cmp_v_w2"][0])]
        loads["ld_s"] = [(wst, A["sgu_w_s_2"][0].rearrange("h t s -> t h s")),
                         (lng, A["sgu_ln_g_2"].broadcast_to([P, D])),
                         (lnb, A["sgu_ln_b_2"].broadcast_to([P, D])),
                         (bsb.rearrange("p h t -> p (h t)"),
                          A["sgu_b_s_2"].rearrange("l h t -> l (h t)").broadcast_to([P, 8 * P]))]
        assert all(DMAS[k] == len(v) for k, v in loads.items()), {k: len(v) for k, v in loads.items()}

        @block.sync
        def _(sp):
            first = 3 * P
            sp.dma_start(cst[:, 0:first], cst_dram[:, 0:first]).then_inc(S("ld_cst0"), 16)
            sp.dma_start(xtok[:, 0, :], A["x"][0, 0:P, :]).then_inc(S("ld_x"), 16)
            sp.dma_start(xtok[:, 1, :], A["x"][0, P:T, :]).then_inc(S("ld_x"), 16)
            for dst, src in loads["ld_A"]:
                sp.dma_start(dst, src).then_inc(S("ld_A"), 16)
            na = 0
            for kind, x in items:
                if kind == "w" and x["i"] == NF:
                    for nm in ("ld_B", "ld_C", "ld_b", "ld_m"):
                        for dst, src in loads[nm]:
                            sp.dma_start(dst, src).then_inc(S(nm), 16)
                    sp.dma_start(cst[:, first:NCST], cst_dram[:, first:NCST]).then_inc(S("ld_cst"), 16)
                if kind == "w":
                    if x["i"] >= NF:
                        sp.wait_ge(*wf_free(halves[x["i"] - NF]))
                    w = wf[:, x["slot"], :].rearrange("p (k n) -> p k n", n=P if x["name"].startswith("cmp") else CW)
                    for p, k, c, src in x["parts"]:
                        sp.dma_start(w[p, k, c], src).then_inc(S(f"w{x['slot']}"), 16)
                else:
                    l, g, q = x
                    if na >= NA:
                        sp.wait_ge(S("wa"), na - NA + 1)
                    sp.dma_start(wa[:, na % NA, :].rearrange("p (k n) -> p k n", n=AG),
                                 A["ada_w_2"][l][q * 2 * P:(q + 1) * 2 * P, g * AG:(g + 1) * AG]
                                 .rearrange("(k p) n -> p k n", p=P)).then_inc(S(f"la{na % NA}"), 16)
                    na += 1
            for i in range(4):
                done(sp, f"f{i}")
            for a in range(NT):
                sp.dma_start(out_dram[0, a * P:(a + 1) * P, :], ot[:, a, :]).then_inc(S("st"), 16)
            sp.wait_ge(S("st"), 16 * NT)

        @block.gpsimd
        def _(g):
            ahead_of["P"] = (g, lambda name: keep("P", g, name))
            def full(name):
                ahead(g, name)
                b, n = place[name]
                g.wait_ge(S(f"full{b}"), n)

            g.memset(hvp, 0.0).then_inc(S("zero"), 1)
            full("par2")
            g.memset(qkp[:, :, 0:3], 0.0).then_inc(S("zero"), 1)
            ahead(g, "v0")
            g.wait_ge(S("ET"), 1)
            g.wait_ge(S("ld_cst"), 16)
            tri = K("tri").unsqueeze(1).broadcast_to([P, MH, P])
            g.tensor_tensor(ET[:, :, 0:P], ET[:, :, 0:P], tri, ALU.mult).then_inc(S("ETm"), 1)
            g.tensor_tensor(ET[:, :, T:T + P], ET[:, :, T:T + P], tri, ALU.mult).then_inc(S("ETm"), 1)
            for n in ("o0", "o1", "z0", "z1"):
                done(g, n)
            g.tensor_tensor(og, og, zg, ALU.mult).then_inc(S("oz"), 1)
            for n in ("nz0", "nz1", "eo0", "eo1", "eo2", "eo3"):
                done(g, n)
            g.memset(rst, 1.0).then_inc(S("rst"), 1)
            g.wait_ge(S("rst"), 1)
            g.memset(rst.rearrange("p (n t) -> p n t", t=P)[:, :, 0:1], 0.0).then_inc(S("rst"), 1)
            g.memset(ATm, 0.0).then_inc(S("AT0"), 1)
            for n in [f"fp{i}" for i in range(4)] + [f"qp{i}" for i in range(4)]:
                done(g, n)
            for l in range(LEVELS + 1):
                ahead(g, f"iv{l}" if l < 2 else f"hz{l - 1}" if l < 5 else f"lv{l - 3}_3")
                g.wait_ge(S("LX"), l + 1)
                m = P >> (l + 1) if l < LEVELS else P
                v = L3[l % 3].rearrange("p (n y t) -> p n y t", y=2, t=m)
                for y, src in ((0, hk), (1, hq))[l >= LK0:]:
                    s = src.rearrange("p (n y t) -> p n y t", y=2, t=m)
                    ins = g.tensor_tensor(v[:, :, y, :], v[:, :, y, :], s[:, :, y, :], ALU.mult)
                ins.then_inc(S("LQ"), 1)
            for j in range(4):
                done(g, f"oo{j}")
            for dst, src in loads["ld_s"]:
                g.dma_start(dst, src).then_inc(S("ld_s"), 16)
            full("ss2")
            g.memset(hT[:, :, 0:PADW], 0.0).then_inc(S("zero"), 1)

            steps_done = [0]

            def step(ins):
                steps_done[0] += 1
                ins.then_inc(S("g"), 1)
                g.wait_ge(S("g"), steps_done[0])

            g.wait_ge(S("zero"), 3)
            pool_group(3, g, step).then_inc(S("plP"), 1)

            def hidden(l):
                for j in range(FF // CW):
                    ahead(g, f"w1_{l}_{min(j + 1, FF // CW - 1)}")
                    done(g, f"w1_{l}_{j}")
                    g.wait_ge(S("h1h"), 16 * l + j + 1)
                    g.tensor_tensor(h1l[:, 2 * j:2 * j + 2, :].rearrange("p f t -> p (f t)"), r2[j % 2],
                                    h1h[:, 2 * j:2 * j + 2, :].rearrange("p f t -> p (f t)"),
                                    ALU.subtract).then_inc(S("h1l"), 1)
                for j in range(4):
                    done(g, f"w2_{l}_{j}")

            hidden(0)
            for n in [f"si{j}" for j in (4, 5, 6, 7, 0, 1, 2, 3)] + [f"so{j}" for j in range(4)]:
                done(g, n)
            hidden(1)

        @block.scalar
        def _(act):
            ahead_of["A"] = (act, lambda name: keep("A", act, name))
            chain = [0]

            def A_(out, in_, f=ACT.Identity, **kw):
                return act.activation(out, in_, f, **kw)

            def step(ins):
                chain[0] += 1
                ins.then_inc(S("a"), 1)
                act.wait_ge(S("a"), chain[0])

            def pc(c):
                return par[:, c:c + 1]

            def flat(v):
                return v.rearrange("p b t -> p (b t)")

            def roots(names, dst, n):
                for i, nm in enumerate(names):
                    free(A_(dst[:, i * n:(i + 1) * n], got(act, nm)[:, 0:n], ACT.Sqrt, bias=EPS), nm)

            def norm(n, prev, shift=None):
                A_(early, one[:, 0:1], ACT.Sqrt)
                for i in range(4):
                    if n:
                        done(act, f"{prev}{i}")
                    A_(sq[:, i * 512:(i + 1) * 512], flat(xT[:, 2 * i:2 * i + 2, :]),
                       ACT.Square).then_inc(S("sq"), 1)
                roots([f"ss{n}"], rstd, T)
                if n == 6:
                    return
                for q, (lo, hi) in enumerate(PIECES):
                    act.wait_ge(S(f"hs{n}"), q + 1)
                    if shift is None:
                        ins = A_(hh[:, lo:hi, :], hx[:, lo:hi, :], ACT.Copy)
                    else:
                        l, c = shift
                        for k in range(lo, hi):
                            ins = A_(hx[:, k, :] if n == 2 else hh[:, k, :], hx[:, k, :],
                                     bias=mod[:, l, c + k:c + k + 1])
                    ins.then_inc(S(f"hh{n}"), 1)

            def parts(src, at, sem, before):
                ahead(act, before)
                act.wait_ge(*sem)
                A_(flat(hh[:, at:at + 2, :]), src, ACT.Copy).then_inc(S("yh"), 1)

            def both(name, dst, f, cols):
                o = got(act, name)
                for j in range(2):
                    ins = A_(dst(j), o[:, j * T:(j + 1) * T], f, bias=cols(j))
                free(ins, name)

            def whole(name, dst, f=ACT.Identity, n=512):
                free(A_(dst, got(act, name)[:, 0:n], f), name)

            for i in (0, 2):
                o = got(act, f"x{i}")
                free(A_(xT[:, 4 * (i % 2):4 * (i % 2) + 4, (i // 2) * P:(i // 2 + 1) * P],
                        o[:, :].rearrange("p (b t) -> p b t", t=P)), f"x{i}")
            for i in range(4):
                done(act, f"x{i}")
            norm(0, None)
            done(act, "par1")
            A_(cs, par[:, PB["c"]:PB["c"] + KT], ACT.Silu).then_inc(S("cs"), 1)
            act.wait_ge(S("lbx"), 1)
            A_(lb, lb, ACT.Exp)
            A_(oml, oml, ACT.Exp).then_inc(S("lbe"), 1)
            done(act, "par0")
            for i, n in enumerate(("q0", "q1", "k0", "k1")):
                both(n, lambda j: qkp[:, 2 * i + j, 3:3 + T], ACT.Identity, lambda j: pc(PA["b20"] + 2 * i + j))
            act.wait_ge(S("gt"), 1)
            A_(gt[:, :, 8:NGATE], gt[:, :, 8:NGATE], ACT.Sigmoid).then_inc(S("gsig"), 1)
            ahead(act, "gtT")
            act.wait_ge(S("absf"), 1)
            step(A_(erow, trow, ACT.Exp, scale=-1.0))
            A_(erow, erow, ACT.Ln, bias=1.0).then_inc(S("lnf"), 1)
            for i in range(2):
                both(f"nq{i}", lambda j: R[:, (2 * i + j) * T:(2 * i + j + 1) * T], ACT.Identity,
                     lambda j: pc(PA["bnq"] + 2 * i + j))
            ahead(act, "ksvs")
            act.wait_ge(S("conv"), 1)
            A_(flat(qkc), flat(qkc), ACT.Silu).then_inc(S("qkc"), 1)
            ahead(act, "kwvw")
            act.wait_ge(S("bg"), 1)
            A_(erow, trow, ACT.Exp, scale=-1.0).then_inc(S("erow"), 1)
            done(act, "nq1")
            done(act, "ksvs")
            done(act, "kwvw")
            A_(sq[:, 0:1536], R[:, 0:1536], ACT.Square).then_inc(S("sqR"), 1)
            done(act, "gb1")
            e2 = flat(ET)
            A_(e2, e2, ACT.Exp, scale=-1.0).then_inc(S("ET"), 1)
            free(A_(qrow, got(act, "rs")[0:12, 0:T], ACT.Sqrt, bias=EPS), "rs")
            o = got(act, "hid")
            A_(hk_[:, 0:2 * NCMP], o[:, 0:2 * NCMP], ACT.Gelu_apprx_tanh)
            free(A_(hv_[:, 0:2 * NCMP], o[:, 32:32 + 2 * NCMP], ACT.Gelu_apprx_tanh), "hid")

            def gate(nm, i):
                t, f, c = dict(o=(og, ACT.Sigmoid, PA["b20"] + 12), z=(zg, ACT.Silu, PA["b20"] + 16),
                               nz=(nz, ACT.Silu, PA["bnz"]))[nm]
                both(f"{nm}{i}", lambda j: t[:, (2 * i + j) * T:(2 * i + j + 1) * T], f, lambda j: pc(c + 2 * i + j))

            gate("o", 0)
            free(A_(drow, got(act, "dn")[0:MH, 0:T], ACT.Abs), "dn")
            gate("o", 1)
            for i in range(2):
                whole(f"dr{i}", denb[:, i * 512:(i + 1) * 512])
            roots(["rsc"], R2[:, 1536:1536 + NCMP], NCMP)
            done(act, "nm1")
            A_(sq[:, 0:1024], hm, ACT.Square).then_inc(S("sqh"), 1)
            gate("z", 0)
            free(A_(hrow, got(act, "hr")[0:MH, 0:T], ACT.Sqrt, bias=EPS), "hr")
            for i, v in enumerate((P0, Pc, P1, P1)):
                if i == 3:
                    gate("z", 1)
                    gate("nz", 0)
                ahead(act, ("s0_3", "sc1", "s1_7", "nz0")[i])
                act.wait_ge(S("smax"), i + 1)
                v = v[:, :, :, 0:NCMP] if i == 1 else v
                if i < 2:
                    ins = A_(v, v, ACT.Exp)
                else:
                    for h in range(4 * i - 8, 4 * i - 4):
                        for y in range(2):
                            c = slice(2 * h + y, 2 * h + y + 1)
                            ins = A_(v[:, h, y, :], v[:, h, y, :], ACT.Exp, bias=mx1[:, c], accum_out=sm1[:, c])
                ins.then_inc(S("sexp"), 1)
            gate("nz", 1)
            for i in range(4):
                whole(f"t0_{i}", PT0[:, 2 * i:2 * i + 2, :, :].rearrange("p h y k -> p (h y k)"))
            whole("tc", PTc.rearrange("p a g k -> p (a g k)"))
            for h in (0, 1, 2, 4, 6):
                whole(f"t1_{h}", PT1[:, h, :, :].rearrange("p y k -> p (y k)"))
            for i in range(2):
                parts(og[:, i * 512:(i + 1) * 512], 2 * i, (S("yA"), 1), "nz1")
            for i in range(2):
                done(act, f"av{i}")
                A_(flat(hh[:, MH + 2 * i:MH + 2 * i + 2, :]), nz[:, i * 512:(i + 1) * 512],
                   ACT.Copy).then_inc(S("yh"), 1)
            norm(1, "eo")
            act.wait_ge(S("ndb"), 1)
            for i in range(4):
                o = got(act, f"fp{i}")
                for j in range(2):
                    b = 2 * i + j
                    A_(hb[:, b * T:(b + 1) * T], o[:, j * T:(j + 1) * T], ACT.Sigmoid, bias=pc(PB["odb"] + b))
                    ins = A_(hk[:, b * T:(b + 1) * T], o[:, j * T:(j + 1) * T], ACT.Sigmoid, bias=nodb[:, b:b + 1],
                             scale=-1.0)
                free(ins, f"fp{i}")
            for i in range(4):
                if i == 1:
                    ahead(act, "qp1")
                    act.wait_ge(S("hf"), 1)
                    A_(hb2, hb, ACT.Ln).then_inc(S("hln"), 1)
                both(f"qp{i}", lambda j: hq[:, (2 * i + j) * T:(2 * i + j + 1) * T], ACT.Silu,
                     lambda j: pc(PB["odb"] + 16 + 2 * i + j))
            for l in range(LEVELS + 1):
                ahead(act, f"iv{l}" if l < 2 else "dg_3" if l < 3 else f"lv{l - 3}_3")
                act.wait_ge(S("LE"), l + 1)
                A_(L3[l % 3], L3[l % 3], ACT.Exp).then_inc(S("LX"), 1)
                if 1 <= l <= 4:
                    both(f"hz{l - 1}", lambda j: hz[:, (2 * l - 2 + j) * T:(2 * l - 1 + j) * T], ACT.Identity,
                         lambda j: pc(PB["odb"] + 24 + 2 * l - 2 + j))
            done(act, "hz3")
            A_(hz, hz, ACT.Silu).then_inc(S("hz"), 1)
            for i in range(2):
                whole(f"lv7_{i}", AT2[:, 4 * i:4 * i + 4, :].rearrange("p h j -> p (h j)"))
            for i in range(4):
                whole(f"ho{i}", hO[:, i * 512:(i + 1) * 512])
                done(act, f"ho{i}")
                A_(sq[:, i * 512:(i + 1) * 512], hO[:, i * 512:(i + 1) * 512], ACT.Square).then_inc(S("sqo"), 1)
            for y in range(2):
                free(A_(oroot[:, y * T:(y + 1) * T], got(act, f"or{y}")[0:MH, 0:T], ACT.Sqrt, bias=EPS), f"or{y}")
            for i in range(4):
                parts(hO[:, i * 512:(i + 1) * 512], 2 * i, (S("yH"), i + 1), "ob3")
            norm(2, "oo", (0, 0))

            def mlp(l, prev):
                norm(3 + 2 * l, prev, (l, 24))

                def copy(j):
                    done(act, f"w1_{l}_{j}")
                    A_(flat(h1h[:, 2 * j:2 * j + 2, :]), r2[j % 2], ACT.Copy).then_inc(S("h1h"), 1)

                for j in range(FF // CW):
                    o = got(act, f"w1_{l}_{j}")
                    if j >= 2:
                        done(act, f"w1_{l}_{j - 2}")
                    A_(rl[j % 2], o[:, :], ACT.Relu).then_inc(S("relu"), 1)
                    if j:
                        copy(j - 1)
                copy(FF // CW - 1)

            mlp(0, "pw")
            norm(4, "w2_0_", (1, 0))
            for j in range(4):
                o = got(act, f"si{4 + j}")
                free(A_(vt[:, :, j * CW:(j + 1) * CW], o[:, :].rearrange("p (a n) -> p a n", a=NT), ACT.Gelu),
                     f"si{4 + j}")
            for j in range(2):
                whole(f"si{j}", flat(uT[:, 2 * j:2 * j + 2, :]), ACT.Gelu)
            for a in range(NT):
                act.wait_ge(S("xc"), a + 1)
                A_(sq[:, a * D:(a + 1) * D], xc[:, a, :], ACT.Square, accum_out=vr[:, a:a + 1]).then_inc(S("vr"), 1)
            act.wait_ge(S("vr"), NT)
            A_(vr, vr, ACT.Sqrt, scale=1.0 / D, bias=LN_EPS).then_inc(S("vs"), 1)
            for j in range(2, 4):
                whole(f"si{j}", flat(uT[:, 2 * j:2 * j + 2, :]), ACT.Gelu)
            for i in range(4):
                parts(flat(xc)[:, i * 512:(i + 1) * 512], 2 * i, (S("yS"), i + 1), f"mx{i}")
            mlp(1, "so")
            norm(6, "w2_1_")
            for i in (0, 2):
                whole(f"f{i}", ot[:, i // 2, (i % 2) * 512:(i % 2 + 1) * 512])

        @block.vector
        def _(dve):
            ahead_of["V"] = (dve, lambda name: keep("V", dve, name))
            chain = [0]

            def V(ins):
                chain[0] += 1
                ins.then_inc(S("v"), 1)
                dve.wait_ge(S("v"), chain[0])

            def pc(c):
                return par[:, c:c + 1]

            ts, tt, stt = dve.tensor_scalar, dve.tensor_tensor, dve.scalar_tensor_tensor
            MUL, ADD, SUB, MAX = ALU.mult, ALU.add, ALU.subtract, ALU.max

            def inverse(name, dst, sem=None):
                done(dve, name)
                ins = dve.reciprocal(dst, dst)
                if sem:
                    ins.then_inc(S(sem), 1)
                else:
                    V(ins)

            def norm(n, gain, shift=None):
                inverse(f"ss{n}", rstd)

                def scale(q):
                    for k in range(*PIECES[q]):
                        ins = stt(hx[:, k, :], xT[:, k, :], gain(k), rstd, MUL, MUL)
                    ins.then_inc(S(f"hs{n}"), 1)

                scale(0)
                scale(1)
                scale(2)
                for q, (lo, hi) in enumerate(PIECES):
                    if n not in (2, 6):
                        dve.wait_ge(S(f"hh{n}"), q + 1)
                        if shift is None:
                            ins = tt(hl[:, lo:hi, :], hx[:, lo:hi, :], hh[:, lo:hi, :], SUB)
                        else:
                            l, c = shift
                            for k in range(lo, hi):
                                ins = stt(hl[:, k, :], hx[:, k, :], mod[:, l, c + k:c + k + 1], hh[:, k, :], ADD, SUB)
                        ins.then_inc(S(f"hp{n}"), 1)
                    if q + 3 < len(PIECES):
                        scale(q + 3)

            yparts = [0]

            def parts(src, at):
                yparts[0] += 1
                dve.wait_ge(S("yh"), yparts[0])
                tt(hl[:, at:at + 2, :].rearrange("p b t -> p (b t)"), src,
                   hh[:, at:at + 2, :].rearrange("p b t -> p (b t)"), SUB).then_inc(S("yp"), 1)

            def residual(name, gain=None):
                for i in range(4):
                    o = got(dve, f"{name}{i}")
                    if gain is None:
                        x = xT[:, 2 * i:2 * i + 2, :].rearrange("p b t -> p (b t)")
                        ins = tt(x, o[:, :], x, ADD)
                    else:
                        for j in range(2):
                            b = 2 * i + j
                            ins = stt(xT[:, b, :], o[:, j * T:(j + 1) * T], gain(b), xT[:, b, :], MUL, ADD)
                    free(ins, f"{name}{i}")

            for i in (1, 3):
                o = got(dve, f"x{i}")
                free(dve.tensor_copy(xT[:, 4 * (i % 2):4 * (i % 2) + 4, (i // 2) * P:(i // 2 + 1) * P],
                                     o[:, :].rearrange("p (b t) -> p b t", t=P)), f"x{i}")
            for i, n in enumerate((NA_ROWS, NB_ROWS, NC_ROWS)):
                free(dve.tensor_copy(par[:, i * P:i * P + n], got(dve, f"par{i}")[:, 0:n]), f"par{i}")
                done(dve, f"par{i}")
                if i == 0:
                    for j in range(4):
                        done(dve, f"x{j}")
                    norm(0, lambda k: pc(PA["nw"] + k))
            V(ts(pc(PA["qn"]), pc(PA["qn"]), ND ** -0.5, None, MUL))
            l0, l1 = par[:, PB["lbl"]:PB["lbl"] + HH], par[:, PB["lbl"] + HH:PB["lbl"] + 2 * HH]
            V(tt(lbt, l0, l1, MAX))
            tt(lb, l0, lbt, SUB)
            tt(oml, l1, lbt, SUB).then_inc(S("lbx"), 1)
            ts(nodb, par[:, PB["odb"]:PB["odb"] + HH], -1.0, None, MUL).then_inc(S("ndb"), 1)
            dve.wait_ge(S("ld_b"), 16 * DMAS["ld_b"])
            dve.wait_ge(S("ld_cst"), 16)
            o = got(dve, "gt")
            free(tt(gt, o[:, 0:NT * NGATE].rearrange("p (a n) -> p a n", a=NT),
                    bcb[:, BG:BG + NGATE].unsqueeze(1).broadcast_to([P, NT, NGATE]), ADD), "gt")
            done(dve, "gt")
            tt(gt[:, :, MH:2 * MH], gt[:, :, MH:2 * MH],
               bcb[:, BF:BF + MH].unsqueeze(1).broadcast_to([P, NT, MH]), ADD).then_inc(S("gt"), 1)
            dve.wait_ge(S("lbe"), 1)
            V(tt(lbt, lb, oml, ADD))
            V(dve.reciprocal(lbt, lbt))
            V(tt(lb, lb, lbt, MUL))
            V(ts(oml, lb, -1.0, 1.0, MUL, ADD))

            def tokens(name, dst, c0, b0, n, last=True):
                o = got(dve, name)
                ins = tt(dst, o[:, c0:c0 + NT * n].rearrange("p (a n) -> p a n", a=NT),
                         bcb[:, b0:b0 + n].unsqueeze(1).broadcast_to([P, NT, n]), ADD)
                free(ins, name)

            free(dve.tensor_copy(ifrow, got(dve, "gtT")[0:MH, :]), "gtT")
            done(dve, "gtT")
            stt(trow, frow, -1.0, frow, MUL, MAX).then_inc(S("absf"), 1)
            dve.wait_ge(S("absf"), 1)
            done(dve, "k1")
            dve.wait_ge(S("zero"), 2)
            for tap in range(TAPS):
                for b in range(8):
                    w = pc(PB["cvw"] + tap * 8 + b)
                    if tap == 0:
                        ins = ts(qkc[:, b, :], qkp[:, b, 0:T], w, pc(PA["cvb"] + b), MUL, ADD)
                    else:
                        ins = stt(qkc[:, b, :], qkp[:, b, tap:tap + T], w, qkc[:, b, :], MUL, ADD)
                if tap < TAPS - 1:
                    V(ins)
                else:
                    ins.then_inc(S("conv"), 1)
                if tap in (0, 2):
                    ahead(dve, ("nq0", "ksvs")[tap // 2])
                if tap == 1:
                    ahead(dve, "nq1")
                    V(ts(frow, frow, 0.0, None, ALU.min))
                    dve.wait_ge(S("lnf"), 1)
                    V(tt(trow, frow, erow, SUB))
                    V(dve.memset(orow, 1.0))
                    V(dve.tensor_tensor_scan(brow, orow, trow, 0.0, MUL, ADD))
                    tt(arow, irow, brow, SUB).then_inc(S("arow"), 1)
                    dve.wait_ge(S("arow"), 1)
                    dve.tensor_tensor_scan(grow, orow, arow, 0.0, MUL, MAX).then_inc(S("grow"), 1)
                    dve.wait_ge(S("grow"), 1)
                    tt(trow, brow, grow, ADD).then_inc(S("bg"), 1)
            for y, n in enumerate(("ksvs", "kwvw")):
                o = got(dve, n)
                ts(R[:, (4 + y) * T:(5 + y) * T], o[:, 0:T], pc(PA["bkv"] + 2 + 2 * y), None, ADD)
                tokens(n, vsw[:, y, :, :], T, BVS + y * P, P)
            free(dve.tensor_copy(acol, got(dve, "aT")[:, 0:NT * MH].rearrange("p (a h) -> p a h", a=NT)), "aT")
            done(dve, "aT")
            for i in range(2):
                o = got(dve, f"gb{i}")
                for j in range(2):
                    h = 2 * i + j
                    ts(ET[:, h, 0:T], o[:, j * T:(j + 1) * T], acol[:, 0, h:h + 1], 0.0, SUB, MAX)
                    ins = ts(ET[:, h, T:T + P], o[:, j * T + P:(j + 1) * T], acol[:, 1, h:h + 1], 0.0, SUB, MAX)
                free(ins, f"gb{i}")
            o = got(dve, "kcvc")
            for y in range(2):
                ins = ts(kcvc[:, y, :], o[:, y * T:(y + 1) * T], pc(PA["bkv"] + y), None, ADD)
            free(ins, "kcvc")
            done(dve, "kcvc")
            for y, X in enumerate((XK, XV)):
                for g in range(NG):
                    src = kcvc[g * ND:(g + 1) * ND, y, :]
                    dve.tensor_copy(X[0:ND, g, :], src)
                    ins = dve.tensor_copy(X[ND:P, g, 0:T - 1], src[:, 1:T])
            V(ins)
            for y, (X, pos) in enumerate(((XK, PA["kpos"]), (XV, PA["vpos"]))):
                for g in range(NG):
                    xv = X[:, g, :].rearrange("p (n s) -> p s n", s=CMP_STRIDE)
                    for u in range(2):
                        tt(CR[:, y, 8 * u:8 * u + 8, g, :], xv[:, 0:CMP_STRIDE:2, u:u + NCMP],
                           par[:, pos + 8 * u:pos + 8 * u + 8].unsqueeze(2).broadcast_to([P, 8, NCMP]),
                           ADD).then_inc(S("CR"), 1)
            tokens("v0", vtok[:, :, 0:CW], 0, BV, CW)
            inverse("rs", qrow, "qrow")
            tokens("v1", vtok[:, :, CW:2 * CW], 0, BV + CW, CW)
            done(dve, "nq1")
            for i in range(3):
                o = got(dve, f"rb{i}")
                for j in range(2):
                    b = 2 * i + j
                    ins = stt(R2[:, b * T:(b + 1) * T], R[:, b * T:(b + 1) * T], pc(PA["qn"] if b < 4 else PA["kn"] + b - 3),
                              o[:, j * T:(j + 1) * T], MUL, MUL)
                free(ins, f"rb{i}")
            dve.wait_ge(S("ETm"), 2)
            for h in range(MH):
                free(stt(ST[:, h, :], got(dve, f"st{h}")[:, 0:T + P], float(P) ** -0.5, ET[:, h, :], MUL, MUL),
                     f"st{h}")
            done(dve, "hid")
            hv4 = hvp.rearrange("p (g i n) -> p g i n", g=NG, i=4)
            for g in range(NG):
                ins = dve.tensor_copy(hv4[:, g, :, 0:NCMP],
                                      hv_[:, g * NCMP:(g + 1) * NCMP].unsqueeze(1).broadcast_to([P, 4, NCMP]))
            ins.then_inc(S("hvp"), 1)
            done(dve, "dn")
            dve.wait_ge(S("erow"), 1)
            V(tt(drow, drow, erow, MAX))
            dve.reciprocal(drow, drow).then_inc(S("drow"), 1)
            kc = slice(1536, 1536 + NCMP)
            o = got(dve, "cmp2")
            dve.tensor_copy(R[:, kc], o[:, 0:NCMP])
            free(dve.tensor_copy(VC, o[:, 64:64 + P]), "cmp2")
            done(dve, "cmp2")
            tt(sq[:, kc], R[:, kc], R[:, kc], MUL).then_inc(S("sqc"), 1)
            for i in range(4):
                ins = ts(VC4[:, i, :], VC, K("rg")[:, i:i + 1], None, MUL)
            ins.then_inc(S("VC4"), 1)
            for i in range(3):
                free(tt(R[:, i * 512:(i + 1) * 512].rearrange("p (b t) -> p b t", t=T),
                        got(dve, f"pr{i}")[:, :].rearrange("p (b t) -> p b t", t=T),
                        K("sin").unsqueeze(1).broadcast_to([P, 2, T]), MUL), f"pr{i}")
            r6 = R2[:, 0:1536].rearrange("p (b t) -> p b t", t=T)
            V(tt(r6, r6, K("cos").unsqueeze(1).broadcast_to([P, 6, T]), MUL))
            done(dve, "pr2")
            tt(R[:, 0:1536], R[:, 0:1536], R2[:, 0:1536], ADD).then_inc(S("rope"), 1)
            for i in range(2):
                done(dve, f"dr{i}")
                free(tt(hm[:, i * 512:(i + 1) * 512], got(dve, f"nm{i}")[:, :], denb[:, i * 512:(i + 1) * 512], MUL),
                     f"nm{i}")
            inverse("rsc", R2[:, kc])
            stt(R2[:, kc], R[:, kc], pc(PA["kn"]), R2[:, kc], MUL, MUL).then_inc(S("Rnc"), 1)
            ends = slice(CMP_LEN - 1, T, CMP_STRIDE)
            free(tt(R[:, kc], got(dve, "prc")[:, 0:NCMP], K("sin")[:, ends], MUL), "prc")
            V(tt(R2[:, kc], R2[:, kc], K("cos")[:, ends], MUL))
            done(dve, "prc")
            tt(R[:, kc], R[:, kc], R2[:, kc], ADD).then_inc(S("ropec"), 1)
            inverse("hr", hrow, "hrow")
            m1 = K("m1")
            mc = K("mc").rearrange("p (a n) -> p a n", a=NT).unsqueeze(2).broadcast_to([P, NT, NH, NCMP])
            mc01 = K("mc01").rearrange("p (a n) -> p a n", a=NT).unsqueeze(2).broadcast_to([P, NT, NH, NCMP])
            pcv = Pc[:, :, :, 0:NCMP]
            g3 = gt[:, :, 8:NGATE].rearrange("p a (h c) -> p a h c", c=3)
            sets = [(v, mx.rearrange("p (a b) -> p a b", a=sh[1]), su.rearrange("p (a b) -> p a b", a=sh[1]), gv, sh)
                    for v, mx, su, gv, sh in ((P0, mx0, sm0, g3[:, 0, :, 1:3], [P, NH, 2, P]),
                                              (pcv, mxc, smc, g3[:, :, :, 0], [P, NT, NH, NCMP]),
                                              (P1[:, 0:4], mx1[:, 0:8], sm1[:, 0:8], g3[:, 1, 0:4, 1:3], [P, 4, 2, T]),
                                              (P1[:, 4:8], mx1[:, 8:16], sm1[:, 8:16], g3[:, 1, 4:8, 1:3],
                                               [P, 4, 2, T]))]

            def less_max(i):
                v, mx, _, _, sh = sets[i]
                V(dve.tensor_reduce(mx, v, AX, MAX))
                if i >= 2:
                    ts(mx, mx, -1.0, None, MUL).then_inc(S("smax"), 1)
                    return
                tt(v, v, mx.unsqueeze(3).broadcast_to(sh), SUB).then_inc(S("smax"), 1)

            def weigh(i, before):
                v, _, su, gv, sh = sets[i]
                ahead(dve, before)
                dve.wait_ge(S("sexp"), i + 1)
                if i < 2:
                    V(dve.tensor_reduce(su, v, AX, ADD))
                V(dve.reciprocal(su, su))
                V(tt(su, su, gv, MUL))
                if i == 1:
                    V(tt(v, v, mc01, MUL))
                tt(v, v, su.unsqueeze(3).broadcast_to(sh), MUL).then_inc(S(("P0", "Pc", "P1", "P1")[i]), 1)

            V(dve.memset(Pc, 0.0))
            for i in range(4):
                free(tt(P0[:, 2 * i:2 * i + 2, :, :].rearrange("p h y k -> p (h y) k"),
                        got(dve, f"s0_{i}")[:, :].rearrange("p (n k) -> p n k", k=P),
                        m1[:, P:T].unsqueeze(1).broadcast_to([P, 4, P]), ADD), f"s0_{i}")
            for g in range(NG):
                hs = slice(g * NR, (g + 1) * NR)
                o = got(dve, f"sc{g}")
                free(tt(pcv[:, :, hs, :], o[:, 0:NT * NR * NCMP].rearrange("p (a h n) -> p a h n", a=NT, h=NR),
                        mc[:, :, hs, :], ADD), f"sc{g}")
            done(dve, "s0_3")
            less_max(0)
            done(dve, "sc1")
            less_max(1)
            for h in range(NH):
                free(tt(P1[:, h, :, :], got(dve, f"s1_{h}")[:, :].rearrange("p (y k) -> p y k", y=2),
                        m1.unsqueeze(1).broadcast_to([P, 2, T]), ADD), f"s1_{h}")
                if h % 4 == 3:
                    for i in range(h - 3, h + 1):
                        done(dve, f"s1_{i}")
                    less_max(2 + h // 4)
            dve.wait_ge(S("gsig"), 1)
            weigh(0, "z1")
            weigh(1, "z1")
            for h in range(MH):
                s = slice(h * T, (h + 1) * T)
                o = got(dve, f"hb{h // 2}")
                ins = stt(R2[:, s], hm[:, s], pc(PA["mhn"] + h), o[:, (h % 2) * T:(h % 2 + 1) * T], MUL, MUL)
                if h % 2:
                    free(ins, f"hb{h // 2}")
            done(dve, "hb1")
            weigh(2, "nz0")
            weigh(3, "nz0")
            ahead(dve, "nz1")
            dve.wait_ge(S("oz"), 1)
            tt(og, R2[:, 0:1024], og, MUL).then_inc(S("yA"), 1)
            for h in (3, 5, 7):
                free(dve.tensor_copy(PT1[:, h, :, :].rearrange("p y k -> p (y k)"), got(dve, f"t1_{h}")[:, :]),
                     f"t1_{h}")
            done(dve, "nz1")
            for i in range(2):
                parts(og[:, i * 512:(i + 1) * 512], 2 * i)
            for i in range(2):
                n = nz[:, i * 512:(i + 1) * 512]
                free(tt(n, got(dve, f"av{i}")[:, :], n, MUL), f"av{i}")
                parts(n, MH + 2 * i)

            def modulation(k):
                l, lo, hi = STAGES[k]
                dve.wait_ge(S("ada"), 12 * l + hi // 4)
                b = PC["adab"] + 48 * l
                tt(mod[:, l, lo:hi], adaps[:, l * 48 + lo:l * 48 + hi], par[:, b + lo:b + hi], ADD).then_inc(S("mod"), 1)
                dve.wait_ge(S("mod"), k + 1)
                for i, (c, g) in enumerate(((8, PC["nmix"]), (32, PC["nmlp"]))):
                    if lo <= c < hi:
                        V(stt(A1[2 * l + i], mod[:, l, c:c + KT], 1.0, par[:, g + 8 * l:g + 8 * l + 8], ADD, MUL))
                if k == 0:
                    V(tt(gsc, mod[:, 0, 16:24], par[:, PB["psc"]:PB["psc"] + KT], MUL))

            residual("eo")
            done(dve, "eo3")
            norm(1, lambda k: pc(PA["nw"] + KT + k))
            done(dve, "fp3")
            for b in range(HH):
                s = slice(b * T, (b + 1) * T)
                ts(hb[:, s], hb[:, s], oml[:, b:b + 1], lb[:, b:b + 1], MUL, ADD)
                ins = ts(hk[:, s], hk[:, s], oml[:, b:b + 1], None, MUL)
                if b == 3:
                    ahead(dve, "qp0")
            ins.then_inc(S("hf"), 1)
            ahead(dve, "qp1")
            dve.wait_ge(S("hln"), 1)
            dve.wait_ge(S("rst"), 2)
            V(dve.tensor_tensor_scan(hb, rst, hb2, 0.0, MUL, ADD))

            def exponents(l):
                m = P >> (l + 1) if l < LEVELS else P
                if l >= 3:
                    got(dve, f"lv{l - 3}_3")
                b = hb.rearrange("p (n y t) -> p n y t", y=2, t=m)
                e = L3[l % 3].rearrange("p (n y t) -> p n y t", y=2, t=m)
                n = 2 * HH * P // (2 * m)
                ref = b[:, :, 0, m - 1:m].broadcast_to([P, n, m])
                tt(e[:, :, 0, :], ref, b[:, :, 0, :], SUB)
                if l < LEVELS:
                    ins = tt(e[:, :, 1, :], b[:, :, 1, :], ref, SUB)
                else:
                    ins = dve.tensor_copy(e[:, :, 1, :], b[:, :, 1, :])
                ins.then_inc(S("LE"), 1)

            def lmask(l):
                return K("lvl")[:, l * P:(l + 1) * P].bitcast(I32).unsqueeze(1).broadcast_to([P, 4, P])

            def pick(name, l, i):
                if l == LEVELS:
                    return free(dve.copy_predicated(ATm[:, 4 * i:4 * i + 4, :], lmask(l),
                                                    got(dve, name)[:, :].rearrange("p (n j) -> p n j", n=4)), name)
                done(dve, f"lv{l - 1}_{i}" if l else f"dg_{i}")
                free(dve.copy_predicated(ATm[:, 4 * i:4 * i + 4, :], lmask(l),
                                         got(dve, name)[:, :].rearrange("p (n j) -> p n j", n=4)), name)

            exponents(0)
            ahead(dve, "qp3")
            exponents(1)
            for j in range(4):
                tokens(f"iv{j}", ht[:, :, j * CW:(j + 1) * CW], 0, BI + j * CW, CW)
            dve.wait_ge(S("AT0"), 1)
            for i in range(4):
                pick(f"dg_{i}", LEVELS, i)
            exponents(2)
            for l in range(LEVELS):
                for i in range(4):
                    pick(f"lv{l}_{i}", l, i)
                if l + 3 <= LEVELS:
                    exponents(l + 3)
                n = l + 2
                if LK0 <= n <= LEVELS:
                    dve.wait_ge(S("LX"), n + 1)
                    m = P >> (n + 1) if n < LEVELS else P
                    v, k = [t.rearrange("p (n y t) -> p n y t", y=2, t=m)[:, :, 0, :] for t in (L3[n % 3], hk)]
                    tt(v, v, k, MUL).then_inc(S("LK"), 1)
            for y in range(2):
                inverse(f"or{y}", oroot[:, y * T:(y + 1) * T], "orow")
            dve.wait_ge(S("hz"), 1)
            for i in range(4):
                o = got(dve, f"ob{i}")
                for h in (2 * i, 2 * i + 1):
                    s = slice(h * T, (h + 1) * T)
                    ins = stt(hO[:, s], hO[:, s], pc(PB["hhn"] + h), o[:, (h % 2) * T:(h % 2 + 1) * T], MUL, MUL)
                free(ins, f"ob{i}")
                done(dve, f"ob{i}")
                s = slice(i * 512, (i + 1) * 512)
                tt(hO[:, s], hO[:, s], hz[:, s], MUL).then_inc(S("yH"), 1)
            for i in range(4):
                parts(hO[:, i * 512:(i + 1) * 512], 2 * i)
            ahead(dve, "ob3")
            modulation(0)
            residual("oo")
            done(dve, "oo3")
            norm(2, lambda k: A1[0][:, k:k + 1])
            dve.wait_ge(S("zero"), 3)
            for g in range(3):
                pool_group(g, dve, V).then_inc(S("pl"), 1)
            residual("pw", lambda b: gsc[:, b:b + 1])
            done(dve, "pw3")

            def mlp(l):
                n = 3 + 2 * l
                norm(n, lambda k: A1[2 * l + 1][:, k:k + 1], (l, 24))
                for j in range(FF // CW):
                    i = 16 * l + j
                    if l == 0 and j == 10:
                        modulation(1)
                    o = got(dve, f"w1_{l}_{j}")
                    dve.wait_ge(S("relu"), i + 1)
                    if j >= 2:
                        dve.wait_ge(S("h1l"), i - 1)
                    free(stt(r2[j % 2], o[:, :], 0.0, rl[j % 2], MAX, MUL), f"w1_{l}_{j}")
                if l == 1:
                    ahead(dve, "w2_1_0")
                    modulation(4)
                residual(f"w2_{l}_", lambda b: mod[:, l, 40 + b:41 + b])
                done(dve, f"w2_{l}_3")

            mlp(0)
            modulation(2)
            dve.wait_ge(S("ld_s"), 16 * DMAS["ld_s"])
            for i in range(2):
                free(tt(wsT[:, 4 * i:4 * i + 4, :], got(dve, f"ws{i}")[:, :].rearrange("p (h t) -> p h t", h=4),
                        K("tri").unsqueeze(1).broadcast_to([P, 4, P]), MUL), f"ws{i}")
            norm(4, lambda k: A1[2][:, k:k + 1], (1, 0))
            done(dve, "si7")
            V(dve.tensor_reduce(mu, vt, AX, ADD))
            V(ts(mu, mu, -1.0 / D, None, MUL))
            for a in range(NT):
                ts(xc[:, a, :], vt[:, a, :], mu[:, a:a + 1], None, ADD).then_inc(S("xc"), 1)
            ahead(dve, "si1")
            dve.wait_ge(S("vs"), 1)
            V(dve.reciprocal(vr, vr))
            for a in range(NT):
                ins = stt(vt[:, a, :], xc[:, a, :], vr[:, a:a + 1], lng, MUL, MUL)
            V(ins)
            for a in range(NT):
                tt(vt[:, a, :], vt[:, a, :], lnb, ADD).then_inc(S("vln"), 1)
            done(dve, "si3")
            for i in range(4):
                t4 = xc.rearrange("p a n -> p (a n)")[:, i * 512:(i + 1) * 512]
                for j in range(2):
                    ins = tt(t4[:, j * T:(j + 1) * T].rearrange("p (a t) -> p a t", a=NT),
                             got(dve, f"mx{i}")[:, j * T:(j + 1) * T].rearrange("p (a t) -> p a t", a=NT),
                             bsb[:, 2 * i + j, :].unsqueeze(1).broadcast_to([P, NT, P]), ADD)
                free(ins, f"mx{i}")
                done(dve, f"mx{i}")
                tt(t4, t4, uT[:, 2 * i:2 * i + 2, :].rearrange("p b t -> p (b t)"), MUL).then_inc(S("yS"), 1)
                if i:
                    parts(xc.rearrange("p a n -> p (a n)")[:, (i - 1) * 512:i * 512], 2 * i - 2)
            parts(xc.rearrange("p a n -> p (a n)")[:, 3 * 512:], 6)
            residual("so", lambda b: mod[:, 1, 16 + b:17 + b])
            done(dve, "so3")
            modulation(3)
            mlp(1)
            norm(6, lambda k: pc(PB["fg"] + k))
            for i in (1, 3):
                free(dve.tensor_copy(ot[:, i // 2, (i % 2) * 512:(i % 2 + 1) * 512], got(dve, f"f{i}")[:, :]), f"f{i}")


DMAS = dict(ld_A=15, ld_B=7, ld_C=3, ld_b=7, ld_m=2, ld_s=4)

_INS = ["x", "norm_w", "ev_w_in", "ev_b_in", "mlstm_f_bias", "mlstm_conv_w", "mlstm_conv_b", "mlstm_head_norm",
        "nsa_q_norm", "nsa_k_norm", "cmp_k_pos", "cmp_k_w1", "cmp_k_w2", "cmp_v_pos", "cmp_v_w1", "cmp_v_w2",
        "ev_w_out", "od_w_in", "od_b_in", "hgrn_lb_logits", "hgrn_head_norm", "od_w_out", "c_2", "ada_w_2",
        "ada_b_2", "norm_mix_g_2", "norm_mlp_g_2", "pool_w_2", "pool_scale_2", "sgu_w_in_2", "sgu_ln_g_2",
        "sgu_ln_b_2", "sgu_w_s_2", "sgu_b_s_2", "sgu_w_out_2", "mlp_w1_2", "mlp_w2_2", "final_g_2"]


def kernel(**inputs):
    import numpy as _np
    import concourse.bacc as _bacc
    from concourse import mybir as _mybir
    from concourse.bass_utils import run_bass_kernel_spmd as _run

    nc = _bacc.Bacc("TRN2", target_bir_lowering=False, num_devices=1)
    arrays, aps = {}, {}
    for name in _INS:
        a = _np.ascontiguousarray(inputs[name])
        if a.ndim == 1:
            a = a.reshape(1, -1)
        arrays[f"in_{name}"] = a
        aps[name] = nc.dram_tensor(f"in_{name}", a.shape, _mybir.dt.from_np(a.dtype), kind="ExternalInput").ap()
    arrays["in_cst"] = constants()
    cst = nc.dram_tensor("in_cst", arrays["in_cst"].shape, _mybir.dt.float32, kind="ExternalInput").ap()
    out = nc.dram_tensor("out_0", (1, T, D), _mybir.dt.float32, kind="ExternalOutput").ap()
    build(nc, aps, cst, out)
    r = _run(nc, [arrays], core_ids=[0])
    return r.results[0]["out_0"]
```
